# Optimizing a Trainium2 kernel written in Bass

```python
import math
import jax, jax.numpy as jnp
from jax import lax
import numpy as np

D_MODEL = 1024
BATCH = 1
SEQ = 256
DEPTH = 2

N_A_LAYERS = DEPTH // 2
N_B_LAYERS = DEPTH - N_A_LAYERS
CONV_WIDTH = 31
DIFF_HEADS = 8
DIFF_HEAD_DIM = 64
DIFF_V_DIM = 2 * DIFF_HEAD_DIM
ROT_DIM = DIFF_HEAD_DIM // 4
ROPE_THETA = 500000.0
Q_BLOCK = 128
MEM_TOKENS = 256
MEM_HEADS = 4
MEM_HEAD_DIM = D_MODEL // MEM_HEADS
FFN_HIDDEN = -(-(8 * D_MODEL) // (3 * 256)) * 256
RMS_EPS = 1e-6
LN_EPS = 1e-5
SUBLN_EPS = 1e-5


def rms_norm(x, g, eps=RMS_EPS):
    xf = x.astype(jnp.float32)
    y = xf * lax.rsqrt(jnp.mean(xf * xf, axis=-1, keepdims=True) + eps)
    return (y * g.astype(jnp.float32)).astype(x.dtype)

def layer_norm(x, g, b, eps=LN_EPS):
    xf = x.astype(jnp.float32)
    mu = jnp.mean(xf, axis=-1, keepdims=True)
    xc = xf - mu
    y = xc * lax.rsqrt(jnp.mean(xc * xc, axis=-1, keepdims=True) + eps)
    return (y * g.astype(jnp.float32) + b.astype(jnp.float32)).astype(x.dtype)

def rope_tables(positions):
    inv_freq = ROPE_THETA ** (-jnp.arange(0, ROT_DIM, 2, dtype=jnp.float32) / ROT_DIM)
    ang = positions.astype(jnp.float32)[..., None] * inv_freq
    return jnp.cos(ang), jnp.sin(ang)

def apply_partial_rope(t, cos, sin):
    half = ROT_DIM // 2
    tf = t.astype(jnp.float32)
    r1 = tf[..., :half]
    r2 = tf[..., half:ROT_DIM]
    c = cos[:, :, None, None, :]
    s = sin[:, :, None, None, :]
    out = jnp.concatenate([r1 * c - r2 * s, r1 * s + r2 * c, tf[..., ROT_DIM:]], axis=-1)
    return out.astype(t.dtype)

def conformer_conv(h, w_pw1, b_pw1, w_dw, b_dw, ln_g, ln_b, w_pw2, b_pw2):
    u = h @ w_pw1 + b_pw1
    a, gate = jnp.split(u, 2, axis=-1)
    u = a * jax.nn.sigmoid(gate)
    u = lax.conv_general_dilated(
        u, w_dw[:, None, :].astype(u.dtype), window_strides=(1,),
        padding=((CONV_WIDTH - 1, 0),),
        dimension_numbers=("NWC", "WIO", "NWC"),
        feature_group_count=D_MODEL) + b_dw
    u = jax.nn.silu(layer_norm(u, ln_g, ln_b))
    return u @ w_pw2 + b_pw2

def shared_kv(x, kv_norm, w_k, w_v, cos, sin):
    B, S, _ = x.shape
    h = rms_norm(x, kv_norm)
    k = apply_partial_rope((h @ w_k).reshape(B, S, DIFF_HEADS, 2, DIFF_HEAD_DIM), cos, sin)
    v = (h @ w_v).reshape(B, S, DIFF_HEADS, DIFF_V_DIM)
    return k, v

def diff_attention(h, k, v, cos, sin, w_q, lq1, lk1, lq2, lk2, subln_g, w_o, lambda_init):
    B, S, _ = h.shape
    q = apply_partial_rope((h @ w_q).reshape(B, S, DIFF_HEADS, 2, DIFF_HEAD_DIM), cos, sin)
    lam = (jnp.exp(jnp.sum(lq1.astype(jnp.float32) * lk1.astype(jnp.float32)))
           - jnp.exp(jnp.sum(lq2.astype(jnp.float32) * lk2.astype(jnp.float32)))
           + lambda_init)
    n_blocks = S // Q_BLOCK
    q_blocks = q.reshape(B, n_blocks, Q_BLOCK, DIFF_HEADS, 2, DIFF_HEAD_DIM).swapaxes(0, 1)
    k_pos = jnp.arange(S)
    scale = DIFF_HEAD_DIM ** -0.5

    def one_block(args):
        blk, qb = args
        q_pos = blk * Q_BLOCK + jnp.arange(Q_BLOCK)
        s = jnp.einsum('bqhcd,bkhcd->bhcqk', qb, k,
                       preferred_element_type=jnp.float32) * scale
        mask = k_pos[None, :] <= q_pos[:, None]
        p = jax.nn.softmax(jnp.where(mask, s, -jnp.inf), axis=-1)
        a = p[:, :, 0] - lam * p[:, :, 1]
        return jnp.einsum('bhqk,bkhe->bqhe', a.astype(v.dtype), v)

    o = lax.map(one_block, (jnp.arange(n_blocks), q_blocks))
    o = o.swapaxes(0, 1).reshape(B, S, DIFF_HEADS, DIFF_V_DIM)
    o = rms_norm(o, subln_g, SUBLN_EPS) * (1.0 - lambda_init)
    return o.reshape(B, S, DIFF_HEADS * DIFF_V_DIM) @ w_o

def memory_cross_attention(h, mem, w_q, w_k, w_v, w_o):
    B, S, _ = h.shape
    M = mem.shape[1]
    q = (h @ w_q).reshape(B, S, MEM_HEADS, MEM_HEAD_DIM)
    k = (mem @ w_k).reshape(B, M, MEM_HEADS, MEM_HEAD_DIM)
    v = (mem @ w_v).reshape(B, M, MEM_HEADS, MEM_HEAD_DIM)
    s = jnp.einsum('bshd,bmhd->bhsm', q, k, preferred_element_type=jnp.float32) * MEM_HEAD_DIM ** -0.5
    p = jax.nn.softmax(s, axis=-1)
    o = jnp.einsum('bhsm,bmhd->bshd', p.astype(v.dtype), v).reshape(B, S, D_MODEL)
    return o @ w_o

def swiglu(h, w_gate, w_up, w_down):
    return (jax.nn.silu(h @ w_gate) * (h @ w_up)) @ w_down

def first_inputs(seed: int = 0) -> dict:
    key = jax.random.key(seed)
    ks = iter(jax.random.split(key, 40))
    f32 = jnp.float32

    def w(shape, fan_in):
        return jax.random.normal(next(ks), shape, f32) * (fan_in ** -0.5)

    def gain(shape):
        return 1.0 + 0.02 * jax.random.normal(next(ks), shape, f32)

    def small(shape, scale=0.01):
        return scale * jax.random.normal(next(ks), shape, f32)

    D, F, A, Bn = D_MODEL, FFN_HIDDEN, N_A_LAYERS, N_B_LAYERS
    QK = DIFF_HEADS * 2 * DIFF_HEAD_DIM
    VW = DIFF_HEADS * DIFF_V_DIM
    x = jax.random.normal(next(ks), (BATCH, SEQ, D), f32)
    mem = jax.random.normal(next(ks), (BATCH, MEM_TOKENS, D), f32)
    offset = jax.random.randint(next(ks), (BATCH, 1), 0, 1024, dtype=jnp.int32)
    positions = (offset + jnp.arange(SEQ, dtype=jnp.int32)[None, :]).astype(jnp.int32)
    return {
        "x": x, "mem": mem, "positions": positions,
        "norm_mix": gain((DEPTH, D)), "norm_mem": gain((DEPTH, D)),
        "norm_ffn": gain((DEPTH, D)), "norm_final": gain((D,)),
        "conv_w_pw1": w((A, D, 2 * D), D), "conv_b_pw1": small((A, 2 * D)),
        "conv_w_dw": w((A, CONV_WIDTH, D), CONV_WIDTH), "conv_b_dw": small((A, D)),
        "conv_ln_g": gain((A, D)), "conv_ln_b": small((A, D)),
        "conv_w_pw2": w((A, D, D), D), "conv_b_pw2": small((A, D)),
        "kv_norm": gain((D,)), "w_k_shared": w((D, QK), D), "w_v_shared": w((D, VW), D),
        "diff_w_q": w((Bn, D, QK), D),
        "diff_lambda_q1": small((Bn, DIFF_HEAD_DIM), 0.1), "diff_lambda_k1": small((Bn, DIFF_HEAD_DIM), 0.1),
        "diff_lambda_q2": small((Bn, DIFF_HEAD_DIM), 0.1), "diff_lambda_k2": small((Bn, DIFF_HEAD_DIM), 0.1),
        "diff_subln_g": gain((Bn, DIFF_V_DIM)), "diff_w_o": w((Bn, VW, D), VW),
        "mem_w_q": w((DEPTH, D, D), D), "mem_w_k": w((DEPTH, D, D), D),
        "mem_w_v": w((DEPTH, D, D), D), "mem_w_o": w((DEPTH, D, D), D),
        "ffn_w_gate": w((DEPTH, D, F), D), "ffn_w_up": w((DEPTH, D, F), D),
        "ffn_w_down": w((DEPTH, F, D), F),
    }

def first_block(x, mem, positions, norm_mix, norm_mem, norm_ffn, norm_final,
              conv_w_pw1, conv_b_pw1, conv_w_dw, conv_b_dw, conv_ln_g, conv_ln_b,
              conv_w_pw2, conv_b_pw2, kv_norm, w_k_shared, w_v_shared,
              diff_w_q, diff_lambda_q1, diff_lambda_k1, diff_lambda_q2, diff_lambda_k2,
              diff_subln_g, diff_w_o, mem_w_q, mem_w_k, mem_w_v, mem_w_o,
              ffn_w_gate, ffn_w_up, ffn_w_down):
    cos, sin = rope_tables(positions)
    k_sh = None
    v_sh = None
    for i in range(DEPTH):
        if i < N_A_LAYERS:
            a = i
            h = rms_norm(x, norm_mix[i])
            x = x + conformer_conv(h, conv_w_pw1[a], conv_b_pw1[a], conv_w_dw[a], conv_b_dw[a],
                                   conv_ln_g[a], conv_ln_b[a], conv_w_pw2[a], conv_b_pw2[a])
        else:
            b = i - N_A_LAYERS
            if b == 0:
                k_sh, v_sh = shared_kv(x, kv_norm, w_k_shared, w_v_shared, cos, sin)
            lambda_init = 0.8 - 0.6 * math.exp(-0.3 * i)
            h = rms_norm(x, norm_mix[i])
            x = x + diff_attention(h, k_sh, v_sh, cos, sin, diff_w_q[b],
                                   diff_lambda_q1[b], diff_lambda_k1[b],
                                   diff_lambda_q2[b], diff_lambda_k2[b],
                                   diff_subln_g[b], diff_w_o[b], lambda_init)
        x = x + memory_cross_attention(rms_norm(x, norm_mem[i]), mem,
                                       mem_w_q[i], mem_w_k[i], mem_w_v[i], mem_w_o[i])
        x = x + swiglu(rms_norm(x, norm_ffn[i]), ffn_w_gate[i], ffn_w_up[i], ffn_w_down[i])
    return rms_norm(x, norm_final)


DEPTH_2 = 1

HEAD_DIM = 64
N_HEADS = D_MODEL // HEAD_DIM
NSA_HEADS = N_HEADS // 2
SWA_HEADS = N_HEADS - NSA_HEADS
NSA_KV = 2
NSA_GROUP = NSA_HEADS // NSA_KV
SWA_KV = 2
SWA_GROUP = SWA_HEADS // SWA_KV
MIX_WIDTH = (NSA_HEADS + SWA_HEADS) * HEAD_DIM
SWA_WINDOW = 128
NSA_WINDOW = 512
CMP_LEN = 32
CMP_STRIDE = 16
CMP_HIDDEN = 256
SLC_BLOCK = 64
SLC_TOPK = 16
NSA_BRANCHES = 3
BAND_QBLOCK = 128
SLC_QCHUNK = 64
D_FF = 2816
CONV_WIDTH_2 = 3
ROPE_THETA_2 = 10000.0
NEG = -1e30
BIG = 1e9

IN_SIZES = [
    NSA_HEADS * HEAD_DIM,
    NSA_KV * HEAD_DIM, NSA_KV * HEAD_DIM,
    NSA_KV * HEAD_DIM, NSA_KV * HEAD_DIM,
    NSA_KV * HEAD_DIM, NSA_KV * HEAD_DIM,
    NSA_HEADS * NSA_BRANCHES,
    SWA_HEADS * HEAD_DIM,
    SWA_KV * HEAD_DIM, SWA_KV * HEAD_DIM,
]
IN_WIDTH = int(sum(IN_SIZES))
IN_SPLITS = [int(v) for v in np.cumsum(IN_SIZES)[:-1]]


def rms_norm_2(x, g):
    xf = x.astype(jnp.float32)
    y = xf * lax.rsqrt(jnp.mean(xf * xf, axis=-1, keepdims=True) + RMS_EPS)
    return (y * g.astype(jnp.float32)).astype(x.dtype)

def rope(x, pos):
    half = HEAD_DIM // 2
    inv = ROPE_THETA_2 ** (-jnp.arange(half, dtype=jnp.float32) / half)
    ang = pos.astype(jnp.float32)[:, None] * inv[None, :]
    cos = jnp.cos(ang)[None, :, None, :]
    sin = jnp.sin(ang)[None, :, None, :]
    xf = x.astype(jnp.float32)
    x1, x2 = xf[..., :half], xf[..., half:]
    return jnp.concatenate([x1 * cos - x2 * sin, x2 * cos + x1 * sin], axis=-1).astype(x.dtype)

def compress(kv, pe, w1, w2):
    B, S, H, D = kv.shape
    ch = kv.reshape(B, S // CMP_STRIDE, CMP_STRIDE, H, D)
    blocks = jnp.concatenate([ch[:, :-1], ch[:, 1:]], axis=2)
    blocks = blocks + pe[None, None, :, None, :]
    nc = blocks.shape[1]
    flat = blocks.transpose(0, 1, 3, 2, 4).reshape(B, nc, H, CMP_LEN * D)
    return jax.nn.gelu(flat @ w1) @ w2

def compressed_attention(q, kc, vc, t):
    nc = kc.shape[1]
    s = jnp.einsum('bthgd,bchd->bhgtc', q, kc).astype(jnp.float32) * (HEAD_DIM ** -0.5)
    ends = jnp.arange(nc) * CMP_STRIDE + CMP_LEN - 1
    valid = ends[None, :] <= t[:, None]
    s = jnp.where(valid, s, NEG)
    m = jnp.max(s, axis=-1, keepdims=True)
    e = jnp.where(valid, jnp.exp(s - m), 0.0)
    p = e / jnp.maximum(jnp.sum(e, axis=-1, keepdims=True), 1e-30)
    o = jnp.einsum('bhgtc,bchd->bthgd', p.astype(vc.dtype), vc)
    return o, p

def overlap_matrix(nc, nsb):
    i = np.arange(nc)[:, None]
    j = np.arange(nsb)[None, :]
    cs, ce = i * CMP_STRIDE, i * CMP_STRIDE + CMP_LEN - 1
    bs, be = j * SLC_BLOCK, j * SLC_BLOCK + SLC_BLOCK - 1
    return jnp.asarray(((cs <= be) & (ce >= bs)).astype(np.float32))

def select_blocks(p_cmp, t, nsb):
    p_grp = jnp.sum(p_cmp, axis=2)
    imp = jnp.einsum('bhtc,cj->bhtj', p_grp, overlap_matrix(p_cmp.shape[-1], nsb))
    jb = jnp.arange(nsb)[None, :]
    tb = (t // SLC_BLOCK)[:, None]
    forced = (jb == 0) | (jb == tb) | (jb == tb - 1)
    causal = jb * SLC_BLOCK <= t[:, None]
    score = jnp.where(forced, BIG, jnp.where(causal, imp, NEG))
    _, idx = lax.top_k(score, min(SLC_TOPK, nsb))
    return idx

def selected_attention(q, k, v, idx, t):
    B, S, Hkv, G, D = q.shape
    nsb = S // SLC_BLOCK
    K = idx.shape[-1]
    nqc = S // SLC_QCHUNK
    kb = k.reshape(B, nsb, SLC_BLOCK, Hkv, D).transpose(0, 3, 1, 2, 4)
    vb = v.reshape(B, nsb, SLC_BLOCK, Hkv, D).transpose(0, 3, 1, 2, 4)
    qc = q.reshape(B, nqc, SLC_QCHUNK, Hkv, G, D).transpose(1, 0, 2, 3, 4, 5)
    ic = idx.reshape(B, Hkv, nqc, SLC_QCHUNK, K).transpose(2, 0, 1, 3, 4)
    tc = t.reshape(nqc, SLC_QCHUNK)
    gather = jax.vmap(jax.vmap(lambda blk, ix: blk[ix]))
    offs = jnp.arange(SLC_BLOCK)

    def chunk(args):
        qx, ix, tx = args
        kg = gather(kb, ix)
        vg = gather(vb, ix)
        s = jnp.einsum('bqhgd,bhqnkd->bhgqnk', qx, kg).astype(jnp.float32) * (HEAD_DIM ** -0.5)
        pos = ix[..., None] * SLC_BLOCK + offs
        mask = pos <= tx[None, None, :, None, None]
        s = jnp.where(mask[:, :, None], s, NEG)
        p = jax.nn.softmax(s.reshape(B, Hkv, G, SLC_QCHUNK, K * SLC_BLOCK), axis=-1)
        p = p.reshape(B, Hkv, G, SLC_QCHUNK, K, SLC_BLOCK).astype(vg.dtype)
        return jnp.einsum('bhgqnk,bhqnkd->bqhgd', p, vg)

    o = lax.map(chunk, (qc, ic, tc))
    return o.transpose(1, 0, 2, 3, 4, 5).reshape(B, S, Hkv, G, D)

def banded_attention(q, k, v, window, sinks):
    B, S, Hkv, G, D = q.shape
    QB = BAND_QBLOCK
    span = window + QB
    kp = jnp.pad(k, ((0, 0), (window, 0), (0, 0), (0, 0)))
    vp = jnp.pad(v, ((0, 0), (window, 0), (0, 0), (0, 0)))
    a = jnp.arange(QB)[:, None]
    j = jnp.arange(span)[None, :]
    band = (j > a) & (j <= a + window)
    scale = HEAD_DIM ** -0.5

    def block(i):
        start = i * QB
        qb = lax.dynamic_slice_in_dim(q, start, QB, axis=1)
        kb = lax.dynamic_slice_in_dim(kp, start, span, axis=1)
        vb = lax.dynamic_slice_in_dim(vp, start, span, axis=1)
        s = jnp.einsum('bqhgd,bkhd->bhgqk', qb, kb).astype(jnp.float32) * scale
        mask = band & (start + j - window >= 0)
        s = jnp.where(mask, s, NEG)
        m = jnp.max(s, axis=-1, keepdims=True)
        if sinks is not None:
            sk = sinks.astype(jnp.float32)[None, :, :, None, None]
            m = jnp.maximum(m, sk)
            e = jnp.exp(s - m)
            den = jnp.sum(e, axis=-1, keepdims=True) + jnp.exp(sk - m)
        else:
            e = jnp.exp(s - m)
            den = jnp.sum(e, axis=-1, keepdims=True)
        p = (e / den).astype(vb.dtype)
        return jnp.einsum('bhgqk,bkhd->bqhgd', p, vb)

    o = lax.map(block, jnp.arange(S // QB))
    return o.transpose(1, 0, 2, 3, 4, 5).reshape(B, S, Hkv, G, D)

def causal_dwconv(x, w, b):
    C = x.shape[-1]
    y = lax.conv_general_dilated(
        x, w[:, None, :].astype(x.dtype), window_strides=(1,),
        padding=[(CONV_WIDTH_2 - 1, 0)], dimension_numbers=('NWC', 'WIO', 'NWC'),
        feature_group_count=C)
    return y + b

def hybrid_layer(h, w_in, w_out, attn_pre_norm, attn_post_norm, nsa_out_norm, swa_out_norm,
                 cmp_pos, cmp_w1, cmp_w2, swa_sinks, ffn_pre_norm, ffn_post_norm,
                 w_up, conv_w, conv_b, w_down):
    B, S, _ = h.shape
    t = jnp.arange(S)
    hn = rms_norm_2(h, attn_pre_norm)
    proj = hn @ w_in
    (q_n, k_c, v_c, k_s, v_s, k_w, v_w, g_n, q_w, k_sw, v_sw) = jnp.split(proj, IN_SPLITS, axis=-1)
    kvh = lambda z, n: z.reshape(B, S, n, HEAD_DIM)

    qn = rope(kvh(q_n, NSA_HEADS), t).reshape(B, S, NSA_KV, NSA_GROUP, HEAD_DIM)
    k_c, k_s, k_w = (rope(kvh(z, NSA_KV), t) for z in (k_c, k_s, k_w))
    v_c, v_s, v_w = (kvh(z, NSA_KV) for z in (v_c, v_s, v_w))
    ckv = jax.vmap(compress)(jnp.stack([k_c, v_c]), cmp_pos, cmp_w1, cmp_w2)
    o_cmp, p_cmp = compressed_attention(qn, ckv[0], ckv[1], t)
    idx = select_blocks(p_cmp, t, S // SLC_BLOCK)
    o_slc = selected_attention(qn, k_s, v_s, idx, t)
    o_win = banded_attention(qn, k_w, v_w, NSA_WINDOW, None)
    gates = jax.nn.sigmoid(g_n).reshape(B, S, NSA_KV, NSA_GROUP, NSA_BRANCHES)
    o_nsa = gates[..., 0:1] * o_cmp + gates[..., 1:2] * o_slc + gates[..., 2:3] * o_win
    o_nsa = rms_norm_2(o_nsa.reshape(B, S, NSA_HEADS * HEAD_DIM), nsa_out_norm)

    qw = rope(kvh(q_w, SWA_HEADS), t).reshape(B, S, SWA_KV, SWA_GROUP, HEAD_DIM)
    kw = rope(kvh(k_sw, SWA_KV), t)
    o_swa = banded_attention(qw, kw, kvh(v_sw, SWA_KV), SWA_WINDOW,
                             swa_sinks.reshape(SWA_KV, SWA_GROUP))
    o_swa = rms_norm_2(o_swa.reshape(B, S, SWA_HEADS * HEAD_DIM), swa_out_norm)

    mixed = jnp.concatenate([o_nsa, o_swa], axis=-1) @ w_out
    h = h + rms_norm_2(mixed, attn_post_norm)

    hn = rms_norm_2(h, ffn_pre_norm)
    u = causal_dwconv(hn @ w_up, conv_w, conv_b)
    gate, up = jnp.split(u, 2, axis=-1)
    y = (jax.nn.gelu(gate, approximate=True) * up) @ w_down
    return h + rms_norm_2(y, ffn_post_norm)

def second_inputs(seed: int = 0) -> dict:
    key = jax.random.key(seed)
    ks = jax.random.split(key, 17)
    f = jnp.float32
    L = DEPTH_2
    nrm = lambda k, shape, sc: jax.random.normal(k, shape, f) * sc
    gain = lambda k, shape: 1.0 + 0.05 * jax.random.normal(k, shape, f)
    return {
        "x": nrm(ks[0], (BATCH, SEQ, D_MODEL), 1.0),
        "w_in": nrm(ks[1], (L, D_MODEL, IN_WIDTH), D_MODEL ** -0.5),
        "w_out": nrm(ks[2], (L, MIX_WIDTH, D_MODEL), MIX_WIDTH ** -0.5),
        "attn_pre_norm": gain(ks[3], (L, D_MODEL)),
        "attn_post_norm": gain(ks[4], (L, D_MODEL)),
        "nsa_out_norm": gain(ks[5], (L, NSA_HEADS * HEAD_DIM)),
        "swa_out_norm": gain(ks[6], (L, SWA_HEADS * HEAD_DIM)),
        "cmp_pos": nrm(ks[7], (L, 2, CMP_LEN, HEAD_DIM), 0.1),
        "cmp_w1": nrm(ks[8], (L, 2, CMP_LEN * HEAD_DIM, CMP_HIDDEN), (CMP_LEN * HEAD_DIM) ** -0.5),
        "cmp_w2": nrm(ks[9], (L, 2, CMP_HIDDEN, HEAD_DIM), CMP_HIDDEN ** -0.5),
        "swa_sinks": nrm(ks[10], (L, SWA_HEADS), 0.5),
        "ffn_pre_norm": gain(ks[11], (L, D_MODEL)),
        "ffn_post_norm": gain(ks[12], (L, D_MODEL)),
        "w_up": nrm(ks[13], (L, D_MODEL, 2 * D_FF), D_MODEL ** -0.5),
        "conv_w": nrm(ks[14], (L, CONV_WIDTH_2, 2 * D_FF), CONV_WIDTH_2 ** -0.5),
        "conv_b": nrm(ks[15], (L, 2 * D_FF), 0.02),
        "w_down": nrm(ks[16], (L, D_FF, D_MODEL), D_FF ** -0.5),
    }

def second_block(x, w_in, w_out, attn_pre_norm, attn_post_norm, nsa_out_norm, swa_out_norm,
              cmp_pos, cmp_w1, cmp_w2, swa_sinks, ffn_pre_norm, ffn_post_norm,
              w_up, conv_w, conv_b, w_down):
    h = x
    for l in range(DEPTH_2):
        h = hybrid_layer(h, w_in[l], w_out[l], attn_pre_norm[l], attn_post_norm[l],
                         nsa_out_norm[l], swa_out_norm[l], cmp_pos[l], cmp_w1[l], cmp_w2[l],
                         swa_sinks[l], ffn_pre_norm[l], ffn_post_norm[l],
                         w_up[l], conv_w[l], conv_b[l], w_down[l])
    return h


def setup_inputs(seed=0):
    out = dict(first_inputs(seed))
    for name, value in second_inputs(seed + 1).items():
        if name != "x":
            out[name + "_2"] = value
    return out


def reference(
    x, mem, positions, norm_mix, norm_mem, norm_ffn, norm_final, conv_w_pw1, conv_b_pw1,
    conv_w_dw, conv_b_dw, conv_ln_g, conv_ln_b, conv_w_pw2, conv_b_pw2, kv_norm, w_k_shared,
    w_v_shared, diff_w_q, diff_lambda_q1, diff_lambda_k1, diff_lambda_q2, diff_lambda_k2,
    diff_subln_g, diff_w_o, mem_w_q, mem_w_k, mem_w_v, mem_w_o, ffn_w_gate, ffn_w_up,
    ffn_w_down, w_in_2, w_out_2, attn_pre_norm_2, attn_post_norm_2, nsa_out_norm_2,
    swa_out_norm_2, cmp_pos_2, cmp_w1_2, cmp_w2_2, swa_sinks_2, ffn_pre_norm_2, ffn_post_norm_2,
    w_up_2, conv_w_2, conv_b_2, w_down_2,
):
    x = first_block(
        x, mem, positions, norm_mix, norm_mem, norm_ffn, norm_final, conv_w_pw1, conv_b_pw1,
        conv_w_dw, conv_b_dw, conv_ln_g, conv_ln_b, conv_w_pw2, conv_b_pw2, kv_norm, w_k_shared,
        w_v_shared, diff_w_q, diff_lambda_q1, diff_lambda_k1, diff_lambda_q2, diff_lambda_k2,
        diff_subln_g, diff_w_o, mem_w_q, mem_w_k, mem_w_v, mem_w_o, ffn_w_gate, ffn_w_up,
        ffn_w_down,
    )
    return second_block(
        x, w_in_2, w_out_2, attn_pre_norm_2, attn_post_norm_2, nsa_out_norm_2, swa_out_norm_2,
        cmp_pos_2, cmp_w1_2, cmp_w2_2, swa_sinks_2, ffn_pre_norm_2, ffn_post_norm_2, w_up_2,
        conv_w_2, conv_b_2, w_down_2,
    )


_drawn_inputs = setup_inputs


def setup_inputs(seed=0):
    import zlib

    import numpy as np

    out = dict(_drawn_inputs(seed))
    spreads = {}
    factors = {'norm_mix': 3.047,
     'norm_mem': 8.0,
     'conv_b_pw1': 4.466,
     'conv_ln_b': 3.877,
     'kv_norm': 3.374,
     'diff_lambda_q1': 3.781,
     'diff_lambda_k1': 5.542,
     'diff_lambda_q2': 2.847,
     'diff_lambda_k2': 5.1,
     'diff_subln_g': 3.686,
     'swa_sinks_2': 4.062,
     'conv_b_2': 3.345}
    for name, (base, spread) in spreads.items():
        noise = np.random.default_rng([zlib.crc32(name.encode()), seed]).standard_normal(out[name].shape)
        drawn = base * np.exp(spread * noise) if base else spread * noise
        out[name] = __import__('jax').numpy.asarray(drawn.astype(out[name].dtype))
    for name, factor in factors.items():
        out[name] = (out[name] * factor).astype(out[name].dtype)
    return out
```

```python
import concourse.bass as bass
from concourse import mybir
from contextlib import ExitStack, contextmanager
import math
import numpy as np

F32 = mybir.dt.float32
F32R = mybir.dt.float32r
BF16 = mybir.dt.bfloat16
I32 = mybir.dt.int32
U32 = mybir.dt.uint32
ALU = mybir.AluOpType
ACT = mybir.ActivationFunctionType
AX_X = mybir.AxisListType.X

P = 128
D = 1024
S = 256
NT = S // P
DC = D // P
FF = 2816
FC = FF // P
KC = 8
MB = 256
CONV = 31
DIFF_HEADS = 8
DIFF_SCALE = 64 ** -0.5
MEM_HEADS = 4
MEM_SCALE = 256 ** -0.5
LAMBDA_INIT = 0.8 - 0.6 * math.exp(-0.3)
ROT1 = 16
CMP_LEN, CMP_STRIDE = 32, 16
NCMP = S // CMP_STRIDE - 1
HD2 = 64
NSA_SCALE = HD2 ** -0.5
NEG = -1e30
MAGIC = 1.5 * 2 ** 23
TWO_PI = (6.28125, 0.0019350051879882812, 3.0199159819573245e-07)
PI_IN = 3.1415925
RMS_EPS, LN_EPS, SUBLN_EPS = 1e-6, 1e-5, 1e-5
LO_DVE = 5

PLAN = [
    ("pw1", 8, 8), ("memk", 8, 8), ("memv", 8, 8), ("pw2", 4, 4),
    ("memq0", 4, 4), ("attn_mem0", 0, 4), ("memo0", 4, 4), ("gu0", 22, 22), ("down0", 12, 4),
    ("diffk", 4, 4), ("diffv", 4, 4), ("diffq", 4, 4), ("attn_diff", 0, 8), ("diffo", 4, 4),
    ("memq1", 4, 4), ("attn_mem1", 0, 4), ("memo1", 4, 4), ("gu1", 22, 22), ("down1", 12, 4),
    ("win", 8, 8), ("winv", 2, 2), ("cmp", 4, 2), ("attn_nsa", 0, 8), ("wout", 4, 4),
    ("up2", 22, 22), ("down2", 12, 4),
]
T0, G0 = {}, {}
_t = _g = 0
for _name, _nt, _ng in PLAN:
    T0[_name], G0[_name] = _t, _g
    _t, _g = _t + _nt, _g + _ng
TILES = _t
NTILES = {n: t for n, t, _ in PLAN}

CONSTS = [
    ("g_mix0", 8), ("g_mem0", 8), ("g_ffn0", 8), ("g_kv", 8), ("g_mix1", 8), ("g_mem1", 8), ("g_ffn1", 8),
    ("g_final", 8), ("b_pw1", 16), ("w_dw", DC * CONV), ("b_dw", 8), ("ln_g", 8), ("ln_b", 8), ("b_pw2", 8),
    ("g_sub", 1), ("lam", 256), ("g_pre2", 8), ("g_post2", 8), ("g_out2", 8), ("pe", 32), ("cmp_w2", 256),
    ("sinks", 8), ("g_fpre2", 8), ("g_fpost2", 8), ("cw2", 132), ("cb2", 44),
    ("invf", 1), ("ident", P), ("perm1", P), ("perm2", P), ("causal", P), ("band", P), ("cmask", 32),
    ("rowok", 2), ("cos2", S), ("sin2", S),
]
C0 = {}
_c = 0
for _name, _n in CONSTS:
    C0[_name] = (_c, _n)
    _c += _n
NCONST = _c


class Chain:

    def __init__(self, eng, sem):
        self.eng, self.sem, self.base, self.k, self.i, self.per = eng, sem, 0, 0, None, 0

    def link(self, ins):
        ins.then_inc(self.sem, 1)
        self.k += 1
        at = self.base + self.k
        self.eng.wait_ge(self.sem, at if self.i is None else self.i * self.per + at)
        return ins

    @contextmanager
    def loop(self, n, per, start=0):
        self.base += self.k
        self.k = 0
        if n - start == 1:
            yield start
            assert self.k == per, (self.k, per)
            self.base += per
        else:
            with self.eng.Fori(start, n) as i:
                self.i, self.per = i, per
                self.base -= start * per
                yield i
                assert self.k == per, (self.k, per)
                self.i = None
            self.base += n * per
        self.k = 0


@contextmanager
def loop(eng, n, start=0):
    if n - start == 1:
        yield start
    else:
        with eng.Fori(start, n) as i:
            yield i


class Steps:

    def __init__(self, sem, steps):
        self.sem, self.first, self.n = sem, {}, dict(steps)
        total = 0
        for name, n in steps:
            self.first[name] = total
            total += n

    def at(self, name, k=None):
        return self.first[name] + (self.n[name] if k is None else k)


def build(nc, weights, consts, x_in, mem_in, positions, out):
    ctx = ExitStack()
    with ctx:
        def sb(name, shape, dt=F32, where=ctx):
            return where.enter_context(nc.sbuf_tensor(name, shape, dt))

        def sem(name):
            return ctx.enter_context(nc.semaphore(name))

        raw = [sb(f"raw{j}", [P, KC, MB]) for j in range(2)]
        whi = [sb(f"whi{j}", [P, KC, MB], F32R) for j in range(2)]
        wlo = [sb(f"wlo{j}", [P, KC, MB], F32R) for j in range(2)]
        X = sb("X", [P, DC, S])
        SQ = sb("SQ", [P, DC, S])
        Hhi, Hlo = sb("Hhi", [P, DC, S], F32R), sb("Hlo", [P, DC, S], F32R)
        H2hi, H2lo = sb("H2hi", [P, DC, S], F32R), sb("H2lo", [P, DC, S], F32R)
        FH = sb("FH", [P, FC, S], F32R)
        MKV = sb("MKV", [P, 4 * DC, S])
        cst = sb("cst", [P, NCONST])
        R = sb("R", [P, S])
        TG, TU = sb("TG", [P, 2, S + 2]), sb("TU", [P, 2, S + 2])
        SG = sb("SG", [P, 2, S])
        E = sb("E", [P, 2, 2, S])
        PT = sb("PT", [P, 2, 2 * S])
        rope_c, rope_s = sb("rope_c", [P, S]), sb("rope_s", [P, S])
        ones = sb("ones", [P, 1])
        rt = sb("rt", [P, 15, 16])
        nw = sb("nw", [P, 4, 16])
        nwi = sb("nwi", [P, 16], I32)
        mx, nb, sm, rs = (sb(n, [P, 2, 2]) for n in ("mx", "nb", "smx", "rs"))
        sk, ske = sb("skm", [P, 2, 2]), sb("ske", [P, 2, 2])
        lam, gsub = sb("lamt", [P, 4]), sb("gsub", [P, 1])
        gates = sb("gates", [P, NT, 24])
        HCm = sb("HCm", [P, 2, 2, 32])
        KCm, VCm = sb("KCm", [P, 16]), sb("VCm", [16, P])
        ident_b, causal_b, band_b = (sb(n, [P, P], BF16) for n in ("ident_b", "causal_b", "band_b"))
        cmask_b = sb("cmask_b", [P, 32], BF16)
        with ExitStack() as shared:
            FL = sb("FL", [P, FC, S], F32R, shared)
        A = sb("A", [P, FC, S])
        Af = A[:, :, :].rearrange("p c s -> p (c s)")
        U = Af[:, 0:DC * (S + CONV - 1)].rearrange("p (c s) -> p c s", c=DC)
        UC = A[:, 10:18, :]
        FHf = FH[:, :, :].rearrange("p c s -> p (c s)")
        Ohi, Olo = FH[:, 0:8, :], FH[:, 8:16, :]
        V2 = Af[:, 16 * S:20 * S].rearrange("p (t n) -> p t n", t=NT)
        ZT = Af[:, 20 * S:20 * S + 480]
        M2 = MKV[:, 0:8, :]

        acc = [ctx.enter_context(nc.psum_tensor(f"acc{j}", [P, 2, S], F32)) for j in range(2)]
        sc = ctx.enter_context(nc.psum_tensor("sc", [P, 4, 2 * S], F32))
        tp = ctx.enter_context(nc.psum_tensor("tp", [P, 2 * S], F32))
        st = ctx.enter_context(nc.psum_tensor("st", [P, 2 * S], F32))

        raw_loaded = [sem(f"raw_loaded{j}") for j in range(2)]
        cst_loaded, x_loaded, mem_loaded, pos_loaded = (sem(n) for n in ("cst_loaded", "x_loaded", "mem_loaded", "pos_loaded"))
        hi_out, lo_dve, lo_pool = sem("hi_out"), sem("lo_dve"), sem("lo_pool")
        tile_done, acc_free = sem("tile_done"), sem("acc_free")
        s_given, s_taken, s_sq, s_h = sem("given"), sem("taken"), sem("sq_ready"), sem("h_ready")
        stat_ready, rt_ready, spread_ready, spread_used = (sem(n) for n in ("stat_ready", "rt_ready", "spread_ready", "spread_used"))
        s_done, nb_ready, exp_done, p_ready = sem("s_done"), sem("nb_ready"), sem("exp_done"), sem("p_ready")
        t_done, pt_ready, pv_done = sem("t_done"), sem("pt_ready"), sem("pv_done")
        rot_ready, rot_used = sem("rot_ready"), sem("rot_used")
        consts_ready, conv_done, hid_ready, cmp_mm, cmp_ready = (sem(n) for n in ("consts_ready", "conv_done", "hid_ready", "cmp_mm", "cmp_ready"))
        x_final, out_done, u_ready = sem("x_final"), sem("out_done"), sem("u_ready")
        dve_chain, act_chain = sem("dve_chain"), sem("act_chain")

        given = Steps(s_given, [("lam", 1), ("rope", 1), ("ln_sq", 1), ("ln", 4), ("gu0", 11), ("sub", 4), ("gu1", 11),
                                ("final", 4), ("z", 2), ("outn", 4), ("post", 4), ("up2", 22)])
        taken = Steps(s_taken, [("x0", 1), ("mem", 1), ("lam", 1), ("rope", 1), ("pw1", 4), ("ln", 4), ("pw2", 4),
                                ("attn_mem0", 4), ("memo0", 4), ("gu0", 22), ("down0", 4), ("sub", 4), ("diffo", 4),
                                ("attn_mem1", 4), ("memo1", 4), ("gu1", 22), ("final", 4), ("gates", 1), ("z", 2),
                                ("outn", 4), ("post", 4), ("up2", 22)])
        sq = Steps(s_sq, [("mix0", 1), ("ln", 1), ("pw2", 4), ("memo0", 4), ("down0", 4), ("attn_diff", 8), ("diffo", 4),
                          ("memo1", 4), ("down1", 4), ("final", 4), ("attn_nsa", 8), ("wout", 4), ("post", 4), ("down2", 4)])
        h = Steps(s_h, [("x0", 1), ("mem", 1), ("ln", 4), ("pw2", 4), ("attn_mem0", 4), ("memo0", 4), ("gu0", 11),
                        ("down0", 4), ("sub", 4), ("diffo", 4), ("attn_mem1", 4), ("memo1", 4), ("gu1", 11), ("final", 4),
                        ("z", 2), ("outn", 4), ("post", 4), ("up2", 11)])
        NORMS = ["mix0", "ln_mu", "ln_var", "mem0", "ffn0", "attn1", "sub", "mem1", "ffn1", "final", "pre2", "out2",
                 "post2", "fpre2", "fpost2"]
        N0 = {name: k for k, name in enumerate(NORMS)}
        ROPES = {"diff": [(s, 2) for s in range(0, 16, 2)],
                 "nsa": [(0, 2), (2, 2), (4, 2), (6, 2), (8, 2), (12, 2), (14, 1)]}
        ROPE0 = {"diff": 0, "nsa": 8}

        def C(name, a=0, n=None):
            c0, width = C0[name]
            return cst[:, c0 + a:c0 + a + (width - a if n is None else n)]

        def mem_units(layer):
            units = []
            for h in range(MEM_HEADS):
                kv = 2 * DC + 8 * layer + 2 * h
                u = dict(kind="mem", scale=MEM_SCALE, keys=S, group=h, last=True, S=[], T=[], PV=[])
                for m in range(2):
                    u["S"].append(([(A[:, 2 * h + c, m * P:(m + 1) * P], MKV[:, 8 * layer + 2 * h + c, :])
                                    for c in range(2)], []))
                for m in range(2):
                    for kt in range(NT):
                        u["T"].append((m, kt * P, P, kt * S + m * P))
                for e in range(2):
                    u["PV"] += [((slice(0, P), e * S, S), MKV[:, kv + kt, e * P:(e + 1) * P],
                                 (P, kt * S, S), kt == 0, kt == NT - 1) for kt in range(NT)]
                units.append(u)
            return units

        def diff_units():
            units = []
            for h in range(DIFF_HEADS):
                for qt in range(NT):
                    nk = (qt + 1) * P
                    u = dict(kind="diff", scale=DIFF_SCALE, keys=nk, group=h, last=qt == NT - 1, S=[], T=[], PV=[])
                    for m in range(2):
                        r = slice(64 * m, 64 * m + 64)
                        u["S"].append(([(A[r, h, qt * P:(qt + 1) * P], A[r, 8 + h, 0:nk])],
                                       [(causal_b, nk - P, P)]))
                    for kt in range(qt + 1):
                        u["T"].append((0, kt * P, P, kt * P))
                        u["PV"].append(((slice(0, P), qt * P, P),
                                        MKV[:, 2 * DC + 2 * (h // 2) + kt, (h % 2) * P:(h % 2 + 1) * P],
                                        (P, kt * P, P), kt == 0, kt == qt))
                    units.append(u)
            return units

        def nsa_units():
            units = []
            for c in range(8):
                swa = c >= 4
                for qt in range(NT):
                    branches = ["swa"] if swa else ["slc", "win", "cmp"]
                    for b, kind in enumerate(branches):
                        nk = NCMP if kind == "cmp" else (qt + 1) * P
                        u = dict(kind=kind, scale=NSA_SCALE, keys=nk, group=c, S=[], T=[], PV=[], qt=qt, c=c,
                                 last=qt == NT - 1 and b == len(branches) - 1)
                        for m in range(2):
                            r = slice(64 * m, 64 * m + 64)
                            k = {"slc": A[r, 12, 0:nk], "win": A[r, 13, 0:nk], "swa": A[r, 14, 0:nk],
                                 "cmp": KCm[r, 0:NCMP]}[kind]
                            masks = [(causal_b, nk - P, P)] if kind != "cmp" else [(cmask_b[:, 16 * qt:16 * qt + NCMP], 0, NCMP)]
                            if kind == "swa" and qt == 1:
                                masks.append((band_b, 0, P))
                            u["S"].append(([(A[r, c, qt * P:(qt + 1) * P], k)], masks))
                            first, end = b == 0, b == len(branches) - 1
                            kts = 1 if kind == "cmp" else qt + 1
                            for kt in range(kts):
                                n = NCMP if kind == "cmp" else P
                                u["T"].append((m, kt * P, n, m * S + kt * P))
                                v = (VCm[0:NCMP, 64 * m:64 * m + 64] if kind == "cmp" else
                                     V2[:, kt, {"slc": 0, "win": P, "swa": 2 * P}[kind] + 64 * m:][:, 0:64])
                                u["PV"].append(((r, qt * P, P), v, (n, m * S + kt * P, P),
                                                first and kt == 0, end and kt == kts - 1))
                        units.append(u)
            return units

        ATTN = {"attn_mem0": mem_units(0), "attn_diff": diff_units(), "attn_mem1": mem_units(1),
                "attn_nsa": nsa_units()}
        U0, n_units = {}, 0
        for name, _, _ in PLAN:
            if name in ATTN:
                U0[name] = n_units
                n_units += len(ATTN[name])

        def tiles_done(name):
            return T0[name] + NTILES[name]

        block = ctx.enter_context(nc.Block())

        @block.sync
        def _(sp):
            cols = lambda ap: ap.rearrange("(c p) t -> p c t", p=P)
            sp.dma_start(cst[:, :], consts).then_inc(cst_loaded, 16)
            sp.dma_start(X[:, :, :], cols(x_in)).then_inc(x_loaded, 16)
            for j in range(2):
                sp.dma_start(raw[j][:, :, :], weights[j].rearrange("p (k m) -> p k m", k=KC)).then_inc(raw_loaded[j], 16)
            sp.dma_start(UC, cols(mem_in)).then_inc(mem_loaded, 16)
            sp.dma_start(PT[:, 0, 0:S].bitcast(I32), positions.partition_broadcast(P)).then_inc(pos_loaded, 16)
            with sp.Fori(1, TILES // 2) as i:
                for j in range(2):
                    sp.wait_ge(lo_dve, 2 * i + (j - 1))
                    sp.wait_ge(lo_pool, 2 * i + (j - 1))
                    sp.dma_start(raw[j][:, :, :], weights[bass.ds(2 * i + j, 1)].rearrange("o p (k m) -> p (o k) m", k=KC))\
                        .then_inc(raw_loaded[j], 16)
            sp.wait_ge(x_final, 4)
            sp.dma_start(cols(out), X[:, :, :]).then_inc(out_done, 16)
            sp.wait_ge(out_done, 16)

        @block.gpsimd
        def _(pool):
            with pool.Fori(0, TILES // 2) as i:
                for j in range(2):
                    pool.wait_ge(hi_out, 2 * i + j + 1)
                    pool.tensor_tensor(out=wlo[j][:, LO_DVE:KC, :], in0=raw[j][:, LO_DVE:KC, :],
                                       in1=whi[j][:, LO_DVE:KC, :].bitcast(F32), op=ALU.subtract).then_inc(lo_pool, 1)

        @block.tensor
        def _(pe):
            ident = C("ident")

            def three(dst, w, wl, x, xl, first, last):
                pe.matmul(dst, w, x, start=first, stop=False)
                pe.matmul(dst, w, xl, start=False, stop=False)
                return pe.matmul(dst, wl, x, start=False, stop=last)

            def tile_in(t):
                pe.wait_ge(hi_out, t + 1)
                pe.wait_ge(lo_dve, t + 1)
                pe.wait_ge(lo_pool, t + 1)

            def stage(name, xhi, xlo, turned=False):
                with loop(pe, NTILES[name] // 2) as i:
                    for j in range(2):
                        tile_in(2 * i + (T0[name] + j))
                        pe.wait_ge(acc_free, 2 * i + (G0[name] + j + 1))
                        for m in range(2):
                            o = slice(m * P, (m + 1) * P)
                            for k in range(KC):
                                w, wl, x, xl = whi[j][:, k, :], wlo[j][:, k, :], xhi[:, k, :], xlo[:, k, :]
                                if turned:
                                    mm = three(acc[j][:, m, :], x[:, o], xl[:, o], w, wl, k == 0, k == KC - 1)
                                else:
                                    mm = three(acc[j][:, m, :], w[:, o], wl[:, o], x, xl, k == 0, k == KC - 1)
                        mm.then_inc(tile_done, 1)

            def down(name):
                with loop(pe, 2) as i:
                    for g in range(2):
                        pe.wait_ge(acc_free, 2 * i + (G0[name] + g + 1))
                        for part in range(3):
                            j = (3 * g + part) % 2
                            ks = range(8 * part, min(8 * part + 8, FC))
                            tile_in(6 * i + (T0[name] + 3 * g + part))
                            for m in range(2):
                                for k in ks:
                                    o = slice(m * P, (m + 1) * P)
                                    mm = three(accd[g][m], whi[j][:, k - 8 * part, o], wlo[j][:, k - 8 * part, o],
                                               FH[:, k, :], FL[:, k, :], m == k == 0, m == 1 and k == FC - 1)
                            mm.then_inc(tile_done, 1)

            def stats(name, jobs):
                if N0[name] > 0:
                    pe.wait_ge(spread_used, N0[name])
                for col, chunks, tt in jobs:
                    for n, ap in enumerate(chunks):
                        mm = pe.matmul(st[:, col:col + 1], ap[:, tt * P:(tt + 1) * P], ones[:, 0:1],
                                       start=n == 0, stop=n == len(chunks) - 1)
                mm.then_inc(stat_ready, 1)

            def spread(name, jobs=None):
                pe.wait_ge(rt_ready, N0[name] + 1)
                for col, dst in jobs or [(tt, st[:, tt * P:(tt + 1) * P]) for tt in range(NT)]:
                    mm = pe.matmul(dst, rt[:, N0[name], col:col + 1].broadcast_to((P, P)), ident, start=True, stop=True)
                mm.then_inc(spread_ready, 1)

            def norm(name, src=SQ):
                stats(name, [(tt, [src[:, k, :] for k in range(DC)], tt) for tt in range(NT)])
                spread(name)

            def rotate(which, perm):
                for n, (slot, w) in enumerate(ROPES[which]):
                    r = ROPE0[which] + n
                    if n >= 4:
                        pe.wait_ge(rot_used, r - 3)
                    pe.matmul(sc[:, n % 4, 0:w * S], C(perm), A[:, slot:slot + w, :], start=True, stop=True)\
                        .then_inc(rot_ready, 1)

            def attention(name):
                units, u0 = ATTN[name], U0[name]
                for s in range(len(units) + 2):
                    if s < len(units):
                        u, n = units[s], u0 + s
                        if n >= 2:
                            pe.wait_ge(exp_done, n - 1)
                        for m, (products, masks) in enumerate(u["S"]):
                            dst = sc[:, 2 * (n % 2) + m, :]
                            for k, (q, key) in enumerate(products):
                                mm = pe.matmul(dst[:, 0:u["keys"]], q, key, start=k == 0,
                                               stop=k == len(products) - 1 and not masks)
                            for k, (mask, c0, w) in enumerate(masks):
                                mm = pe.matmul(dst[:, c0:c0 + w], ident_b[:, :], mask if w < P else mask[:, :],
                                               start=False, stop=k == len(masks) - 1)
                        mm.then_inc(s_done, 1)
                    if 1 <= s <= len(units):
                        u, n = units[s - 1], u0 + s - 1
                        pe.wait_ge(p_ready, n + 1)
                        if n >= 1:
                            pe.wait_ge(pt_ready, n)
                        for m, c0, w, to in u["T"]:
                            mm = pe.transpose(tp[0:w, to:to + P], E[:, n % 2, m, c0:c0 + w], ident)
                        mm.then_inc(t_done, 1)
                    if s >= 2:
                        u, n = units[s - 2], u0 + s - 2
                        g = G0[name] + u["group"]
                        pe.wait_ge(pt_ready, n + 1)
                        pe.wait_ge(acc_free, g + 1)
                        for (rows, c0, w), v, (kn, p0, pw), first, last in u["PV"]:
                            dst = acc[g % 2][:, :, :].rearrange("p a b -> p (a b)")
                            mm = pe.matmul(dst[rows, c0:c0 + w], v, PT[0:kn, n % 2, p0:p0 + pw], start=first, stop=last)
                        mm.then_inc(pv_done, 1)

            def wait_h(name):
                pe.wait_ge(s_h, h.at(name))

            accd = [[acc[g][:, m, :] for m in range(2)] for g in range(2)]
            pe.wait_ge(consts_ready, 1)
            pe.wait_ge(s_sq, sq.at("mix0"))
            norm("mix0")
            wait_h("x0")
            stage("pw1", Hhi, Hlo)
            wait_h("mem")
            stage("memk", H2hi, H2lo)
            stage("memv", H2hi, H2lo, turned=True)
            pe.wait_ge(conv_done, 8)
            norm("ln_mu", UC)
            pe.wait_ge(s_sq, sq.at("ln"))
            norm("ln_var")
            wait_h("ln")
            stage("pw2", Ohi, Olo)
            for layer, before in ((0, "pw2"), (1, "diffo")):
                pe.wait_ge(s_sq, sq.at(before))
                norm(f"mem{layer}")
                wait_h(before)
                stage(f"memq{layer}", Hhi, Hlo)
                pe.wait_ge(acc_free, G0[f"attn_mem{layer}"] + 2)
                attention(f"attn_mem{layer}")
                wait_h(f"attn_mem{layer}")
                stage(f"memo{layer}", Ohi, Olo)
                pe.wait_ge(s_sq, sq.at(f"memo{layer}"))
                norm(f"ffn{layer}")
                wait_h(f"memo{layer}")
                stage(f"gu{layer}", Hhi, Hlo)
                wait_h(f"gu{layer}")
                down(f"down{layer}")
                pe.wait_ge(s_sq, sq.at(f"down{layer}"))
                if layer == 1:
                    break
                norm("attn1")
                wait_h("down0")
                stage("diffk", Hhi, Hlo)
                stage("diffv", Hhi, Hlo, turned=True)
                stage("diffq", H2hi, H2lo)
                pe.wait_ge(acc_free, G0["attn_diff"] + 2)
                rotate("diff", "perm1")
                pe.wait_ge(rot_used, ROPE0["nsa"])
                attention("attn_diff")
                pe.wait_ge(s_sq, sq.at("attn_diff"))
                stats("sub", [(2 * hd + tt, [SQ[:, hd, :]], tt) for hd in range(DIFF_HEADS) for tt in range(NT)])
                spread("sub", [(2 * hd + tt, sc[:, hd // 2, (hd % 2) * S + tt * P:][:, 0:P])
                               for hd in range(DIFF_HEADS) for tt in range(NT)])
                wait_h("sub")
                stage("diffo", Ohi, Olo)
            norm("final")
            pe.wait_ge(s_sq, sq.at("final"))
            norm("pre2")
            wait_h("final")
            stage("win", Hhi, Hlo)
            stage("winv", Hhi, Hlo, turned=True)
            pe.wait_ge(acc_free, G0["cmp"] + 2)
            rotate("nsa", "perm2")
            for kv in range(2):
                pe.wait_ge(s_h, h.at("z", kv + 1))
                pe.wait_ge(acc_free, G0["cmp"] + kv + 1)
                for part in range(2):
                    tile_in(T0["cmp"] + 2 * kv + part)
                    for m in range(2):
                        for k in range(KC):
                            o = slice(m * P, (m + 1) * P)
                            z = [FHf[:, (2 * kv + l) * 480 + (8 * part + k) * 30:][:, 0:30] for l in range(2)]
                            mm = three(acc[kv][:, m, 0:30], whi[part][:, k, o], wlo[part][:, k, o], z[0], z[1],
                                       part == m == k == 0, part == m == 1 and k == KC - 1)
                    mm.then_inc(tile_done, 1)
            pe.wait_ge(hid_ready, 2)
            pe.wait_ge(spread_used, N0["pre2"] + 1)
            for hd in range(2):
                for m in range(2):
                    pe.matmul(st[64 * hd:64 * hd + 64, 0:NCMP], C("cmp_w2", 64 * m, 64),
                              HCm[:, 0, m, hd * NCMP:(hd + 1) * NCMP], start=m == 0, stop=m == 1)
            for hd in range(2):
                for m in range(2):
                    mm = pe.matmul(tp[0:NCMP, 64 * hd:64 * hd + 64], HCm[:, 1, m, hd * NCMP:(hd + 1) * NCMP],
                                   C("cmp_w2", 128 + 64 * m, 64), start=m == 0, stop=m == 1)
            mm.then_inc(cmp_mm, 1)
            pe.wait_ge(cmp_ready, 1)
            pe.wait_ge(rot_used, ROPE0["nsa"] + len(ROPES["nsa"]))
            attention("attn_nsa")
            pe.wait_ge(s_sq, sq.at("attn_nsa"))
            stats("out2", [(2 * b + tt, [SQ[:, 4 * b + k, :] for k in range(4)], tt) for b in range(2) for tt in range(NT)])
            spread("out2", [(2 * b + tt, sc[:, 0, b * S + tt * P:][:, 0:P]) for b in range(2) for tt in range(NT)])
            wait_h("outn")
            stage("wout", Ohi, Olo)
            pe.wait_ge(s_sq, sq.at("wout"))
            norm("post2")
            pe.wait_ge(s_sq, sq.at("post"))
            norm("fpre2")
            wait_h("post")
            stage("up2", Hhi, Hlo)
            wait_h("up2")
            down("down2")
            pe.wait_ge(s_sq, sq.at("down2"))
            norm("fpost2")

        @block.scalar
        def _(act):
            ac = Chain(act, act_chain)

            def split(load, j, done=None):
                act.wait_ge(raw_loaded[j], load)
                if done is not None:
                    act.wait_ge(tile_done, done)
                act.activation(whi[j][:, :, :], raw[j][:, :, :], ACT.Copy).then_inc(hi_out, 1)

            def ahead(name, i, per, k, last=False):
                if not last:
                    t = T0[name] + k
                    split(16 * (per // 2) * i + 16 * (t // 2 + 2), k % 2, per * i + (t + 1))

            def acc_out(name, g):
                act.wait_ge(acc_free, g + (G0[name] + 3))

            def hi_scaled(dst, src, gain, g0):
                for c in range(2):
                    ins = act.activation(dst[:, c, :], src[:, c, :], ACT.Copy, scale=gain(g0 + c))
                return ins

            def gcol(name):
                return lambda c: cst[:, bass.ds(c + C0[name][0], 1)] if not isinstance(c, int) else C(name, c, 1)

            def pair(t, c):
                return t[:, bass.ds(c, 2), :] if not isinstance(c, int) else t[:, c:c + 2, :]

            def residual(name, per, outs, last_stage=False):
                n = 2
                for start, stop in ([(0, 2)] if not last_stage else [(0, 1), (1, 2)]):
                    with loop(act, stop, start) as i:
                        for g in range(2):
                            for k in range(per // 2):
                                kk = g * per // 2 + k
                                ahead(name, i, per, kk, last=last_stage and start == 1 and kk >= per - 2)
                            c = 4 * i + 2 * g
                            acc_out(name, 2 * i + g)
                            src = X if name not in ("wout", "down2") else M2
                            for b, gain in outs:
                                ins = hi_scaled(pair(b, c), pair(src, c), gcol(gain), c)
                            if outs:
                                ins.then_inc(s_taken, 1)
                            act.activation(pair(SQ, c), pair(src, c), ACT.Square).then_inc(s_sq, 1)

            def plain(name):
                with loop(act, NTILES[name] // 2) as i:
                    for j in range(2):
                        ahead(name, i, 2, j)

            def ffn(name, func):
                with loop(act, 11) as i:
                    ahead(name, i, 2, 0)
                    if name == "up2":
                        act.wait_ge(s_given, 2 * i + given.at(name, 1))
                        for c in range(2):
                            ins = act.activation(SG[:, c, :], E[:, 0, c, :], func, bias=gcol("cb2")(4 * i + c))
                        ins.then_inc(s_taken, 1)
                    else:
                        acc_out(name, 2 * i)
                        act.activation(SG[:, :, :], TG[:, :, 2:2 + S], func).then_inc(s_taken, 1)
                    ahead(name, i, 2, 1)
                    act.wait_ge(s_given, 2 * i + given.at(name, 2) if name == "up2" else i + given.at(name, 1))
                    act.activation(pair(FH, 2 * i), E[:, 1, :, :] if name == "up2" else TU[:, :, 2:2 + S],
                                   ACT.Copy).then_inc(s_taken, 1)

            def attention(name):
                units, u0 = ATTN[name], U0[name]
                for s in range(len(units) + 3):
                    if s < len(units):
                        u, n = units[s], u0 + s
                        act.wait_ge(nb_ready, n + 1)
                        if n >= 2:
                            act.wait_ge(t_done, n - 1)
                        for m in range(2):
                            ins = act.activation(E[:, n % 2, m, 0:u["keys"]], sc[:, 2 * (n % 2) + m, 0:u["keys"]], ACT.Exp,
                                                 bias=nb[:, n % 2, m:m + 1], scale=u["scale"],
                                                 accum_out=rs[:, n % 2, m:m + 1])
                        if u["kind"] == "swa":
                            ins = act.activation(ske[:, n % 2, :], sk[:, n % 2, :], ACT.Exp)
                        ins.then_inc(exp_done, 1)
                    if 1 <= s <= len(units):
                        u, n = units[s - 1], u0 + s - 1
                        act.wait_ge(t_done, n + 1)
                        if n >= 2:
                            act.wait_ge(pv_done, n - 1)
                        rows = u["T"][0][2]
                        if u["kind"] == "cmp":
                            a, b = (t.rearrange("p (m k) -> p m k", m=2)[0:rows, :, 0:P] for t in (PT[:, n % 2, :], tp[:, :]))
                        elif u["kind"] in ("mem", "diff") or u["keys"] == S:
                            w = max(to for *_, to in u["T"]) + P
                            a, b = PT[:, n % 2, 0:w], tp[:, 0:w]
                        else:
                            a, b = (t.rearrange("p (m k) -> p m k", m=2)[:, :, 0:P] for t in (PT[:, n % 2, :], tp[:, :]))
                        act.activation(a, b, ACT.Copy).then_inc(pt_ready, 1)
                    if s >= 3 and units[s - 3]["last"]:
                        g = units[s - 3]["group"]
                        acc_out(name, g)
                        if "mem" in name:
                            act.activation(Ohi[:, 2 * g:2 * g + 2, :], A[:, 2 * g:2 * g + 2, :], ACT.Copy).then_inc(s_taken, 1)
                        else:
                            act.activation(SQ[:, g, :], A[:, g, :], ACT.Square).then_inc(s_sq, 1)

            act.wait_ge(cst_loaded, 16)
            act.wait_ge(x_loaded, 16)
            act.activation(SQ[:, :, :], X[:, :, :], ACT.Square).then_inc(s_sq, 1)
            for c in range(DC):
                ins = act.activation(Hhi[:, c, :], X[:, c, :], ACT.Copy, scale=C("g_mix0", c, 1))
            ins.then_inc(s_taken, 1)
            for j in range(2):
                split(16, j)
            act.wait_ge(mem_loaded, 16)
            act.activation(H2hi[:, :, :], UC, ACT.Copy).then_inc(s_taken, 1)
            act.wait_ge(s_given, given.at("lam"))
            act.activation(lam[:, 2:4], lam[:, 0:2], ACT.Exp).then_inc(s_taken, 1)
            act.wait_ge(s_given, given.at("rope"))
            act.activation(rope_s[:, :], TG[:, 0, 0:S], ACT.Sin)
            act.activation(rope_c[:, :], TG[:, 1, 0:S], ACT.Sin).then_inc(s_taken, 1)
            with loop(act, 4) as i:
                ahead("pw1", i, 2, 0)
                ahead("pw1", i, 2, 1)
                acc_out("pw1", 2 * i + 1)
                for c in range(2):
                    ins = act.activation(SG[:, c, :], TU[:, c, 2:2 + S], ACT.Sigmoid, bias=gcol("b_pw1")(4 * i + (2 + c)))
                ins.then_inc(s_taken, 1)
            plain("memk")
            plain("memv")
            act.wait_ge(s_given, given.at("ln_sq"))
            act.activation(SQ[:, :, :], UC, ACT.Square).then_inc(s_sq, 1)
            for p in range(4):
                act.wait_ge(s_given, given.at("ln", p + 1))
                for c in range(2 * p, 2 * p + 2):
                    ac.link(act.activation(SQ[:, c, :], UC[:, c, :], ACT.Silu, scale=C("ln_g", c, 1), bias=C("ln_b", c, 1)))
                act.activation(Ohi[:, 2 * p:2 * p + 2, :], SQ[:, 2 * p:2 * p + 2, :], ACT.Copy).then_inc(s_taken, 1)
            residual("pw2", 2, [(Hhi, "g_mem0")])
            for layer in range(2):
                plain(f"memq{layer}")
                attention(f"attn_mem{layer}")
                residual(f"memo{layer}", 2, [(Hhi, f"g_ffn{layer}")])
                ffn(f"gu{layer}", ACT.Silu)
                if layer == 1:
                    break
                residual("down0", 6, [(Hhi, "g_kv"), (H2hi, "g_mix1")])
                plain("diffk")
                plain("diffv")
                plain("diffq")
                attention("attn_diff")
                for p in range(4):
                    act.wait_ge(s_given, given.at("sub", p + 1))
                    act.activation(Ohi[:, 2 * p:2 * p + 2, :], A[:, 2 * p:2 * p + 2, :], ACT.Copy,
                                   scale=gsub[:, 0:1]).then_inc(s_taken, 1)
                residual("diffo", 2, [(Hhi, "g_mem1")])
            residual("down1", 6, [])

            def ready_chunks(name, src, dst, gain, squares=True):
                for p in range(4):
                    act.wait_ge(s_given, given.at(name, p + 1))
                    hi_scaled(pair(dst, 2 * p), pair(src, 2 * p), gcol(gain), 2 * p).then_inc(s_taken, 1)
                    if squares:
                        act.activation(pair(SQ, 2 * p), pair(src, 2 * p), ACT.Square).then_inc(s_sq, 1)

            ready_chunks("final", X, Hhi, "g_pre2")
            plain("win")
            plain("winv")
            acc_out("winv", 1)
            act.activation(gates[:, :, :], V2[:, :, 3 * P:3 * P + 24], ACT.Sigmoid).then_inc(s_taken, 1)
            for kv in range(2):
                act.wait_ge(s_given, given.at("z", kv + 1))
                act.activation(FHf[:, 2 * kv * 480:(2 * kv + 1) * 480], ZT, ACT.Copy).then_inc(s_taken, 1)
            for kv in range(2):
                ahead("cmp", 0, 4, 2 * kv)
                ahead("cmp", 0, 4, 2 * kv + 1)
                acc_out("cmp", kv)
                act.activation(HCm[:, kv, :, 0:30], TG[:, :, 2 + 30 * kv:32 + 30 * kv], ACT.Gelu_apprx_tanh).then_inc(hid_ready, 1)
            attention("attn_nsa")
            ready_chunks("outn", A, Ohi, "g_out2", squares=False)
            residual("wout", 2, [])
            ready_chunks("post", X, Hhi, "g_fpre2")
            ffn("up2", ACT.Gelu_apprx_tanh)
            residual("down2", 6, [], last_stage=True)

        @block.vector
        def _(dve):
            ch = Chain(dve, dve_chain)
            link = ch.link
            f = lambda ap: ap.bitcast(F32)

            def lower(j, after):
                dve.wait_ge(hi_out, after)
                dve.tensor_tensor(out=wlo[j][:, 0:LO_DVE, :], in0=raw[j][:, 0:LO_DVE, :], in1=f(whi[j][:, 0:LO_DVE, :]),
                                  op=ALU.subtract).then_inc(lo_dve, 1)

            def tile(name, i, per, k, last=False):
                if not last:
                    lower(k % 2, per * i + (T0[name] + k + 3))
                dve.wait_ge(tile_done, per * i + (T0[name] + k + 1))

            def col(name, c):
                return cst[:, bass.ds(c + C0[name][0], 1)] if not isinstance(c, int) else C(name, c, 1)

            def pair(t, c):
                return t[:, bass.ds(c, 2), :] if not isinstance(c, int) else t[:, c:c + 2, :]

            def both(ap):
                return ap.unsqueeze(1).broadcast_to((P, 2, S))

            def out_acc(ins):
                ins.then_inc(acc_free, 1)

            def lo_scaled(dst, src, hi, name, c):
                for k in range(2):
                    ins = dve.scalar_tensor_tensor(out=dst[:, k, :], in0=src[:, k, :], scalar=col(name, c + k),
                                                   in1=f(hi[:, k, :]), op0=ALU.mult, op1=ALU.subtract)
                return ins

            def rsqrt(name, n, div, eps):
                dve.wait_ge(stat_ready, N0[name] + 1)
                v, y, a, b = (nw[:, q, 0:n] for q in range(4))
                link(dve.tensor_scalar(v, st[:, 0:n], 1.0 / div, eps, op0=ALU.mult, op1=ALU.add))
                link(dve.tensor_scalar(nwi[:, 0:n], v.bitcast(I32), 1, None, op0=ALU.logical_shift_right))
                link(dve.tensor_scalar(y.bitcast(I32), nwi[:, 0:n], -1, 0x5F3759DF, op0=ALU.mult, op1=ALU.add))
                for step in range(4):
                    dst = y if step < 3 else rt[:, N0[name], 0:n]
                    link(dve.scalar_tensor_tensor(out=a, in0=y, scalar=-0.5, in1=v, op0=ALU.mult, op1=ALU.mult))
                    link(dve.tensor_tensor(out=b, in0=a, in1=y, op=ALU.mult))
                    ins = dve.scalar_tensor_tensor(out=dst, in0=b, scalar=1.5, in1=y, op0=ALU.add, op1=ALU.mult)
                    if step < 3:
                        link(ins)
                ins.then_inc(rt_ready, 1)

            def take_spread(name):
                dve.wait_ge(spread_ready, N0[name] + 1)
                dve.tensor_copy(R[:, :], st[:, 0:S]).then_inc(spread_used, 1)
                dve.wait_ge(spread_used, N0[name] + 1)

            def norm(name):
                rsqrt(name, NT, D, RMS_EPS)
                take_spread(name)

            def residual(name, per, outs, last_stage=False):
                for start, stop in ([(0, 2)] if not last_stage else [(0, 1), (1, 2)]):
                    with loop(dve, stop, start) as i:
                        for g in range(2):
                            for k in range(per // 2):
                                kk = g * per // 2 + k
                                tile(name, i, per, kk, last=last_stage and start == 1 and kk >= per - 2)
                            c = 4 * i + 2 * g
                            if name in ("wout", "down2"):
                                dve.tensor_copy(pair(M2, c), acc[g][:, :, :]).then_inc(acc_free, 1)
                            elif name == "pw2":
                                dve.scalar_tensor_tensor(out=pair(X, c)[:, 0, :], in0=acc[g][:, 0, :], scalar=col("b_pw2", c),
                                                         in1=pair(X, c)[:, 0, :], op0=ALU.add, op1=ALU.add)
                                dve.scalar_tensor_tensor(out=pair(X, c)[:, 1, :], in0=acc[g][:, 1, :], scalar=col("b_pw2", c + 1),
                                                         in1=pair(X, c)[:, 1, :], op0=ALU.add, op1=ALU.add).then_inc(acc_free, 1)
                            else:
                                dve.tensor_tensor(out=pair(X, c), in0=acc[g][:, :, :], in1=pair(X, c), op=ALU.add)\
                                    .then_inc(acc_free, 1)
                            if outs:
                                dve.wait_ge(acc_free, 2 * i + (G0[name] + g + 3))
                                dve.wait_ge(s_taken, 2 * i + taken.at(name, g + 1))
                            for hi, lo, gain in outs:
                                ins = lo_scaled(pair(lo, c), pair(X, c), pair(hi, c), gain, c)
                            if outs:
                                ins.then_inc(s_h, 1)

            def project(name, dst, scaled=True):
                with loop(dve, NTILES[name] // 2) as i:
                    for j in range(2):
                        tile(name, i, 2, j)
                        if scaled:
                            ins = dve.tensor_tensor(out=pair(dst, 4 * i + 2 * j), in0=acc[j][:, :, :], in1=both(R[:, :]), op=ALU.mult)
                        else:
                            ins = dve.tensor_copy(pair(dst, 4 * i + 2 * j), acc[j][:, :, :])
                        out_acc(ins)

            def ffn(name):
                with loop(dve, 11) as i:
                    tile(name, i, 2, 0)
                    out_acc(dve.tensor_tensor(out=TG[:, :, 2:2 + S], in0=acc[0][:, :, :], in1=both(R[:, :]), op=ALU.mult))
                    tile(name, i, 2, 1)
                    out_acc(dve.tensor_tensor(out=TU[:, :, 2:2 + S], in0=acc[1][:, :, :], in1=both(R[:, :]), op=ALU.mult))
                    dve.wait_ge(acc_free, 2 * i + (G0[name] + 4))
                    dve.wait_ge(s_taken, 2 * i + taken.at(name, 1))
                    dve.tensor_tensor(out=TU[:, :, 2:2 + S], in0=TU[:, :, 2:2 + S], in1=SG[:, :, :], op=ALU.mult).then_inc(s_given, 1)
                    dve.wait_ge(s_given, i + given.at(name, 1))
                    dve.wait_ge(s_taken, 2 * i + taken.at(name, 2))
                    dve.tensor_tensor(out=pair(FL, 2 * i), in0=TU[:, :, 2:2 + S], in1=f(pair(FH, 2 * i)), op=ALU.subtract)\
                        .then_inc(s_h, 1)

            def short_conv(ch, dst, src, c):
                for k in range(2):
                    for tap in range(3):
                        w = cst[:, bass.ds(3 * (c + k) + (C0["cw2"][0] + tap), 1)]
                        s_ = src[:, k, tap:tap + S]
                        if tap == 0:
                            link(dve.tensor_scalar(dst[:, k, :], s_, w, None, op0=ALU.mult))
                        else:
                            ins = dve.scalar_tensor_tensor(out=dst[:, k, :], in0=s_, scalar=w, in1=dst[:, k, :],
                                                           op0=ALU.mult, op1=ALU.add)
                            if tap == 1 or k == 0:
                                link(ins)
                return ins

            def conv_ffn(name):
                with ch.loop(11, 5 + 6) as i:
                    tile(name, i, 2, 0)
                    out_acc(dve.tensor_tensor(out=TG[:, :, 2:2 + S], in0=acc[0][:, :, :], in1=both(R[:, :]), op=ALU.mult))
                    dve.wait_ge(acc_free, 2 * i + (G0[name] + 3))
                    short_conv(ch, E[:, 0, :, :], TG, 4 * i).then_inc(s_given, 1)
                    tile(name, i, 2, 1)
                    out_acc(dve.tensor_tensor(out=TU[:, :, 2:2 + S], in0=acc[1][:, :, :], in1=both(R[:, :]), op=ALU.mult))
                    dve.wait_ge(acc_free, 2 * i + (G0[name] + 4))
                    link(short_conv(ch, E[:, 1, :, :], TU, 4 * i + 2))
                    dve.wait_ge(s_taken, 2 * i + taken.at(name, 1))
                    for k in range(2):
                        ins = dve.scalar_tensor_tensor(out=E[:, 1, k, :], in0=E[:, 1, k, :], scalar=col("cb2", 4 * i + (2 + k)),
                                                       in1=SG[:, k, :], op0=ALU.add, op1=ALU.mult)
                    ins.then_inc(s_given, 1)
                    dve.wait_ge(s_given, 2 * i + given.at(name, 2))
                    dve.wait_ge(s_taken, 2 * i + taken.at(name, 2))
                    dve.tensor_tensor(out=pair(FL, 2 * i), in0=E[:, 1, :, :], in1=f(pair(FH, 2 * i)), op=ALU.subtract)\
                        .then_inc(s_h, 1)

            def rotate(which, cos, sin):
                for n, (slot, w) in enumerate(ROPES[which]):
                    r = ROPE0[which] + n
                    wide = lambda ap: ap.unsqueeze(1).broadcast_to((P, w, S))
                    q, t = A[:, slot:slot + w, :], E[:, n % 2, 0:w, :]
                    dve.wait_ge(rot_ready, r + 1)
                    link(dve.tensor_tensor(out=t, in0=sc[:, n % 4, 0:w * S].rearrange("p (a b) -> p a b", a=w), in1=wide(sin), op=ALU.mult))
                    link(dve.tensor_tensor(out=q, in0=q, in1=wide(cos), op=ALU.mult))
                    dve.tensor_tensor(out=q, in0=q, in1=t, op=ALU.add).then_inc(rot_used, 1)

            def attention(name):
                units, u0 = ATTN[name], U0[name]
                for s in range(len(units) + 4):
                    if s < len(units):
                        u, n = units[s], u0 + s
                        r = n % 2
                        dve.wait_ge(s_done, n + 1)
                        link(dve.reduce_max(mx[:, r, :], sc[:, 2 * r:2 * r + 2, 0:u["keys"]], axis=AX_X))
                        if u["kind"] == "swa":
                            sinks = C("sinks", 2 * (u["c"] - 4), 2)
                            link(dve.scalar_tensor_tensor(out=mx[:, r, :], in0=mx[:, r, :], scalar=u["scale"], in1=sinks,
                                                          op0=ALU.mult, op1=ALU.max))
                            link(dve.tensor_scalar(nb[:, r, :], mx[:, r, :], -1.0, None, op0=ALU.mult))
                            dve.tensor_tensor(out=sk[:, r, :], in0=nb[:, r, :], in1=sinks, op=ALU.add).then_inc(nb_ready, 1)
                        else:
                            dve.tensor_scalar(nb[:, r, :], mx[:, r, :], -u["scale"], None, op0=ALU.mult).then_inc(nb_ready, 1)
                    if 1 <= s <= len(units):
                        u, n = units[s - 1], u0 + s - 1
                        r, kind = n % 2, u["kind"]
                        dve.wait_ge(exp_done, n + 1)
                        rr = rs[:, r, :]
                        if kind == "swa":
                            link(dve.tensor_tensor(out=rr, in0=rr, in1=ske[:, r, :], op=ALU.add))
                        if kind == "cmp":
                            link(dve.tensor_scalar(rr, rr, 1e-30, None, op0=ALU.max))
                        link(dve.reciprocal(rr, rr))
                        if kind in ("slc", "win", "cmp"):
                            b = {"cmp": 0, "slc": 1, "win": 2}[kind]
                            gate = gates[:, u["qt"], 8 * b + 2 * u["c"]:][:, 0:2]
                            if kind == "cmp":
                                link(dve.scalar_tensor_tensor(out=rr, in0=rr, scalar=C("rowok", u["qt"], 1), in1=gate,
                                                              op0=ALU.mult, op1=ALU.mult))
                            else:
                                link(dve.tensor_tensor(out=rr, in0=rr, in1=gate, op=ALU.mult))
                        if kind == "diff":
                            link(dve.tensor_scalar(rr[:, 1:2], rr[:, 1:2], lam[:, 0:1], None, op0=ALU.mult))
                        e = [E[:, r, m, 0:u["keys"]] for m in range(2)]
                        ins = dve.tensor_scalar(e[0], e[0], rr[:, 0:1], None, op0=ALU.mult)
                        if kind == "diff":
                            link(ins)
                            ins = dve.scalar_tensor_tensor(out=e[0], in0=e[1], scalar=rr[:, 1:2], in1=e[0],
                                                           op0=ALU.mult, op1=ALU.add)
                        else:
                            ins = dve.tensor_scalar(e[1], e[1], rr[:, 1:2], None, op0=ALU.mult)
                        ins.then_inc(p_ready, 1)
                    if 2 <= s < len(units) + 2 and units[s - 2]["last"]:
                        n, g = u0 + s - 2, units[s - 2]["group"]
                        a = acc[(G0[name] + g) % 2]
                        dve.wait_ge(pv_done, n + 1)
                        if "mem" in name:
                            out_acc(dve.tensor_copy(A[:, 2 * g:2 * g + 2, :], a[:, :, :]))
                        else:
                            out_acc(dve.tensor_copy(A[:, g, :], a[:, 0, :]))
                    if "mem" in name and s >= 4:
                        g = units[s - 4]["group"]
                        dve.wait_ge(s_taken, taken.at(name, g + 1))
                        dve.tensor_tensor(out=Olo[:, 2 * g:2 * g + 2, :], in0=A[:, 2 * g:2 * g + 2, :],
                                          in1=f(Ohi[:, 2 * g:2 * g + 2, :]), op=ALU.subtract).then_inc(s_h, 1)

            dve.memset(ones[:, :], 1.0)
            dve.memset(TG[:, :, :], 0.0)
            link(dve.memset(TU[:, :, :], 0.0))
            dve.memset(U[:, :, 0:CONV - 1], 0.0).then_inc(acc_free, 2)
            dve.wait_ge(cst_loaded, 16)
            dve.tensor_copy(ident_b[:, :], C("ident"))
            dve.tensor_copy(causal_b[:, :], C("causal"))
            dve.tensor_copy(band_b[:, :], C("band"))
            dve.tensor_copy(cmask_b[:, :], C("cmask")).then_inc(consts_ready, 1)
            dve.wait_ge(x_loaded, 16)
            norm("mix0")
            dve.wait_ge(s_taken, taken.at("x0"))
            for c in range(0, DC, 2):
                ins = lo_scaled(Hlo[:, c:c + 2, :], X[:, c:c + 2, :], Hhi[:, c:c + 2, :], "g_mix0", c)
            ins.then_inc(s_h, 1)
            for j in range(2):
                lower(j, j + 1)
            dve.wait_ge(mem_loaded, 16)
            dve.wait_ge(s_taken, taken.at("mem"))
            dve.tensor_tensor(out=H2lo[:, :, :], in0=UC, in1=f(H2hi[:, :, :]), op=ALU.subtract).then_inc(s_h, 1)
            lv = C("lam").rearrange("p (a b c) -> p a b c", a=2, b=2)
            prod = TU[:, 1, 0:P].rearrange("p (a c) -> p a c", a=2)
            link(dve.tensor_tensor(out=prod, in0=lv[:, :, 0, :], in1=lv[:, :, 1, :], op=ALU.mult))
            dve.reduce_sum(lam[:, 0:2], prod, axis=AX_X).then_inc(s_given, 1)
            dve.wait_ge(s_taken, taken.at("lam"))
            link(dve.tensor_tensor(out=lam[:, 0:1], in0=lam[:, 3:4], in1=lam[:, 2:3], op=ALU.subtract))
            link(dve.tensor_scalar(lam[:, 0:1], lam[:, 0:1], -LAMBDA_INIT, None, op0=ALU.add))
            link(dve.tensor_scalar(gsub[:, :], C("g_sub"), 1.0 - LAMBDA_INIT, None, op0=ALU.mult))
            dve.wait_ge(pos_loaded, 16)
            ang, turn, r0, r1 = TU[:, 0, 0:S], TU[:, 1, 0:S], TG[:, 0, 0:S], TG[:, 1, 0:S]
            link(dve.tensor_copy(ang, PT[:, 0, 0:S].bitcast(I32)))
            link(dve.tensor_scalar(ang, ang, C("invf"), None, op0=ALU.mult))
            link(dve.tensor_scalar(turn, ang, 1.0 / (2 * math.pi), MAGIC, op0=ALU.mult, op1=ALU.add))
            link(dve.tensor_scalar(turn, turn, -MAGIC, None, op0=ALU.add))
            for k, part in enumerate(TWO_PI):
                link(dve.scalar_tensor_tensor(out=r0, in0=turn, scalar=-part, in1=ang if k == 0 else r0,
                                              op0=ALU.mult, op1=ALU.add))
            link(dve.tensor_scalar(r0, r0, -PI_IN, PI_IN, op0=ALU.max, op1=ALU.min))
            link(dve.scalar_tensor_tensor(out=r1, in0=r0, scalar=-1.0, in1=r0, op0=ALU.mult, op1=ALU.max))
            dve.tensor_scalar(r1, r1, -1.0, math.pi / 2, op0=ALU.mult, op1=ALU.add).then_inc(s_given, 1)
            dve.wait_ge(s_taken, taken.at("rope"))
            with loop(dve, 4) as i:
                tile("pw1", i, 2, 0)
                out_acc(dve.tensor_tensor(out=TG[:, :, 2:2 + S], in0=acc[0][:, :, :], in1=both(R[:, :]), op=ALU.mult))
                tile("pw1", i, 2, 1)
                out_acc(dve.tensor_tensor(out=TU[:, :, 2:2 + S], in0=acc[1][:, :, :], in1=both(R[:, :]), op=ALU.mult))
                dve.wait_ge(s_taken, i + taken.at("pw1", 1))
                for k in range(2):
                    ins = dve.scalar_tensor_tensor(out=U[:, bass.ds(2 * i + k, 1), CONV - 1:CONV - 1 + S].rearrange("p o s -> p (o s)"),
                                                   in0=TG[:, k, 2:2 + S], scalar=col("b_pw1", 4 * i + k), in1=SG[:, k, :],
                                                   op0=ALU.add, op1=ALU.mult)
                    ins.then_inc(u_ready, 1)
                dve.wait_ge(u_ready, 2 * i + 2)
            for base, name, slots in ((0, "memk", 0), (4, "memv", 2 * DC)):
                with ch.loop(4, CONV - 1) as i:
                    for j in range(2):
                        tile(name, i, 2, j)
                        out_acc(dve.tensor_copy(pair(MKV, 4 * i + (slots + 2 * j)), acc[j][:, :, :]))
                        if j == 0:
                            taps = range(CONV // 2)
                        else:
                            taps = range(CONV // 2, CONV)
                        for tap in taps:
                            w = cst[:, bass.ds(CONV * i + (C0["w_dw"][0] + CONV * base + tap), 1)]
                            src = U[:, bass.ds(i + base, 1), tap:tap + S].rearrange("p o s -> p (o s)")
                            dst = UC[:, bass.ds(i + base, 1), :].rearrange("p o s -> p (o s)")
                            if tap == 0:
                                link(dve.tensor_scalar(dst, src, w, col("b_dw", i + base), op0=ALU.mult, op1=ALU.add))
                            else:
                                ins = dve.scalar_tensor_tensor(out=dst, in0=src, scalar=w, in1=dst, op0=ALU.mult, op1=ALU.add)
                                if tap < CONV - 1:
                                    link(ins)
                                else:
                                    ins.then_inc(conv_done, 1)
            dve.wait_ge(conv_done, 8)
            dve.wait_ge(stat_ready, N0["ln_mu"] + 1)
            dve.tensor_scalar(rt[:, N0["ln_mu"], 0:NT], st[:, 0:NT], 1.0 / D, None, op0=ALU.mult).then_inc(rt_ready, 1)
            take_spread("ln_mu")
            all8 = lambda ap: ap.unsqueeze(1).broadcast_to((P, DC, S))
            dve.tensor_tensor(out=UC, in0=UC, in1=all8(R[:, :]), op=ALU.subtract).then_inc(s_given, 1)
            rsqrt("ln_var", NT, D, LN_EPS)
            take_spread("ln_var")
            dve.wait_ge(s_given, given.at("ln_sq"))
            for p in range(4):
                dve.tensor_tensor(out=UC[:, 2 * p:2 * p + 2, :], in0=UC[:, 2 * p:2 * p + 2, :], in1=both(R[:, :]), op=ALU.mult)\
                    .then_inc(s_given, 1)
            for p in range(4):
                dve.wait_ge(s_taken, taken.at("ln", p + 1))
                dve.tensor_tensor(out=Olo[:, 2 * p:2 * p + 2, :], in0=SQ[:, 2 * p:2 * p + 2, :],
                                  in1=f(Ohi[:, 2 * p:2 * p + 2, :]), op=ALU.subtract).then_inc(s_h, 1)
            residual("pw2", 2, [(Hhi, Hlo, "g_mem0")])

            def values(name, dst, norm_name):
                with loop(dve, NTILES[name] // 2) as i:
                    for j in range(2):
                        tile(name, i, 2, j)
                        for tt in range(NT):
                            ins = dve.tensor_scalar(dst(i, j, tt), acc[j][:, tt, :], rt[:, N0[norm_name], tt:tt + 1], None, op0=ALU.mult)
                        out_acc(ins)

            def slot(t, c):
                return t[:, bass.ds(c, 1), :].rearrange("p o s -> p (o s)") if not isinstance(c, int) else t[:, c, :]

            for layer in range(2):
                norm(f"mem{layer}")
                project(f"memq{layer}", A)
                dve.wait_ge(acc_free, G0[f"attn_mem{layer}"] + 2)
                attention(f"attn_mem{layer}")
                residual(f"memo{layer}", 2, [(Hhi, Hlo, f"g_ffn{layer}")])
                norm(f"ffn{layer}")
                ffn(f"gu{layer}")
                if layer == 1:
                    break
                residual("down0", 6, [(Hhi, Hlo, "g_kv"), (H2hi, H2lo, "g_mix1")])
                norm("attn1")
                project("diffk", A[:, 8:16, :])
                values("diffv", lambda i, j, tt: slot(MKV, 4 * i + (2 * DC + 2 * j + tt)), "attn1")
                project("diffq", A[:, 0:8, :])
                dve.wait_ge(acc_free, G0["attn_diff"] + 2)
                rotate("diff", rope_c[:, :], rope_s[:, :])
                attention("attn_diff")
                rsqrt("sub", 16, P, SUBLN_EPS)
                dve.wait_ge(spread_ready, N0["sub"] + 1)
                dve.wait_ge(acc_free, G0["attn_diff"] + 8 + 2)
                for p in range(4):
                    q = A[:, 2 * p:2 * p + 2, :]
                    dve.tensor_tensor(out=q, in0=sc[:, p, :].rearrange("p (a b) -> p a b", a=2), in1=q, op=ALU.mult).then_inc(s_given, 1)
                for p in range(4):
                    dve.wait_ge(s_taken, taken.at("sub", p + 1))
                    q = slice(2 * p, 2 * p + 2)
                    dve.scalar_tensor_tensor(out=Olo[:, q, :], in0=A[:, q, :], scalar=gsub[:, 0:1], in1=f(Ohi[:, q, :]),
                                             op0=ALU.mult, op1=ALU.subtract).then_inc(s_h, 1)
                dve.sem_inc(spread_used, 1)
                residual("diffo", 2, [(Hhi, Hlo, "g_mem1")])
            residual("down1", 6, [])

            def lower_chunks(name, dst, src, hi, gain):
                for p in range(4):
                    dve.wait_ge(s_taken, taken.at(name, p + 1))
                    lo_scaled(pair(dst, 2 * p), pair(src, 2 * p), pair(hi, 2 * p), gain, 2 * p).then_inc(s_h, 1)

            norm("final")
            for c in range(DC):
                ins = dve.scalar_tensor_tensor(out=X[:, c, :], in0=X[:, c, :], scalar=C("g_final", c, 1), in1=R[:, :],
                                               op0=ALU.mult, op1=ALU.mult)
                if c % 2:
                    ins.then_inc(s_given, 1)
            lower_chunks("final", Hlo, X, Hhi, "g_pre2")
            norm("pre2")
            project("win", A)
            values("winv", lambda i, j, tt: V2[:, tt, j * S:(j + 1) * S], "pre2")
            dve.wait_ge(acc_free, G0["cmp"] + 2)
            dve.wait_ge(s_taken, taken.at("gates"))
            rotate("nsa", C("cos2"), C("sin2"))
            dve.wait_ge(rot_used, ROPE0["nsa"] + len(ROPES["nsa"]))
            for kv in range(2):
                if kv:
                    dve.wait_ge(s_h, h.at("z", kv))
                z = ZT.rearrange("p (j h c) -> p j h c", j=16, h=2)
                for hd in range(2):
                    for half in range(2):
                        rows = slice(64 * half, 64 * half + 64)
                        for jh in range(2):
                            at = (8 + 2 * kv + hd) * S + half + 16 * jh
                            src = Af[rows, at:at + 16 * NCMP].rearrange("p (c j two) -> p j c two", j=8, two=2)[:, :, :, 0]
                            pe_ = C("pe", 16 * kv + 8 * jh, 8)[rows, :].unsqueeze(2).broadcast_to((64, 8, NCMP))
                            ins = dve.tensor_tensor(out=z[rows, 8 * jh:8 * jh + 8, hd, :], in0=src, in1=pe_, op=ALU.add)
                ins.then_inc(s_given, 1)
                dve.wait_ge(s_given, given.at("z", kv + 1))
                dve.wait_ge(s_taken, taken.at("z", kv + 1))
                dve.tensor_tensor(out=FHf[:, (2 * kv + 1) * 480:(2 * kv + 2) * 480], in0=ZT,
                                  in1=f(FHf[:, 2 * kv * 480:(2 * kv + 1) * 480]), op=ALU.subtract).then_inc(s_h, 1)
            for kv in range(2):
                tile("cmp", 0, 4, 2 * kv)
                tile("cmp", 0, 4, 2 * kv + 1)
                out_acc(dve.tensor_copy(TG[:, :, 2 + 30 * kv:32 + 30 * kv], acc[kv][:, :, 0:30]))
            dve.wait_ge(cmp_mm, 1)
            dve.tensor_copy(KCm[:, 0:NCMP], st[:, 0:NCMP])
            dve.tensor_copy(VCm[0:NCMP, :], tp[0:NCMP, 0:P]).then_inc(cmp_ready, 1)
            dve.wait_ge(cmp_ready, 1)
            attention("attn_nsa")
            rsqrt("out2", 4, D // 2, RMS_EPS)
            dve.wait_ge(spread_ready, N0["out2"] + 1)
            dve.wait_ge(acc_free, G0["attn_nsa"] + 8 + 2)
            for p in range(4):
                b = p // 2
                dve.tensor_tensor(out=pair(A, 2 * p), in0=both(sc[:, 0, b * S:(b + 1) * S]), in1=pair(A, 2 * p), op=ALU.mult)\
                    .then_inc(s_given, 1)
            lower_chunks("outn", Olo, A, Ohi, "g_out2")
            dve.sem_inc(spread_used, 1)
            residual("wout", 2, [])
            norm("post2")

            def add_normed(gain, done):
                for c in range(DC):
                    link(dve.scalar_tensor_tensor(out=M2[:, c, :], in0=M2[:, c, :], scalar=C(gain, c, 1), in1=R[:, :],
                                                  op0=ALU.mult, op1=ALU.mult))
                    if c % 2:
                        dve.tensor_tensor(out=pair(X, c - 1), in0=pair(X, c - 1), in1=pair(M2, c - 1), op=ALU.add).then_inc(done, 1)

            add_normed("g_post2", s_given)
            lower_chunks("post", Hlo, X, Hhi, "g_fpre2")
            norm("fpre2")
            dve.memset(TG[:, :, 0:2], 0.0)
            link(dve.memset(TU[:, :, 0:2], 0.0))
            conv_ffn("up2")
            residual("down2", 6, [], last_stage=True)
            norm("fpost2")
            add_normed("g_fpost2", x_final)


def column_tile(w, cols, k0=0):
    part = w[k0:k0 + KC * P][:, cols]
    tile = np.zeros((KC * P, MB), w.dtype)
    tile[:part.shape[0], :part.shape[1]] = part
    return tile.reshape(KC, P, MB).transpose(1, 0, 2).reshape(P, KC * MB)


def weight_tiles(w):
    rng = lambda a, n=MB: list(range(a, a + n))
    tiles = []

    def plain(m):
        for c in range(0, m.shape[1], MB):
            tiles.append(column_tile(m, rng(c)))

    def halves(m, width):
        for c in range(0, width, MB):
            tiles.append(column_tile(m, rng(c)))
            tiles.append(column_tile(m, rng(width + c)))

    def deep(m):
        for c in range(0, D, MB):
            for k in range(0, FF, KC * P):
                tiles.append(column_tile(m, rng(c), k))

    halves(w["conv_w_pw1"][0], D)
    for name in ("mem_w_k", "mem_w_v"):
        for layer in range(2):
            plain(w[name][layer])
    plain(w["conv_w_pw2"][0])
    for layer in range(2):
        plain(w["mem_w_q"][layer])
        plain(w["mem_w_o"][layer])
        for c in range(0, FF, MB):
            tiles.append(column_tile(w["ffn_w_gate"][layer], rng(c)))
            tiles.append(column_tile(w["ffn_w_up"][layer], rng(c)))
        deep(w["ffn_w_down"][layer])
        if layer == 0:
            plain(w["w_k_shared"])
            plain(w["w_v_shared"])
            plain(w["diff_w_q"][0])
            plain(w["diff_w_o"][0])
    win = w["w_in_2"][0]
    at = np.cumsum([0, 512, 128, 128, 128, 128, 128, 128, 24, 512, 128, 128])
    q_n, k_c, v_c, k_s, v_s, k_w, v_w, g_n, q_w, k_sw, v_sw = (int(a) for a in at[:-1])
    pairs = [hd for c in range(4) for hd in (c, 4 + c)]
    for q in (q_n, q_w):
        order = [q + 64 * hd + d for hd in pairs for d in range(64)]
        tiles.append(column_tile(win, order[0:MB]))
        tiles.append(column_tile(win, order[MB:]))
    for c in (k_c, v_c):
        tiles.append(column_tile(win, rng(c, 64) * 2 + rng(c + 64, 64) * 2))
    tiles.append(column_tile(win, rng(k_s, P) + rng(k_w, P)))
    tiles.append(column_tile(win, rng(k_sw, P)))
    tiles.append(column_tile(win, rng(v_s, P) + rng(v_w, P)))
    tiles.append(column_tile(win, rng(v_sw, P) + [g_n + 3 * hd + b for b in range(3) for hd in pairs]))
    for kv in range(2):
        for k in range(0, CMP_LEN * HD2, KC * P):
            tiles.append(column_tile(w["cmp_w1_2"][0, kv], rng(0), k))
    rows = [64 * hd + d for hd in pairs for d in range(64)]
    plain(w["w_out_2"][0][rows + [512 + r for r in rows]])
    halves(w["w_up_2"][0], FF)
    deep(w["w_down_2"][0])
    assert len(tiles) == TILES
    return np.stack(tiles), rows


def packed_constants(w, rows):
    def vec(v):
        return v.reshape(-1, P).T

    def every(v):
        return np.broadcast_to(v.reshape(1, -1), (P, v.size))

    def in_turn(v, width):
        m = v.reshape(v.shape[:-1] + (2, width // MB, MB))
        return np.moveaxis(m, -3, -2).reshape(v.shape)

    pairs = [hd for c in range(4) for hd in (c, 4 + c)]
    parts = {
        "g_mix0": vec(w["norm_mix"][0]), "g_mem0": vec(w["norm_mem"][0]), "g_ffn0": vec(w["norm_ffn"][0]),
        "g_kv": vec(w["kv_norm"]), "g_mix1": vec(w["norm_mix"][1]), "g_mem1": vec(w["norm_mem"][1]),
        "g_ffn1": vec(w["norm_ffn"][1]), "g_final": vec(w["norm_final"]),
        "b_pw1": vec(in_turn(w["conv_b_pw1"][0], D)),
        "w_dw": w["conv_w_dw"][0].reshape(CONV, DC, P).transpose(2, 1, 0).reshape(P, DC * CONV),
        "b_dw": vec(w["conv_b_dw"][0]), "ln_g": vec(w["conv_ln_g"][0]), "ln_b": vec(w["conv_ln_b"][0]),
        "b_pw2": vec(w["conv_b_pw2"][0]), "g_sub": vec(w["diff_subln_g"][0]),
        "lam": np.concatenate([every(w[f"diff_lambda_{n}"][0]) for n in ("q1", "k1", "q2", "k2")], 1),
        "g_pre2": vec(w["attn_pre_norm_2"][0]), "g_post2": vec(w["attn_post_norm_2"][0]),
        "g_out2": np.concatenate([vec(w["nsa_out_norm_2"][0][rows]), vec(w["swa_out_norm_2"][0][rows])], 1),
        "pe": w["cmp_pos_2"][0].reshape(2, 16, 2, HD2).transpose(2, 3, 0, 1).reshape(P, 32),
        "cmp_w2": w["cmp_w2_2"][0].reshape(2, 2, P, HD2).transpose(2, 0, 1, 3).reshape(P, 256),
        "sinks": every(w["swa_sinks_2"][0][pairs]),
        "g_fpre2": vec(w["ffn_pre_norm_2"][0]), "g_fpost2": vec(w["ffn_post_norm_2"][0]),
        "cw2": in_turn(w["conv_w_2"][0], FF).reshape(3, 2 * FC, P).transpose(2, 1, 0).reshape(P, 6 * FC),
        "cb2": vec(in_turn(w["conv_b_2"][0], FF)),
    }
    p, t = np.arange(P), np.arange(S)
    f32 = np.float32
    inv1 = (np.float32(500000.0) ** (-np.arange(0, ROT1, 2, dtype=f32) / f32(ROT1))).astype(f32)
    parts["invf"] = np.where(p % 64 < ROT1, inv1[p % 8], 0).astype(f32)[:, None]
    parts["ident"] = np.eye(P, dtype=f32)
    perm1, perm2 = np.zeros((P, P), f32), np.zeros((P, P), f32)
    for c in range(0, P, 64):
        for k in range(8):
            perm1[c + 8 + k, c + k], perm1[c + k, c + 8 + k] = -1, 1
        for k in range(32):
            perm2[c + 32 + k, c + k], perm2[c + k, c + 32 + k] = -1, 1
    parts["perm1"], parts["perm2"] = perm1, perm2
    parts["causal"] = np.where(p[None, :] <= p[:, None], 0, NEG).astype(f32)
    parts["band"] = np.where(p[None, :] > p[:, None], 0, NEG).astype(f32)
    cm = np.zeros((P, 2, 16), f32)
    ends = np.arange(NCMP) * CMP_STRIDE + CMP_LEN - 1
    for tt in range(NT):
        cm[:, tt, :NCMP] = np.where(ends[None, :] <= (tt * P + p)[:, None], 0, NEG)
    parts["cmask"] = cm.reshape(P, 32)
    parts["rowok"] = np.stack([(tt * P + p >= CMP_LEN - 1) for tt in range(NT)], 1).astype(f32)
    inv2 = (np.float32(10000.0) ** (-np.arange(32, dtype=f32) / f32(32))).astype(f32)
    ang = t.astype(f32)[None, :] * inv2[p % 32][:, None]
    parts["cos2"], parts["sin2"] = np.cos(ang).astype(f32), np.sin(ang).astype(f32)
    for name, n in CONSTS:
        assert parts[name].shape == (P, n), (name, parts[name].shape)
    return np.concatenate([parts[name] for name, _ in CONSTS], 1)


def kernel(**inputs):
    import concourse.bacc as bacc
    from concourse.bass_utils import run_bass_kernel_spmd

    w = {k: np.asarray(v) for k, v in inputs.items()}
    tiles, rows = weight_tiles(w)
    arrays = {
        "weights": tiles, "consts": np.ascontiguousarray(packed_constants(w, rows)),
        "x_in": np.ascontiguousarray(w["x"][0].T), "mem_in": np.ascontiguousarray(w["mem"][0].T),
        "positions": w["positions"],
    }
    nc = bacc.Bacc("TRN2", target_bir_lowering=False, num_devices=1)
    args = [nc.dram_tensor(n, a.shape, mybir.dt.from_np(a.dtype), kind="ExternalInput").ap() for n, a in arrays.items()]
    args.append(nc.dram_tensor("out", (D, S), F32, kind="ExternalOutput").ap())
    build(nc, *args)
    r = run_bass_kernel_spmd(nc, [arrays], core_ids=[0])
    return np.ascontiguousarray(r.results[0]["out"].T)[None]
```

```python
import concourse.bass as bass
from concourse import mybir
from contextlib import ExitStack, contextmanager
import math
import numpy as np

F32 = mybir.dt.float32
F32R = mybir.dt.float32r
BF16 = mybir.dt.bfloat16
I32 = mybir.dt.int32
U32 = mybir.dt.uint32
ALU = mybir.AluOpType
ACT = mybir.ActivationFunctionType
AX_X = mybir.AxisListType.X

P = 128
D = 1024
S = 256
NT = S // P
DC = D // P
FF = 2816
FC = FF // P
KC = 8
MB = 256
CONV = 31
DIFF_HEADS = 8
DIFF_SCALE = 64 ** -0.5
MEM_HEADS = 4
MEM_SCALE = 256 ** -0.5
LAMBDA_INIT = 0.8 - 0.6 * math.exp(-0.3)
ROT1 = 16
CMP_LEN, CMP_STRIDE = 32, 16
NCMP = S // CMP_STRIDE - 1
HD2 = 64
NSA_SCALE = HD2 ** -0.5
NEG = -1e30
MAGIC = 1.5 * 2 ** 23
TWO_PI = (6.28125, 0.0019350051879882812, 3.0199159819573245e-07)
PI_IN = 3.1415925
RMS_EPS, LN_EPS, SUBLN_EPS = 1e-6, 1e-5, 1e-5
LO_POOL = 3

PLAN = [
    ("pw1", 8, 8), ("memk", 8, 8), ("memv", 8, 8), ("pw2", 4, 4),
    ("memq0", 4, 4), ("attn_mem0", 0, 4), ("memo0", 4, 4), ("gu0", 22, 22), ("down0", 12, 4),
    ("diffk", 4, 4), ("diffv", 4, 4), ("diffq", 4, 4), ("attn_diff", 0, 8), ("diffo", 4, 4),
    ("memq1", 4, 4), ("attn_mem1", 0, 4), ("memo1", 4, 4), ("gu1", 22, 22), ("down1", 12, 4),
    ("win", 8, 8), ("winv", 2, 2), ("cmp", 4, 2), ("attn_nsa", 0, 8), ("wout", 4, 4),
    ("up2", 22, 22), ("down2", 12, 4),
]
T0, G0 = {}, {}
_t = _g = 0
for _name, _nt, _ng in PLAN:
    T0[_name], G0[_name] = _t, _g
    _t, _g = _t + _nt, _g + _ng
TILES = _t
NTILES = {n: t for n, t, _ in PLAN}

CONSTS = [
    ("g_mix0", 8), ("g_mem0", 8), ("g_ffn0", 8), ("g_kv", 8), ("g_mix1", 8), ("g_mem1", 8), ("g_ffn1", 8),
    ("g_final", 8), ("b_pw1", 16), ("w_dw", DC * CONV), ("b_dw", 8), ("ln_g", 8), ("ln_b", 8), ("b_pw2", 8),
    ("g_sub", 1), ("lam", 256), ("g_pre2", 8), ("g_post2", 8), ("g_out2", 8), ("pe", 32), ("cmp_w2", 256),
    ("sinks", 8), ("g_fpre2", 8), ("g_fpost2", 8), ("cw2", 132), ("cb2", 44),
    ("invf", 1), ("ident", P), ("perm1", P), ("perm2", P), ("causal", P), ("band", P), ("cmask", 32),
    ("rowok", 2), ("cos2", S), ("sin2", S),
]
C0 = {}
_c = 0
for _name, _n in CONSTS:
    C0[_name] = (_c, _n)
    _c += _n
NCONST = _c


class Chain:

    def __init__(self, eng, sem):
        self.eng, self.sem, self.base, self.k, self.i, self.per = eng, sem, 0, 0, None, 0

    def link(self, ins):
        self.wait(self.mark(ins))
        return ins

    def mark(self, ins):
        ins.then_inc(self.sem, 1)
        self.k += 1
        return self.k

    def wait(self, k):
        at = self.base + k
        self.eng.wait_ge(self.sem, at if self.i is None else self.i * self.per + at)

    @contextmanager
    def loop(self, n, per, start=0):
        self.base += self.k
        self.k = 0
        if n - start == 1:
            yield start
            assert self.k == per, (self.k, per)
            self.base += per
        else:
            with self.eng.Fori(start, n) as i:
                self.i, self.per = i, per
                self.base -= start * per
                yield i
                assert self.k == per, (self.k, per)
                self.i = None
            self.base += n * per
        self.k = 0


@contextmanager
def loop(eng, n, start=0):
    if n - start == 1:
        yield start
    else:
        with eng.Fori(start, n) as i:
            yield i


class Steps:

    def __init__(self, sem, steps):
        self.sem, self.first, self.n = sem, {}, dict(steps)
        total = 0
        for name, n in steps:
            self.first[name] = total
            total += n

    def at(self, name, k=None):
        return self.first[name] + (self.n[name] if k is None else k)


def build(nc, weights, consts, x_in, mem_in, positions, out):
    ctx = ExitStack()
    with ctx:
        def sb(name, shape, dt=F32, where=ctx):
            return where.enter_context(nc.sbuf_tensor(name, shape, dt))

        def sem(name):
            return ctx.enter_context(nc.semaphore(name))

        raw = [sb(f"raw{j}", [P, KC, MB]) for j in range(2)]
        whi = [sb(f"whi{j}", [P, KC, MB], F32R) for j in range(2)]
        wlo = [sb(f"wlo{j}", [P, KC, MB], F32R) for j in range(2)]
        X = sb("X", [P, DC, S])
        SQ = sb("SQ", [P, DC, S])
        Hhi, Hlo = sb("Hhi", [P, DC, S], F32R), sb("Hlo", [P, DC, S], F32R)
        H2hi, H2lo = sb("H2hi", [P, DC, S], F32R), sb("H2lo", [P, DC, S], F32R)
        FH = sb("FH", [P, FC, S], F32R)
        MKV = sb("MKV", [P, 4 * DC, S])
        cst = sb("cst", [P, NCONST])
        R = sb("R", [P, S])
        TG, TU = sb("TG", [P, 2, S + 2]), sb("TU", [P, 2, S + 2])
        SG = sb("SG", [P, 2, S])
        E = sb("E", [P, 3, 2, S])
        PT = sb("PT", [P, 2, 2 * S])
        rope_c, rope_s = sb("rope_c", [P, S]), sb("rope_s", [P, S])
        ones = sb("ones", [P, 1])
        rt = sb("rt", [P, 15, 16])
        nw = sb("nw", [P, 4, 16])
        nwi = sb("nwi", [P, 16], I32)
        mx, nb, sm, rs = (sb(n, [P, 2, 2]) for n in ("mx", "nb", "smx", "rs"))
        sk, ske = sb("skm", [P, 2, 2]), sb("ske", [P, 2, 2])
        lam, gsub = sb("lamt", [P, 4]), sb("gsub", [P, 1])
        gates = sb("gates", [P, NT, 24])
        HCm = sb("HCm", [P, 2, 2, 32])
        KCm, VCm = sb("KCm", [P, 16]), sb("VCm", [16, P])
        ident_b, causal_b, band_b = (sb(n, [P, P], BF16) for n in ("ident_b", "causal_b", "band_b"))
        cmask_b = sb("cmask_b", [P, 32], BF16)
        with ExitStack() as shared:
            FL = sb("FL", [P, FC, S], F32R, shared)
        A = sb("A", [P, FC, S])
        Af = A[:, :, :].rearrange("p c s -> p (c s)")
        U = Af[:, 0:DC * (S + CONV - 1)].rearrange("p (c s) -> p c s", c=DC)
        UC = A[:, 10:18, :]
        FHf = FH[:, :, :].rearrange("p c s -> p (c s)")
        Ohi, Olo = FH[:, 0:8, :], FH[:, 8:16, :]
        V2 = Af[:, 16 * S:20 * S].rearrange("p (t n) -> p t n", t=NT)
        ZT = Af[:, 20 * S:20 * S + 480]
        M2 = MKV[:, 0:8, :]

        acc = [ctx.enter_context(nc.psum_tensor(f"acc{j}", [P, 2, S], F32)) for j in range(2)]
        sc = ctx.enter_context(nc.psum_tensor("sc", [P, 4, 2 * S], F32))
        tp = ctx.enter_context(nc.psum_tensor("tp", [P, 2 * S], F32))
        st = ctx.enter_context(nc.psum_tensor("st", [P, 2 * S], F32))

        raw_loaded = [sem(f"raw_loaded{j}") for j in range(2)]
        cst_loaded, x_loaded, mem_loaded, pos_loaded = (sem(n) for n in ("cst_loaded", "x_loaded", "mem_loaded", "pos_loaded"))
        hi_out, lo_dve, lo_pool = sem("hi_out"), sem("lo_dve"), sem("lo_pool")
        tile_done, acc_free = sem("tile_done"), sem("acc_free")
        s_given, s_taken, s_sq, s_h = sem("given"), sem("taken"), sem("sq_ready"), sem("h_ready")
        stat_ready, rt_ready, spread_ready, spread_used = (sem(n) for n in ("stat_ready", "rt_ready", "spread_ready", "spread_used"))
        s_done, nb_ready, exp_done, p_ready = sem("s_done"), sem("nb_ready"), sem("exp_done"), sem("p_ready")
        t_done, pt_ready, pv_done = sem("t_done"), sem("pt_ready"), sem("pv_done")
        rot_ready, rot_used = sem("rot_ready"), sem("rot_used")
        consts_ready, conv_done, hid_ready, cmp_mm, cmp_ready = (sem(n) for n in ("consts_ready", "conv_done", "hid_ready", "cmp_mm", "cmp_ready"))
        x_final, out_done, u_ready = sem("x_final"), sem("out_done"), sem("u_ready")
        dve_chain, act_chain = sem("dve_chain"), sem("act_chain")

        given = Steps(s_given, [("lam", 1), ("rope", 1), ("ln_sq", 1), ("ln", 4), ("gu0", 11), ("sub", 4), ("gu1", 11),
                                ("final", 4), ("z", 2), ("outn", 4), ("post", 4), ("up2", 22)])
        taken = Steps(s_taken, [("x0", 1), ("mem", 1), ("lam", 1), ("rope", 1), ("pw1", 4), ("ln", 4), ("pw2", 4),
                                ("attn_mem0", 4), ("memo0", 4), ("gu0", 22), ("down0", 4), ("sub", 4), ("diffo", 4),
                                ("attn_mem1", 4), ("memo1", 4), ("gu1", 22), ("final", 4), ("gates", 1), ("z", 2),
                                ("outn", 4), ("post", 4), ("up2", 22)])
        sq = Steps(s_sq, [("mix0", 1), ("ln", 1), ("pw2", 4), ("memo0", 4), ("down0", 4), ("attn_diff", 8), ("diffo", 4),
                          ("memo1", 4), ("down1", 4), ("final", 4), ("attn_nsa", 8), ("wout", 4), ("post", 4), ("down2", 4)])
        h = Steps(s_h, [("x0", 1), ("mem", 1), ("ln", 4), ("pw2", 4), ("attn_mem0", 4), ("memo0", 4), ("gu0", 11),
                        ("down0", 4), ("sub", 4), ("diffo", 4), ("attn_mem1", 4), ("memo1", 4), ("gu1", 11), ("final", 4),
                        ("z", 2), ("outn", 4), ("post", 4), ("up2", 11)])
        NORMS = ["mix0", "ln_mu", "ln_var", "mem0", "ffn0", "attn1", "sub", "mem1", "ffn1", "final", "pre2", "out2",
                 "post2", "fpre2", "fpost2"]
        N0 = {name: k for k, name in enumerate(NORMS)}
        SQ_OF = {"mix0": "mix0", "mem0": "pw2", "ffn0": "memo0", "attn1": "down0", "mem1": "diffo", "ffn1": "memo1",
                 "pre2": "final", "fpre2": "post"}
        ROPES = {"diff": [(s, 2) for s in range(0, 16, 2)],
                 "nsa": [(0, 2), (2, 2), (4, 2), (6, 2), (8, 2), (12, 2), (14, 1)]}
        ROPE0 = {"diff": 0, "nsa": 8}

        def C(name, a=0, n=None):
            c0, width = C0[name]
            return cst[:, c0 + a:c0 + a + (width - a if n is None else n)]

        def mem_units(layer):
            units = []
            for h in range(MEM_HEADS):
                kv = 2 * DC + 8 * layer + 2 * h
                u = dict(kind="mem", scale=MEM_SCALE, keys=S, group=h, last=True, S=[], T=[], PV=[])
                for m in range(2):
                    u["S"].append(([(A[:, 2 * h + c, m * P:(m + 1) * P], MKV[:, 8 * layer + 2 * h + c, :])
                                    for c in range(2)], []))
                for m in range(2):
                    for kt in range(NT):
                        u["T"].append((m, kt * P, P, kt * S + m * P))
                for e in range(2):
                    u["PV"] += [((slice(0, P), e * S, S), MKV[:, kv + kt, e * P:(e + 1) * P],
                                 (P, kt * S, S), kt == 0, kt == NT - 1) for kt in range(NT)]
                units.append(u)
            return units

        def diff_units():
            units = []
            for h in range(DIFF_HEADS):
                for qt in range(NT):
                    nk = (qt + 1) * P
                    u = dict(kind="diff", scale=DIFF_SCALE, keys=nk, group=h, last=qt == NT - 1, S=[], T=[], PV=[])
                    for m in range(2):
                        r = slice(64 * m, 64 * m + 64)
                        u["S"].append(([(A[r, h, qt * P:(qt + 1) * P], A[r, 8 + h, 0:nk])],
                                       [(causal_b, nk - P, P)]))
                    for kt in range(qt + 1):
                        u["T"].append((0, kt * P, P, kt * P))
                        u["PV"].append(((slice(0, P), qt * P, P),
                                        MKV[:, 2 * DC + 2 * (h // 2) + kt, (h % 2) * P:(h % 2 + 1) * P],
                                        (P, kt * P, P), kt == 0, kt == qt))
                    units.append(u)
            return units

        def nsa_units():
            units = []
            for c in range(8):
                swa = c >= 4
                for qt in range(NT):
                    branches = ["swa"] if swa else ["slc", "win", "cmp"]
                    for b, kind in enumerate(branches):
                        nk = NCMP if kind == "cmp" else (qt + 1) * P
                        u = dict(kind=kind, scale=NSA_SCALE, keys=nk, group=c, S=[], T=[], PV=[], qt=qt, c=c,
                                 last=qt == NT - 1 and b == len(branches) - 1)
                        for m in range(2):
                            r = slice(64 * m, 64 * m + 64)
                            k = {"slc": A[r, 12, 0:nk], "win": A[r, 13, 0:nk], "swa": A[r, 14, 0:nk],
                                 "cmp": KCm[r, 0:NCMP]}[kind]
                            masks = [(causal_b, nk - P, P)] if kind != "cmp" else [(cmask_b[:, 16 * qt:16 * qt + NCMP], 0, NCMP)]
                            if kind == "swa" and qt == 1:
                                masks.append((band_b, 0, P))
                            u["S"].append(([(A[r, c, qt * P:(qt + 1) * P], k)], masks))
                            first, end = b == 0, b == len(branches) - 1
                            kts = 1 if kind == "cmp" else qt + 1
                            for kt in range(kts):
                                n = NCMP if kind == "cmp" else P
                                u["T"].append((m, kt * P, n, m * S + kt * P))
                                v = (VCm[0:NCMP, 64 * m:64 * m + 64] if kind == "cmp" else
                                     V2[:, kt, {"slc": 0, "win": P, "swa": 2 * P}[kind] + 64 * m:][:, 0:64])
                                u["PV"].append(((r, qt * P, P), v, (n, m * S + kt * P, P),
                                                first and kt == 0, end and kt == kts - 1))
                        units.append(u)
            return units

        ATTN = {"attn_mem0": mem_units(0), "attn_diff": diff_units(), "attn_mem1": mem_units(1),
                "attn_nsa": nsa_units()}
        U0, n_units = {}, 0
        for name, _, _ in PLAN:
            if name in ATTN:
                U0[name] = n_units
                n_units += len(ATTN[name])

        def tiles_done(name):
            return T0[name] + NTILES[name]

        block = ctx.enter_context(nc.Block())

        @block.sync
        def _(sp):
            cols = lambda ap: ap.rearrange("(c p) t -> p c t", p=P)
            sp.dma_start(cst[:, :], consts).then_inc(cst_loaded, 16)
            sp.dma_start(X[:, :, :], cols(x_in)).then_inc(x_loaded, 16)
            for j in range(2):
                sp.dma_start(raw[j][:, :, :], weights[j].rearrange("p (k m) -> p k m", k=KC)).then_inc(raw_loaded[j], 16)
            sp.dma_start(UC, cols(mem_in)).then_inc(mem_loaded, 16)
            sp.dma_start(PT[:, 0, 0:S].bitcast(I32), positions.partition_broadcast(P)).then_inc(pos_loaded, 16)
            with sp.Fori(1, TILES // 2) as i:
                for j in range(2):
                    sp.wait_ge(lo_dve, 2 * i + (j - 1))
                    sp.wait_ge(lo_pool, 2 * i + (j - 1))
                    sp.dma_start(raw[j][:, :, :], weights[bass.ds(2 * i + j, 1)].rearrange("o p (k m) -> p (o k) m", k=KC))\
                        .then_inc(raw_loaded[j], 16)
            sp.wait_ge(x_final, 4)
            sp.dma_start(cols(out), X[:, :, :]).then_inc(out_done, 16)
            sp.wait_ge(out_done, 16)

        @block.gpsimd
        def _(pool):
            with pool.Fori(0, TILES // 2) as i:
                for j in range(2):
                    pool.wait_ge(hi_out, 4 * i + (2 * j + 1))
                    pool.tensor_tensor(out=wlo[j][:, 0:LO_POOL, :], in0=raw[j][:, 0:LO_POOL, :],
                                       in1=whi[j][:, 0:LO_POOL, :].bitcast(F32), op=ALU.subtract).then_inc(lo_pool, 1)

        @block.tensor
        def _(pe):
            ident = C("ident")

            def three(dst, w, wl, x, xl, first, last):
                pe.matmul(dst, w, x, start=first, stop=False)
                pe.matmul(dst, w, xl, start=False, stop=False)
                return pe.matmul(dst, wl, x, start=False, stop=last)

            def tile_in(t):
                pe.wait_ge(lo_dve, t + 1)
                pe.wait_ge(lo_pool, t + 1)

            def columns(j, xhi, xlo, m, ks=range(KC), turned=False, first=True, last=True):
                o = slice(m * P, (m + 1) * P)
                for k in ks:
                    w, wl, x, xl = whi[j][:, k, :], wlo[j][:, k, :], xhi[:, k, :], xlo[:, k, :]
                    a, z = first and k == ks[0], last and k == ks[-1]
                    if turned:
                        mm = three(acc[j][:, m, :], x[:, o], xl[:, o], w, wl, a, z)
                    else:
                        mm = three(acc[j][:, m, :], w[:, o], wl[:, o], x, xl, a, z)
                return mm

            def stage(name, xhi, xlo, turned=False, source=None, norm_name=None):
                start = 0
                if source is not None:
                    start = 1
                    tile_in(T0[name])
                    pe.wait_ge(acc_free, G0[name] + 1)
                    if h.n[source] == 4:
                        pe.wait_ge(s_h, h.at(source, 3))
                        for m in range(2):
                            columns(0, xhi, xlo, m, range(6), first=m == 0, last=False)
                        pe.wait_ge(s_h, h.at(source))
                        for m in range(2):
                            mm = columns(0, xhi, xlo, m, range(6, KC), first=False, last=m == 1)
                    else:
                        pe.wait_ge(s_h, h.at(source))
                        for m in range(2):
                            mm = columns(0, xhi, xlo, m)
                    mm.then_inc(tile_done, 1)
                    if norm_name:
                        pe.wait_ge(s_sq, sq.at(SQ_OF[norm_name]))
                        norm_stats(norm_name)
                    tile_in(T0[name] + 1)
                    pe.wait_ge(acc_free, G0[name] + 2)
                    columns(1, xhi, xlo, 0)
                    if norm_name:
                        spread(norm_name)
                    columns(1, xhi, xlo, 1).then_inc(tile_done, 1)
                with loop(pe, NTILES[name] // 2, start) as i:
                    for j in range(2):
                        tile_in(2 * i + (T0[name] + j))
                        pe.wait_ge(acc_free, 2 * i + (G0[name] + j + 1))
                        for m in range(2):
                            mm = columns(j, xhi, xlo, m, turned=turned)
                        mm.then_inc(tile_done, 1)

            def down(name, source):
                def group(i, g, follow=False):
                    pe.wait_ge(acc_free, 2 * i + (G0[name] + g + 1))
                    for part in range(3):
                        j = (3 * g + part) % 2
                        ks = range(8 * part, min(8 * part + 8, FC))
                        tile_in(6 * i + (T0[name] + 3 * g + part))
                        for some in (ks[:4], ks[4:]):
                            if follow:
                                pe.wait_ge(s_h, h.at(source, some[-1] // 2 + 1))
                            for m in range(2):
                                for k in some:
                                    o = slice(m * P, (m + 1) * P)
                                    mm = three(acc[g][:, m, :], whi[j][:, k - 8 * part, o], wlo[j][:, k - 8 * part, o],
                                               FH[:, k, :], FL[:, k, :], m == k == 0, m == 1 and k == FC - 1)
                        mm.then_inc(tile_done, 1)

                group(0, 0, follow=True)
                group(0, 1)
                for g in range(2):
                    group(1, g)

            def stats(name, jobs):
                if N0[name] > 0:
                    pe.wait_ge(spread_used, N0[name])
                for col, chunks, tt in jobs:
                    for n, ap in enumerate(chunks):
                        mm = pe.matmul(st[:, col:col + 1], ap[:, tt * P:(tt + 1) * P], ones[:, 0:1],
                                       start=n == 0, stop=n == len(chunks) - 1)
                mm.then_inc(stat_ready, 1)

            def spread(name, jobs=None):
                pe.wait_ge(rt_ready, N0[name] + 1)
                for col, dst in jobs or [(tt, st[:, tt * P:(tt + 1) * P]) for tt in range(NT)]:
                    mm = pe.matmul(dst, rt[:, N0[name], col:col + 1].broadcast_to((P, P)), ident, start=True, stop=True)
                mm.then_inc(spread_ready, 1)

            def norm_stats(name, src=SQ):
                stats(name, [(tt, [src[:, k, :] for k in range(DC)], tt) for tt in range(NT)])

            def norm(name, src=SQ):
                norm_stats(name, src)
                spread(name)

            def rotate(which, perm):
                for n, (slot, w) in enumerate(ROPES[which]):
                    r = ROPE0[which] + n
                    if n >= 4:
                        pe.wait_ge(rot_used, r - 3)
                    pe.matmul(sc[:, n % 4, 0:w * S], C(perm), A[:, slot:slot + w, :], start=True, stop=True)\
                        .then_inc(rot_ready, 1)

            def attention(name):
                units, u0 = ATTN[name], U0[name]
                for s in range(len(units) + 3):
                    if s < len(units):
                        u, n = units[s], u0 + s
                        if n >= 2:
                            pe.wait_ge(exp_done, n - 1)
                        for m, (products, masks) in enumerate(u["S"]):
                            dst = sc[:, 2 * (n % 2) + m, :]
                            for k, (q, key) in enumerate(products):
                                mm = pe.matmul(dst[:, 0:u["keys"]], q, key, start=k == 0,
                                               stop=k == len(products) - 1 and not masks)
                            for k, (mask, c0, w) in enumerate(masks):
                                mm = pe.matmul(dst[:, c0:c0 + w], ident_b[:, :], mask if w < P else mask[:, :],
                                               start=False, stop=k == len(masks) - 1)
                        mm.then_inc(s_done, 1)
                    if 2 <= s < len(units) + 2:
                        u, n = units[s - 2], u0 + s - 2
                        pe.wait_ge(p_ready, n + 1)
                        if n >= 1:
                            pe.wait_ge(pt_ready, n)
                        for m, c0, w, to in u["T"]:
                            mm = pe.transpose(tp[0:w, to:to + P], E[:, n % 3, m, c0:c0 + w], ident)
                        mm.then_inc(t_done, 1)
                    if s >= 3:
                        u, n = units[s - 3], u0 + s - 3
                        g = G0[name] + u["group"]
                        pe.wait_ge(pt_ready, n + 1)
                        pe.wait_ge(acc_free, g + 1)
                        for (rows, c0, w), v, (kn, p0, pw), first, last in u["PV"]:
                            dst = acc[g % 2][:, :, :].rearrange("p a b -> p (a b)")
                            mm = pe.matmul(dst[rows, c0:c0 + w], v, PT[0:kn, n % 2, p0:p0 + pw], start=first, stop=last)
                        mm.then_inc(pv_done, 1)

            def wait_h(name):
                pe.wait_ge(s_h, h.at(name))

            pe.wait_ge(consts_ready, 1)
            stage("pw1", Hhi, Hlo, source="x0", norm_name="mix0")
            wait_h("mem")
            stage("memk", H2hi, H2lo)
            stage("memv", H2hi, H2lo, turned=True)
            pe.wait_ge(conv_done, 8)
            norm("ln_mu", UC)
            pe.wait_ge(s_sq, sq.at("ln"))
            norm("ln_var")
            stage("pw2", Ohi, Olo, source="ln")
            for layer, before in ((0, "pw2"), (1, "diffo")):
                stage(f"memq{layer}", Hhi, Hlo, source=before, norm_name=f"mem{layer}")
                pe.wait_ge(acc_free, G0[f"attn_mem{layer}"] + 2)
                attention(f"attn_mem{layer}")
                stage(f"memo{layer}", Ohi, Olo, source=f"attn_mem{layer}")
                stage(f"gu{layer}", Hhi, Hlo, source=f"memo{layer}", norm_name=f"ffn{layer}")
                down(f"down{layer}", f"gu{layer}")
                if layer == 1:
                    break
                stage("diffk", Hhi, Hlo, source="down0", norm_name="attn1")
                stage("diffv", Hhi, Hlo, turned=True)
                stage("diffq", H2hi, H2lo)
                pe.wait_ge(acc_free, G0["attn_diff"] + 2)
                rotate("diff", "perm1")
                pe.wait_ge(rot_used, ROPE0["nsa"])
                attention("attn_diff")
                pe.wait_ge(s_sq, sq.at("attn_diff"))
                stats("sub", [(2 * hd + tt, [SQ[:, hd, :]], tt) for hd in range(DIFF_HEADS) for tt in range(NT)])
                spread("sub", [(2 * hd + tt, sc[:, hd // 2, (hd % 2) * S + tt * P:][:, 0:P])
                               for hd in range(DIFF_HEADS) for tt in range(NT)])
                stage("diffo", Ohi, Olo, source="sub")
            pe.wait_ge(s_sq, sq.at("down1"))
            norm("final")
            stage("win", Hhi, Hlo, source="final", norm_name="pre2")
            stage("winv", Hhi, Hlo, turned=True)
            pe.wait_ge(acc_free, G0["cmp"] + 2)
            rotate("nsa", "perm2")
            for kv in range(2):
                pe.wait_ge(s_h, h.at("z", kv + 1))
                pe.wait_ge(acc_free, G0["cmp"] + kv + 1)
                for part in range(2):
                    tile_in(T0["cmp"] + 2 * kv + part)
                    for m in range(2):
                        for k in range(KC):
                            o = slice(m * P, (m + 1) * P)
                            z = [FHf[:, (2 * kv + l) * 480 + (8 * part + k) * 30:][:, 0:30] for l in range(2)]
                            mm = three(acc[kv][:, m, 0:30], whi[part][:, k, o], wlo[part][:, k, o], z[0], z[1],
                                       part == m == k == 0, part == m == 1 and k == KC - 1)
                    mm.then_inc(tile_done, 1)
            pe.wait_ge(hid_ready, 2)
            pe.wait_ge(spread_used, N0["pre2"] + 1)
            for hd in range(2):
                for m in range(2):
                    pe.matmul(st[64 * hd:64 * hd + 64, 0:NCMP], C("cmp_w2", 64 * m, 64),
                              HCm[:, 0, m, hd * NCMP:(hd + 1) * NCMP], start=m == 0, stop=m == 1)
            for hd in range(2):
                for m in range(2):
                    mm = pe.matmul(tp[0:NCMP, 64 * hd:64 * hd + 64], HCm[:, 1, m, hd * NCMP:(hd + 1) * NCMP],
                                   C("cmp_w2", 128 + 64 * m, 64), start=m == 0, stop=m == 1)
            mm.then_inc(cmp_mm, 1)
            pe.wait_ge(cmp_ready, 1)
            pe.wait_ge(rot_used, ROPE0["nsa"] + len(ROPES["nsa"]))
            attention("attn_nsa")
            pe.wait_ge(s_sq, sq.at("attn_nsa"))
            stats("out2", [(2 * b + tt, [SQ[:, 4 * b + k, :] for k in range(4)], tt) for b in range(2) for tt in range(NT)])
            spread("out2", [(2 * b + tt, sc[:, 0, b * S + tt * P:][:, 0:P]) for b in range(2) for tt in range(NT)])
            stage("wout", Ohi, Olo, source="outn")
            pe.wait_ge(s_sq, sq.at("wout"))
            norm("post2")
            stage("up2", Hhi, Hlo, source="post", norm_name="fpre2")
            down("down2", "up2")
            pe.wait_ge(s_sq, sq.at("down2"))
            norm("fpost2")

        @block.scalar
        def _(act):
            ac = Chain(act, act_chain)

            def split(load, j, done=None):
                act.wait_ge(raw_loaded[j], load)
                if done is not None:
                    act.wait_ge(tile_done, done)
                act.activation(whi[j][:, 0:LO_POOL, :], raw[j][:, 0:LO_POOL, :], ACT.Copy).then_inc(hi_out, 1)
                act.activation(whi[j][:, LO_POOL:KC, :], raw[j][:, LO_POOL:KC, :], ACT.Copy).then_inc(hi_out, 1)

            def ahead(name, i, per, k, last=False):
                if not last:
                    t = T0[name] + k
                    split(16 * (per // 2) * i + 16 * (t // 2 + 2), k % 2, per * i + (t + 1))

            def acc_out(name, g):
                act.wait_ge(acc_free, g + (G0[name] + 3))

            def hi_scaled(dst, src, gain, g0):
                for c in range(2):
                    ins = act.activation(dst[:, c, :], src[:, c, :], ACT.Copy, scale=gain(g0 + c))
                return ins

            def gcol(name):
                return lambda c: cst[:, bass.ds(c + C0[name][0], 1)] if not isinstance(c, int) else C(name, c, 1)

            def pair(t, c):
                return t[:, bass.ds(c, 2), :] if not isinstance(c, int) else t[:, c:c + 2, :]

            def residual(name, per, outs, last_stage=False):
                n = 2
                for start, stop in ([(0, 2)] if not last_stage else [(0, 1), (1, 2)]):
                    with loop(act, stop, start) as i:
                        for g in range(2):
                            def weights(ks):
                                for kk in ks:
                                    ahead(name, i, per, kk, last=last_stage and start == 1 and kk >= per - 2)

                            ks = range(g * per // 2, (g + 1) * per // 2)
                            weights(ks[:-1] if g else ks)
                            c = 4 * i + 2 * g
                            acc_out(name, 2 * i + g)
                            src = X if name not in ("wout", "down2") else M2
                            for b, gain in outs:
                                ins = hi_scaled(pair(b, c), pair(src, c), gcol(gain), c)
                            if outs:
                                ins.then_inc(s_taken, 1)
                            if g:
                                weights(ks[-1:])
                            act.activation(pair(SQ, c), pair(src, c), ACT.Square).then_inc(s_sq, 1)

            def plain(name):
                with loop(act, NTILES[name] // 2) as i:
                    for j in range(2):
                        ahead(name, i, 2, j)

            def copied(name, slots):
                with loop(act, NTILES[name] // 2) as i:
                    for j in range(2):
                        ahead(name, i, 2, j)
                        act.activation(pair(MKV, 4 * i + (slots + 2 * j)), acc[j][:, :, :], ACT.Copy).then_inc(acc_free, 1)

            def ffn(name, func):
                conv = name == "up2"
                src = E[:, 1, :, :] if conv else TU[:, :, 2:2 + S]

                def hidden(i):
                    act.wait_ge(s_given, 2 * i + given.at(name, 2) if conv else i + given.at(name, 1))
                    act.activation(pair(FH, 2 * i), src, ACT.Copy).then_inc(s_taken, 1)

                for start, stop in ((0, 1), (1, 11)):
                    with loop(act, stop, start) as i:
                        ahead(name, i, 2, 0)
                        if start:
                            hidden(i + (-1))
                        if conv:
                            act.wait_ge(s_given, 2 * i + given.at(name, 1))
                            for c in range(2):
                                ins = act.activation(SG[:, c, :], E[:, 0, c, :], func, bias=gcol("cb2")(4 * i + c))
                            ins.then_inc(s_taken, 1)
                        else:
                            acc_out(name, 2 * i)
                            act.activation(SG[:, :, :], TG[:, :, 2:2 + S], func).then_inc(s_taken, 1)
                        ahead(name, i, 2, 1)
                hidden(10)

            def attention(name):
                units, u0 = ATTN[name], U0[name]
                for s in range(len(units) + 5):
                    if s < len(units):
                        u, n = units[s], u0 + s
                        act.wait_ge(nb_ready, n + 1)
                        if n >= 3:
                            act.wait_ge(t_done, n - 2)
                        for m in range(2):
                            ins = act.activation(E[:, n % 3, m, 0:u["keys"]], sc[:, 2 * (n % 2) + m, 0:u["keys"]], ACT.Exp,
                                                 bias=nb[:, n % 2, m:m + 1], scale=u["scale"],
                                                 accum_out=rs[:, n % 2, m:m + 1])
                        if u["kind"] == "swa":
                            ins = act.activation(ske[:, n % 2, :], sk[:, n % 2, :], ACT.Exp)
                        ins.then_inc(exp_done, 1)
                    if 2 <= s < len(units) + 2:
                        u, n = units[s - 2], u0 + s - 2
                        act.wait_ge(t_done, n + 1)
                        if n >= 2:
                            act.wait_ge(pv_done, n - 1)
                        rows = u["T"][0][2]
                        if u["kind"] == "cmp":
                            a, b = (t.rearrange("p (m k) -> p m k", m=2)[0:rows, :, 0:P] for t in (PT[:, n % 2, :], tp[:, :]))
                        elif u["kind"] in ("mem", "diff") or u["keys"] == S:
                            w = max(to for *_, to in u["T"]) + P
                            a, b = PT[:, n % 2, 0:w], tp[:, 0:w]
                        else:
                            a, b = (t.rearrange("p (m k) -> p m k", m=2)[:, :, 0:P] for t in (PT[:, n % 2, :], tp[:, :]))
                        act.activation(a, b, ACT.Copy).then_inc(pt_ready, 1)
                    if s >= 5 and units[s - 5]["last"]:
                        g = units[s - 5]["group"]
                        acc_out(name, g)
                        if "mem" in name:
                            act.activation(Ohi[:, 2 * g:2 * g + 2, :], A[:, 2 * g:2 * g + 2, :], ACT.Copy).then_inc(s_taken, 1)
                        else:
                            act.activation(SQ[:, g, :], A[:, g, :], ACT.Square).then_inc(s_sq, 1)

            act.wait_ge(cst_loaded, 16)
            act.wait_ge(x_loaded, 16)
            act.activation(SQ[:, :, :], X[:, :, :], ACT.Square).then_inc(s_sq, 1)
            for c in range(DC):
                ins = act.activation(Hhi[:, c, :], X[:, c, :], ACT.Copy, scale=C("g_mix0", c, 1))
            ins.then_inc(s_taken, 1)
            for j in range(2):
                split(16, j)
            act.wait_ge(mem_loaded, 16)
            act.activation(H2hi[:, :, :], UC, ACT.Copy).then_inc(s_taken, 1)
            act.wait_ge(s_given, given.at("lam"))
            act.activation(lam[:, 2:4], lam[:, 0:2], ACT.Exp).then_inc(s_taken, 1)
            act.wait_ge(s_given, given.at("rope"))
            act.activation(rope_s[:, :], TG[:, 0, 0:S], ACT.Sin)
            act.activation(rope_c[:, :], TG[:, 1, 0:S], ACT.Sin).then_inc(s_taken, 1)
            with loop(act, 4) as i:
                ahead("pw1", i, 2, 0)
                ahead("pw1", i, 2, 1)
                acc_out("pw1", 2 * i + 1)
                for c in range(2):
                    ins = act.activation(SG[:, c, :], TU[:, c, 2:2 + S], ACT.Sigmoid, bias=gcol("b_pw1")(4 * i + (2 + c)))
                ins.then_inc(s_taken, 1)
            act.wait_ge(acc_free, G0["memk"] + 2)
            copied("memk", 0)
            copied("memv", 2 * DC)
            act.wait_ge(s_given, given.at("ln_sq"))
            act.activation(SQ[:, :, :], UC, ACT.Square).then_inc(s_sq, 1)
            for p in range(4):
                act.wait_ge(s_given, given.at("ln", p + 1))
                for c in range(2 * p, 2 * p + 2):
                    ac.link(act.activation(SQ[:, c, :], UC[:, c, :], ACT.Silu, scale=C("ln_g", c, 1), bias=C("ln_b", c, 1)))
                act.activation(Ohi[:, 2 * p:2 * p + 2, :], SQ[:, 2 * p:2 * p + 2, :], ACT.Copy).then_inc(s_taken, 1)
            residual("pw2", 2, [(Hhi, "g_mem0")])
            for layer in range(2):
                plain(f"memq{layer}")
                attention(f"attn_mem{layer}")
                residual(f"memo{layer}", 2, [(Hhi, f"g_ffn{layer}")])
                ffn(f"gu{layer}", ACT.Silu)
                if layer == 1:
                    break
                residual("down0", 6, [(Hhi, "g_kv"), (H2hi, "g_mix1")])
                plain("diffk")
                plain("diffv")
                plain("diffq")
                attention("attn_diff")
                for p in range(4):
                    act.wait_ge(s_given, given.at("sub", p + 1))
                    act.activation(Ohi[:, 2 * p:2 * p + 2, :], A[:, 2 * p:2 * p + 2, :], ACT.Copy,
                                   scale=gsub[:, 0:1]).then_inc(s_taken, 1)
                residual("diffo", 2, [(Hhi, "g_mem1")])
            residual("down1", 6, [])

            def ready_chunks(name, src, dst, gain, squares=True):
                for p in range(4):
                    act.wait_ge(s_given, given.at(name, p + 1))
                    hi_scaled(pair(dst, 2 * p), pair(src, 2 * p), gcol(gain), 2 * p).then_inc(s_taken, 1)
                    if squares:
                        act.activation(pair(SQ, 2 * p), pair(src, 2 * p), ACT.Square).then_inc(s_sq, 1)

            ready_chunks("final", X, Hhi, "g_pre2")
            plain("win")
            plain("winv")
            acc_out("winv", 1)
            act.activation(gates[:, :, :], V2[:, :, 3 * P:3 * P + 24], ACT.Sigmoid).then_inc(s_taken, 1)
            for kv in range(2):
                act.wait_ge(s_given, given.at("z", kv + 1))
                act.activation(FHf[:, 2 * kv * 480:(2 * kv + 1) * 480], ZT, ACT.Copy).then_inc(s_taken, 1)
            for kv in range(2):
                ahead("cmp", 0, 4, 2 * kv)
                ahead("cmp", 0, 4, 2 * kv + 1)
                acc_out("cmp", kv)
                act.activation(HCm[:, kv, :, 0:30], TG[:, :, 2 + 30 * kv:32 + 30 * kv], ACT.Gelu_apprx_tanh).then_inc(hid_ready, 1)
            attention("attn_nsa")
            ready_chunks("outn", A, Ohi, "g_out2", squares=False)
            residual("wout", 2, [])
            ready_chunks("post", X, Hhi, "g_fpre2")
            ffn("up2", ACT.Gelu_apprx_tanh)
            residual("down2", 6, [], last_stage=True)

        @block.vector
        def _(dve):
            ch = Chain(dve, dve_chain)
            link = ch.link
            f = lambda ap: ap.bitcast(F32)

            def lower(j, after):
                dve.wait_ge(hi_out, after)
                dve.tensor_tensor(out=wlo[j][:, LO_POOL:KC, :], in0=raw[j][:, LO_POOL:KC, :], in1=f(whi[j][:, LO_POOL:KC, :]),
                                  op=ALU.subtract).then_inc(lo_dve, 1)

            def ahead(name, i, per, k, last=False):
                if not last:
                    lower(k % 2, 2 * per * i + 2 * (T0[name] + k + 3))

            def tile(name, i, per, k):
                dve.wait_ge(tile_done, per * i + (T0[name] + k + 1))

            def col(name, c):
                return cst[:, bass.ds(c + C0[name][0], 1)] if not isinstance(c, int) else C(name, c, 1)

            def pair(t, c):
                return t[:, bass.ds(c, 2), :] if not isinstance(c, int) else t[:, c:c + 2, :]

            def both(ap):
                return ap.unsqueeze(1).broadcast_to((P, 2, S))

            def out_acc(ins):
                ins.then_inc(acc_free, 1)

            def lo_scaled(dst, src, hi, name, c):
                for k in range(2):
                    ins = dve.scalar_tensor_tensor(out=dst[:, k, :], in0=src[:, k, :], scalar=col(name, c + k),
                                                   in1=f(hi[:, k, :]), op0=ALU.mult, op1=ALU.subtract)
                return ins

            def rsqrt(name, n, div, eps):
                dve.wait_ge(stat_ready, N0[name] + 1)
                v, y, a, b = (nw[:, q, 0:n] for q in range(4))
                link(dve.tensor_scalar(v, st[:, 0:n], 1.0 / div, eps, op0=ALU.mult, op1=ALU.add))
                link(dve.tensor_scalar(nwi[:, 0:n], v.bitcast(I32), 1, None, op0=ALU.logical_shift_right))
                link(dve.tensor_scalar(y.bitcast(I32), nwi[:, 0:n], -1, 0x5F3759DF, op0=ALU.mult, op1=ALU.add))
                for step in range(3):
                    dst = y if step < 2 else rt[:, N0[name], 0:n]
                    link(dve.scalar_tensor_tensor(out=a, in0=y, scalar=-0.5, in1=v, op0=ALU.mult, op1=ALU.mult))
                    link(dve.tensor_tensor(out=b, in0=a, in1=y, op=ALU.mult))
                    ins = dve.scalar_tensor_tensor(out=dst, in0=b, scalar=1.5, in1=y, op0=ALU.add, op1=ALU.mult)
                    if step < 2:
                        link(ins)
                ins.then_inc(rt_ready, 1)

            def take_spread(name):
                dve.wait_ge(spread_ready, N0[name] + 1)
                dve.tensor_copy(R[:, :], st[:, 0:S]).then_inc(spread_used, 1)
                dve.wait_ge(spread_used, N0[name] + 1)

            def norm(name):
                rsqrt(name, NT, D, RMS_EPS)
                take_spread(name)

            def residual(name, per, outs, last_stage=False):
                for start, stop in ([(0, 2)] if not last_stage else [(0, 1), (1, 2)]):
                    with loop(dve, stop, start) as i:
                        for g in range(2):
                            def weights(ks):
                                for kk in ks:
                                    ahead(name, i, per, kk, last=last_stage and start == 1 and kk >= per - 2)

                            ks = range(g * per // 2, (g + 1) * per // 2)
                            weights(ks[:-1])
                            tile(name, i, per, ks[-1])
                            c = 4 * i + 2 * g
                            if name in ("wout", "down2"):
                                dve.tensor_copy(pair(M2, c), acc[g][:, :, :]).then_inc(acc_free, 1)
                            elif name == "pw2":
                                dve.scalar_tensor_tensor(out=pair(X, c)[:, 0, :], in0=acc[g][:, 0, :], scalar=col("b_pw2", c),
                                                         in1=pair(X, c)[:, 0, :], op0=ALU.add, op1=ALU.add)
                                dve.scalar_tensor_tensor(out=pair(X, c)[:, 1, :], in0=acc[g][:, 1, :], scalar=col("b_pw2", c + 1),
                                                         in1=pair(X, c)[:, 1, :], op0=ALU.add, op1=ALU.add).then_inc(acc_free, 1)
                            else:
                                dve.tensor_tensor(out=pair(X, c), in0=acc[g][:, :, :], in1=pair(X, c), op=ALU.add)\
                                    .then_inc(acc_free, 1)
                            if not g:
                                weights(ks[-1:])
                            if outs:
                                dve.wait_ge(acc_free, 2 * i + (G0[name] + g + 3))
                                dve.wait_ge(s_taken, 2 * i + taken.at(name, g + 1))
                            for hi, lo, gain in outs:
                                ins = lo_scaled(pair(lo, c), pair(X, c), pair(hi, c), gain, c)
                            if outs:
                                ins.then_inc(s_h, 1)
                            if g:
                                weights(ks[-1:])

            def first_turn(eng_loop, norm_name):
                return ((0, 1), (1, eng_loop)) if norm_name and eng_loop > 1 else ((0, eng_loop),)

            def evacuate(name, i, j, ins, norm_name, more=None):
                tile(name, i, 2, j)
                if norm_name and j == 0 and isinstance(i, int) and i == 0:
                    ahead(name, i, 2, j)
                    take_spread(norm_name)
                    out_acc(ins())
                    if more:
                        more()
                else:
                    out_acc(ins())
                    if more:
                        more()
                    ahead(name, i, 2, j)

            def times_r(dst, j):
                return lambda: dve.tensor_tensor(out=dst, in0=acc[j][:, :, :], in1=both(R[:, :]), op=ALU.mult)

            def project(name, dst, norm_name=None):
                for start, stop in first_turn(NTILES[name] // 2, norm_name):
                    with loop(dve, stop, start) as i:
                        for j in range(2):
                            evacuate(name, i, j, times_r(pair(dst, 4 * i + 2 * j), j), norm_name)

            def hidden_rest(name, i, src):
                dve.wait_ge(s_taken, 2 * i + taken.at(name, 2))
                dve.tensor_tensor(out=pair(FL, 2 * i), in0=src, in1=f(pair(FH, 2 * i)), op=ALU.subtract).then_inc(s_h, 1)

            def ffn(name, norm_name):
                up = TU[:, :, 2:2 + S]
                for start, stop in first_turn(11, norm_name):
                    with loop(dve, stop, start) as i:
                        evacuate(name, i, 0, times_r(TG[:, :, 2:2 + S], 0), norm_name)
                        if start:
                            dve.wait_ge(s_given, i + given.at(name, 0))
                            hidden_rest(name, i + (-1), up)
                            dve.wait_ge(s_h, i + h.at(name, 0))
                        evacuate(name, i, 1, times_r(up, 1), norm_name)
                        dve.wait_ge(acc_free, 2 * i + (G0[name] + 4))
                        dve.wait_ge(s_taken, 2 * i + taken.at(name, 1))
                        dve.tensor_tensor(out=up, in0=up, in1=SG[:, :, :], op=ALU.mult).then_inc(s_given, 1)
                dve.wait_ge(s_given, given.at(name, 11))
                hidden_rest(name, 10, up)

            def short_conv(dst, src, c):
                before = [None, None]
                for tap in range(3):
                    for k in range(2):
                        w = col("cw2", 3 * (c + k) + tap)
                        s_ = src[:, k, tap:tap + S]
                        if tap == 0:
                            ins = dve.tensor_scalar(dst[:, k, :], s_, w, None, op0=ALU.mult)
                        else:
                            ch.wait(before[k])
                            ins = dve.scalar_tensor_tensor(out=dst[:, k, :], in0=s_, scalar=w, in1=dst[:, k, :],
                                                           op0=ALU.mult, op1=ALU.add)
                        if tap < 2 or k == 0:
                            before[k] = ch.mark(ins)
                return ins

            def conv_ffn(name, norm_name):
                up = E[:, 1, :, :]
                for start, stop in first_turn(11, norm_name):
                    with ch.loop(stop, 5 + 6, start) as i:
                        def gate_conv():
                            dve.wait_ge(acc_free, 2 * i + (G0[name] + 3))
                            short_conv(E[:, 0, :, :], TG, 4 * i).then_inc(s_given, 1)

                        def up_conv():
                            dve.wait_ge(acc_free, 2 * i + (G0[name] + 4))
                            ch.link(short_conv(up, TU, 4 * i + 2))

                        evacuate(name, i, 0, times_r(TG[:, :, 2:2 + S], 0), norm_name, gate_conv)
                        if start:
                            dve.wait_ge(s_given, 2 * i + given.at(name, 0))
                            hidden_rest(name, i + (-1), up)
                            dve.wait_ge(s_h, i + h.at(name, 0))
                        evacuate(name, i, 1, times_r(TU[:, :, 2:2 + S], 1), norm_name, up_conv)
                        dve.wait_ge(s_taken, 2 * i + taken.at(name, 1))
                        for k in range(2):
                            ins = dve.scalar_tensor_tensor(out=up[:, k, :], in0=up[:, k, :], scalar=col("cb2", 4 * i + (2 + k)),
                                                           in1=SG[:, k, :], op0=ALU.add, op1=ALU.mult)
                        ins.then_inc(s_given, 1)
                dve.wait_ge(s_given, given.at(name))
                hidden_rest(name, 10, up)

            def rotate(which, cos, sin):
                for n, (slot, w) in enumerate(ROPES[which]):
                    r = ROPE0[which] + n
                    wide = lambda ap: ap.unsqueeze(1).broadcast_to((P, w, S))
                    q, t = A[:, slot:slot + w, :], E[:, n % 2, 0:w, :]
                    dve.wait_ge(rot_ready, r + 1)
                    link(dve.tensor_tensor(out=t, in0=sc[:, n % 4, 0:w * S].rearrange("p (a b) -> p a b", a=w), in1=wide(sin), op=ALU.mult))
                    link(dve.tensor_tensor(out=q, in0=q, in1=wide(cos), op=ALU.mult))
                    dve.tensor_tensor(out=q, in0=q, in1=t, op=ALU.add).then_inc(rot_used, 1)

            def attention(name):
                units, u0 = ATTN[name], U0[name]
                for s in range(len(units) + 6):
                    if s < len(units):
                        u, n = units[s], u0 + s
                        r = n % 2
                        dve.wait_ge(s_done, n + 1)
                        link(dve.reduce_max(mx[:, r, :], sc[:, 2 * r:2 * r + 2, 0:u["keys"]], axis=AX_X))
                        if u["kind"] == "swa":
                            sinks = C("sinks", 2 * (u["c"] - 4), 2)
                            link(dve.scalar_tensor_tensor(out=mx[:, r, :], in0=mx[:, r, :], scalar=u["scale"], in1=sinks,
                                                          op0=ALU.mult, op1=ALU.max))
                            link(dve.tensor_scalar(nb[:, r, :], mx[:, r, :], -1.0, None, op0=ALU.mult))
                            dve.tensor_tensor(out=sk[:, r, :], in0=nb[:, r, :], in1=sinks, op=ALU.add).then_inc(nb_ready, 1)
                        else:
                            dve.tensor_scalar(nb[:, r, :], mx[:, r, :], -u["scale"], None, op0=ALU.mult).then_inc(nb_ready, 1)
                    if 1 <= s <= len(units):
                        u, n = units[s - 1], u0 + s - 1
                        r, kind = n % 2, u["kind"]
                        dve.wait_ge(exp_done, n + 1)
                        rr = rs[:, r, :]
                        if kind == "swa":
                            link(dve.tensor_tensor(out=rr, in0=rr, in1=ske[:, r, :], op=ALU.add))
                        if kind == "cmp":
                            link(dve.tensor_scalar(rr, rr, 1e-30, None, op0=ALU.max))
                        link(dve.reciprocal(rr, rr))
                        if kind in ("slc", "win", "cmp"):
                            b = {"cmp": 0, "slc": 1, "win": 2}[kind]
                            gate = gates[:, u["qt"], 8 * b + 2 * u["c"]:][:, 0:2]
                            if kind == "cmp":
                                link(dve.scalar_tensor_tensor(out=rr, in0=rr, scalar=C("rowok", u["qt"], 1), in1=gate,
                                                              op0=ALU.mult, op1=ALU.mult))
                            else:
                                link(dve.tensor_tensor(out=rr, in0=rr, in1=gate, op=ALU.mult))
                        if kind == "diff":
                            link(dve.tensor_scalar(rr[:, 1:2], rr[:, 1:2], lam[:, 0:1], None, op0=ALU.mult))
                        e = [E[:, n % 3, m, 0:u["keys"]] for m in range(2)]
                        ins = dve.tensor_scalar(e[0], e[0], rr[:, 0:1], None, op0=ALU.mult)
                        if kind == "diff":
                            link(ins)
                            ins = dve.scalar_tensor_tensor(out=e[0], in0=e[1], scalar=rr[:, 1:2], in1=e[0],
                                                           op0=ALU.mult, op1=ALU.add)
                        else:
                            ins = dve.tensor_scalar(e[1], e[1], rr[:, 1:2], None, op0=ALU.mult)
                        ins.then_inc(p_ready, 1)
                    if 4 <= s < len(units) + 4 and units[s - 4]["last"]:
                        n, g = u0 + s - 4, units[s - 4]["group"]
                        a = acc[(G0[name] + g) % 2]
                        dve.wait_ge(pv_done, n + 1)
                        if "mem" in name:
                            out_acc(dve.tensor_copy(A[:, 2 * g:2 * g + 2, :], a[:, :, :]))
                        else:
                            out_acc(dve.tensor_copy(A[:, g, :], a[:, 0, :]))
                    if "mem" in name and s >= 6:
                        g = units[s - 6]["group"]
                        dve.wait_ge(s_taken, taken.at(name, g + 1))
                        dve.tensor_tensor(out=Olo[:, 2 * g:2 * g + 2, :], in0=A[:, 2 * g:2 * g + 2, :],
                                          in1=f(Ohi[:, 2 * g:2 * g + 2, :]), op=ALU.subtract).then_inc(s_h, 1)

            dve.memset(ones[:, :], 1.0)
            dve.memset(TG[:, :, :], 0.0)
            link(dve.memset(TU[:, :, :], 0.0))
            dve.memset(U[:, :, 0:CONV - 1], 0.0).then_inc(acc_free, 2)
            dve.wait_ge(cst_loaded, 16)
            dve.tensor_copy(ident_b[:, :], C("ident"))
            dve.tensor_copy(causal_b[:, :], C("causal"))
            dve.tensor_copy(band_b[:, :], C("band"))
            dve.tensor_copy(cmask_b[:, :], C("cmask")).then_inc(consts_ready, 1)
            dve.wait_ge(x_loaded, 16)
            dve.wait_ge(s_taken, taken.at("x0"))
            for c in range(0, DC, 2):
                ins = lo_scaled(Hlo[:, c:c + 2, :], X[:, c:c + 2, :], Hhi[:, c:c + 2, :], "g_mix0", c)
            ins.then_inc(s_h, 1)
            for j in range(2):
                lower(j, 2 * j + 2)
            dve.wait_ge(mem_loaded, 16)
            dve.wait_ge(s_taken, taken.at("mem"))
            dve.tensor_tensor(out=H2lo[:, :, :], in0=UC, in1=f(H2hi[:, :, :]), op=ALU.subtract).then_inc(s_h, 1)
            lv = C("lam").rearrange("p (a b c) -> p a b c", a=2, b=2)
            prod = TU[:, 1, 0:P].rearrange("p (a c) -> p a c", a=2)
            link(dve.tensor_tensor(out=prod, in0=lv[:, :, 0, :], in1=lv[:, :, 1, :], op=ALU.mult))
            dve.reduce_sum(lam[:, 0:2], prod, axis=AX_X).then_inc(s_given, 1)
            dve.wait_ge(s_taken, taken.at("lam"))
            link(dve.tensor_tensor(out=lam[:, 0:1], in0=lam[:, 3:4], in1=lam[:, 2:3], op=ALU.subtract))
            link(dve.tensor_scalar(lam[:, 0:1], lam[:, 0:1], -LAMBDA_INIT, None, op0=ALU.add))
            link(dve.tensor_scalar(gsub[:, :], C("g_sub"), 1.0 - LAMBDA_INIT, None, op0=ALU.mult))
            dve.wait_ge(pos_loaded, 16)
            ang, turn, r0, r1 = TU[:, 0, 0:S], TU[:, 1, 0:S], TG[:, 0, 0:S], TG[:, 1, 0:S]
            link(dve.tensor_copy(ang, PT[:, 0, 0:S].bitcast(I32)))
            link(dve.tensor_scalar(ang, ang, C("invf"), None, op0=ALU.mult))
            link(dve.tensor_scalar(turn, ang, 1.0 / (2 * math.pi), MAGIC, op0=ALU.mult, op1=ALU.add))
            link(dve.tensor_scalar(turn, turn, -MAGIC, None, op0=ALU.add))
            for k, part in enumerate(TWO_PI):
                link(dve.scalar_tensor_tensor(out=r0, in0=turn, scalar=-part, in1=ang if k == 0 else r0,
                                              op0=ALU.mult, op1=ALU.add))
            link(dve.tensor_scalar(r0, r0, -PI_IN, PI_IN, op0=ALU.max, op1=ALU.min))
            link(dve.scalar_tensor_tensor(out=r1, in0=r0, scalar=-1.0, in1=r0, op0=ALU.mult, op1=ALU.max))
            dve.tensor_scalar(r1, r1, -1.0, math.pi / 2, op0=ALU.mult, op1=ALU.add).then_inc(s_given, 1)
            dve.wait_ge(s_taken, taken.at("rope"))
            rsqrt("mix0", NT, D, RMS_EPS)
            for start, stop in first_turn(4, "mix0"):
                with loop(dve, stop, start) as i:
                    evacuate("pw1", i, 0, times_r(TG[:, :, 2:2 + S], 0), "mix0")
                    evacuate("pw1", i, 1, times_r(TU[:, :, 2:2 + S], 1), "mix0")
                    dve.wait_ge(acc_free, 2 * i + (G0["pw1"] + 4))
                    dve.wait_ge(s_taken, i + taken.at("pw1", 1))
                    for k in range(2):
                        dve.scalar_tensor_tensor(out=U[:, bass.ds(2 * i + k, 1), CONV - 1:CONV - 1 + S].rearrange("p o s -> p (o s)"),
                                                 in0=TG[:, k, 2:2 + S], scalar=col("b_pw1", 4 * i + k), in1=SG[:, k, :],
                                                 op0=ALU.add, op1=ALU.mult).then_inc(u_ready, 1)
                    dve.wait_ge(u_ready, 2 * i + 2)
            for base, name in ((0, "memk"), (4, "memv")):
                with ch.loop(4, CONV) as i:
                    dst = [UC[:, bass.ds(i + base, 1), :].rearrange("p o s -> p (o s)"), TU[:, 0, 2:2 + S]]
                    before = [None, None]
                    for tap in range(CONV):
                        if tap in (5, 20):
                            ahead(name, i, 2, tap // 20)
                        k = tap % 2
                        w = cst[:, bass.ds(CONV * i + (C0["w_dw"][0] + CONV * base + tap), 1)]
                        src = U[:, bass.ds(i + base, 1), tap:tap + S].rearrange("p o s -> p (o s)")
                        if tap == 0:
                            ins = dve.tensor_scalar(dst[k], src, w, col("b_dw", i + base), op0=ALU.mult, op1=ALU.add)
                        elif tap == 1:
                            ins = dve.tensor_scalar(dst[k], src, w, None, op0=ALU.mult)
                        else:
                            ch.wait(before[k])
                            ins = dve.scalar_tensor_tensor(out=dst[k], in0=src, scalar=w, in1=dst[k], op0=ALU.mult, op1=ALU.add)
                        before[k] = ch.mark(ins)
                    ch.wait(before[0])
                    dve.tensor_tensor(out=dst[0], in0=dst[0], in1=dst[1], op=ALU.add).then_inc(conv_done, 1)
                    dve.wait_ge(conv_done, i + (base + 1))
            dve.wait_ge(conv_done, 8)
            dve.wait_ge(stat_ready, N0["ln_mu"] + 1)
            dve.tensor_scalar(rt[:, N0["ln_mu"], 0:NT], st[:, 0:NT], 1.0 / D, None, op0=ALU.mult).then_inc(rt_ready, 1)
            take_spread("ln_mu")
            all8 = lambda ap: ap.unsqueeze(1).broadcast_to((P, DC, S))
            dve.tensor_tensor(out=UC, in0=UC, in1=all8(R[:, :]), op=ALU.subtract).then_inc(s_given, 1)
            rsqrt("ln_var", NT, D, LN_EPS)
            take_spread("ln_var")
            dve.wait_ge(s_given, given.at("ln_sq"))
            for p in range(4):
                dve.tensor_tensor(out=UC[:, 2 * p:2 * p + 2, :], in0=UC[:, 2 * p:2 * p + 2, :], in1=both(R[:, :]), op=ALU.mult)\
                    .then_inc(s_given, 1)
            for p in range(4):
                dve.wait_ge(s_taken, taken.at("ln", p + 1))
                dve.tensor_tensor(out=Olo[:, 2 * p:2 * p + 2, :], in0=SQ[:, 2 * p:2 * p + 2, :],
                                  in1=f(Ohi[:, 2 * p:2 * p + 2, :]), op=ALU.subtract).then_inc(s_h, 1)
            residual("pw2", 2, [(Hhi, Hlo, "g_mem0")])

            def values(name, dst, norm_name):
                with loop(dve, NTILES[name] // 2) as i:
                    for j in range(2):
                        tile(name, i, 2, j)
                        for tt in range(NT):
                            ins = dve.tensor_scalar(dst(i, j, tt), acc[j][:, tt, :], rt[:, N0[norm_name], tt:tt + 1], None, op0=ALU.mult)
                        out_acc(ins)
                        ahead(name, i, 2, j)

            def slot(t, c):
                return t[:, bass.ds(c, 1), :].rearrange("p o s -> p (o s)") if not isinstance(c, int) else t[:, c, :]

            for layer in range(2):
                rsqrt(f"mem{layer}", NT, D, RMS_EPS)
                project(f"memq{layer}", A, f"mem{layer}")
                dve.wait_ge(acc_free, G0[f"attn_mem{layer}"] + 2)
                attention(f"attn_mem{layer}")
                residual(f"memo{layer}", 2, [(Hhi, Hlo, f"g_ffn{layer}")])
                rsqrt(f"ffn{layer}", NT, D, RMS_EPS)
                ffn(f"gu{layer}", f"ffn{layer}")
                if layer == 1:
                    break
                residual("down0", 6, [(Hhi, Hlo, "g_kv"), (H2hi, H2lo, "g_mix1")])
                rsqrt("attn1", NT, D, RMS_EPS)
                project("diffk", A[:, 8:16, :], "attn1")
                values("diffv", lambda i, j, tt: slot(MKV, 4 * i + (2 * DC + 2 * j + tt)), "attn1")
                project("diffq", A[:, 0:8, :])
                dve.wait_ge(acc_free, G0["attn_diff"] + 2)
                rotate("diff", rope_c[:, :], rope_s[:, :])
                attention("attn_diff")
                rsqrt("sub", 16, P, SUBLN_EPS)
                dve.wait_ge(spread_ready, N0["sub"] + 1)
                dve.wait_ge(acc_free, G0["attn_diff"] + 8 + 2)
                for p in range(4):
                    q = A[:, 2 * p:2 * p + 2, :]
                    dve.tensor_tensor(out=q, in0=sc[:, p, :].rearrange("p (a b) -> p a b", a=2), in1=q, op=ALU.mult).then_inc(s_given, 1)
                for p in range(4):
                    dve.wait_ge(s_taken, taken.at("sub", p + 1))
                    q = slice(2 * p, 2 * p + 2)
                    dve.scalar_tensor_tensor(out=Olo[:, q, :], in0=A[:, q, :], scalar=gsub[:, 0:1], in1=f(Ohi[:, q, :]),
                                             op0=ALU.mult, op1=ALU.subtract).then_inc(s_h, 1)
                dve.sem_inc(spread_used, 1)
                residual("diffo", 2, [(Hhi, Hlo, "g_mem1")])
            residual("down1", 6, [])

            def lower_chunks(name, dst, src, hi, gain):
                for p in range(4):
                    dve.wait_ge(s_taken, taken.at(name, p + 1))
                    lo_scaled(pair(dst, 2 * p), pair(src, 2 * p), pair(hi, 2 * p), gain, 2 * p).then_inc(s_h, 1)

            norm("final")
            for c in range(DC):
                ins = dve.scalar_tensor_tensor(out=X[:, c, :], in0=X[:, c, :], scalar=C("g_final", c, 1), in1=R[:, :],
                                               op0=ALU.mult, op1=ALU.mult)
                if c % 2:
                    ins.then_inc(s_given, 1)
            lower_chunks("final", Hlo, X, Hhi, "g_pre2")
            rsqrt("pre2", NT, D, RMS_EPS)
            project("win", A, "pre2")
            values("winv", lambda i, j, tt: V2[:, tt, j * S:(j + 1) * S], "pre2")
            dve.wait_ge(acc_free, G0["cmp"] + 2)
            dve.wait_ge(s_taken, taken.at("gates"))
            rotate("nsa", C("cos2"), C("sin2"))
            dve.wait_ge(rot_used, ROPE0["nsa"] + len(ROPES["nsa"]))
            for kv in range(2):
                if kv:
                    dve.wait_ge(s_h, h.at("z", kv))
                z = ZT.rearrange("p (j h c) -> p j h c", j=16, h=2)
                for hd in range(2):
                    for half in range(2):
                        rows = slice(64 * half, 64 * half + 64)
                        for jh in range(2):
                            at = (8 + 2 * kv + hd) * S + half + 16 * jh
                            src = Af[rows, at:at + 16 * NCMP].rearrange("p (c j two) -> p j c two", j=8, two=2)[:, :, :, 0]
                            pe_ = C("pe", 16 * kv + 8 * jh, 8)[rows, :].unsqueeze(2).broadcast_to((64, 8, NCMP))
                            ins = dve.tensor_tensor(out=z[rows, 8 * jh:8 * jh + 8, hd, :], in0=src, in1=pe_, op=ALU.add)
                ins.then_inc(s_given, 1)
                dve.wait_ge(s_given, given.at("z", kv + 1))
                dve.wait_ge(s_taken, taken.at("z", kv + 1))
                dve.tensor_tensor(out=FHf[:, (2 * kv + 1) * 480:(2 * kv + 2) * 480], in0=ZT,
                                  in1=f(FHf[:, 2 * kv * 480:(2 * kv + 1) * 480]), op=ALU.subtract).then_inc(s_h, 1)
            for kv in range(2):
                ahead("cmp", 0, 4, 2 * kv)
                tile("cmp", 0, 4, 2 * kv + 1)
                out_acc(dve.tensor_copy(TG[:, :, 2 + 30 * kv:32 + 30 * kv], acc[kv][:, :, 0:30]))
                ahead("cmp", 0, 4, 2 * kv + 1)
            dve.wait_ge(cmp_mm, 1)
            dve.tensor_copy(KCm[:, 0:NCMP], st[:, 0:NCMP])
            dve.tensor_copy(VCm[0:NCMP, :], tp[0:NCMP, 0:P]).then_inc(cmp_ready, 1)
            dve.wait_ge(cmp_ready, 1)
            attention("attn_nsa")
            rsqrt("out2", 4, D // 2, RMS_EPS)
            dve.wait_ge(spread_ready, N0["out2"] + 1)
            dve.wait_ge(acc_free, G0["attn_nsa"] + 8 + 2)
            for p in range(4):
                b = p // 2
                dve.tensor_tensor(out=pair(A, 2 * p), in0=both(sc[:, 0, b * S:(b + 1) * S]), in1=pair(A, 2 * p), op=ALU.mult)\
                    .then_inc(s_given, 1)
            lower_chunks("outn", Olo, A, Ohi, "g_out2")
            dve.sem_inc(spread_used, 1)
            residual("wout", 2, [])
            norm("post2")

            def add_normed(gain, done):
                for c in range(DC):
                    link(dve.scalar_tensor_tensor(out=M2[:, c, :], in0=M2[:, c, :], scalar=C(gain, c, 1), in1=R[:, :],
                                                  op0=ALU.mult, op1=ALU.mult))
                    if c % 2:
                        dve.tensor_tensor(out=pair(X, c - 1), in0=pair(X, c - 1), in1=pair(M2, c - 1), op=ALU.add).then_inc(done, 1)

            add_normed("g_post2", s_given)
            lower_chunks("post", Hlo, X, Hhi, "g_fpre2")
            dve.memset(TG[:, :, 0:2], 0.0)
            link(dve.memset(TU[:, :, 0:2], 0.0))
            rsqrt("fpre2", NT, D, RMS_EPS)
            conv_ffn("up2", "fpre2")
            residual("down2", 6, [], last_stage=True)
            norm("fpost2")
            add_normed("g_fpost2", x_final)


def column_tile(w, cols, k0=0):
    part = w[k0:k0 + KC * P][:, cols]
    tile = np.zeros((KC * P, MB), w.dtype)
    tile[:part.shape[0], :part.shape[1]] = part
    return tile.reshape(KC, P, MB).transpose(1, 0, 2).reshape(P, KC * MB)


def weight_tiles(w):
    rng = lambda a, n=MB: list(range(a, a + n))
    tiles = []

    def plain(m):
        for c in range(0, m.shape[1], MB):
            tiles.append(column_tile(m, rng(c)))

    def halves(m, width):
        for c in range(0, width, MB):
            tiles.append(column_tile(m, rng(c)))
            tiles.append(column_tile(m, rng(width + c)))

    def deep(m):
        for c in range(0, D, MB):
            for k in range(0, FF, KC * P):
                tiles.append(column_tile(m, rng(c), k))

    halves(w["conv_w_pw1"][0], D)
    for name in ("mem_w_k", "mem_w_v"):
        for layer in range(2):
            plain(w[name][layer])
    plain(w["conv_w_pw2"][0])
    for layer in range(2):
        plain(w["mem_w_q"][layer])
        plain(w["mem_w_o"][layer])
        for c in range(0, FF, MB):
            tiles.append(column_tile(w["ffn_w_gate"][layer], rng(c)))
            tiles.append(column_tile(w["ffn_w_up"][layer], rng(c)))
        deep(w["ffn_w_down"][layer])
        if layer == 0:
            plain(w["w_k_shared"])
            plain(w["w_v_shared"])
            plain(w["diff_w_q"][0])
            plain(w["diff_w_o"][0])
    win = w["w_in_2"][0]
    at = np.cumsum([0, 512, 128, 128, 128, 128, 128, 128, 24, 512, 128, 128])
    q_n, k_c, v_c, k_s, v_s, k_w, v_w, g_n, q_w, k_sw, v_sw = (int(a) for a in at[:-1])
    pairs = [hd for c in range(4) for hd in (c, 4 + c)]
    for q in (q_n, q_w):
        order = [q + 64 * hd + d for hd in pairs for d in range(64)]
        tiles.append(column_tile(win, order[0:MB]))
        tiles.append(column_tile(win, order[MB:]))
    for c in (k_c, v_c):
        tiles.append(column_tile(win, rng(c, 64) * 2 + rng(c + 64, 64) * 2))
    tiles.append(column_tile(win, rng(k_s, P) + rng(k_w, P)))
    tiles.append(column_tile(win, rng(k_sw, P)))
    tiles.append(column_tile(win, rng(v_s, P) + rng(v_w, P)))
    tiles.append(column_tile(win, rng(v_sw, P) + [g_n + 3 * hd + b for b in range(3) for hd in pairs]))
    for kv in range(2):
        for k in range(0, CMP_LEN * HD2, KC * P):
            tiles.append(column_tile(w["cmp_w1_2"][0, kv], rng(0), k))
    rows = [64 * hd + d for hd in pairs for d in range(64)]
    plain(w["w_out_2"][0][rows + [512 + r for r in rows]])
    halves(w["w_up_2"][0], FF)
    deep(w["w_down_2"][0])
    assert len(tiles) == TILES
    return np.stack(tiles), rows


def packed_constants(w, rows):
    def vec(v):
        return v.reshape(-1, P).T

    def every(v):
        return np.broadcast_to(v.reshape(1, -1), (P, v.size))

    def in_turn(v, width):
        m = v.reshape(v.shape[:-1] + (2, width // MB, MB))
        return np.moveaxis(m, -3, -2).reshape(v.shape)

    pairs = [hd for c in range(4) for hd in (c, 4 + c)]
    parts = {
        "g_mix0": vec(w["norm_mix"][0]), "g_mem0": vec(w["norm_mem"][0]), "g_ffn0": vec(w["norm_ffn"][0]),
        "g_kv": vec(w["kv_norm"]), "g_mix1": vec(w["norm_mix"][1]), "g_mem1": vec(w["norm_mem"][1]),
        "g_ffn1": vec(w["norm_ffn"][1]), "g_final": vec(w["norm_final"]),
        "b_pw1": vec(in_turn(w["conv_b_pw1"][0], D)),
        "w_dw": w["conv_w_dw"][0].reshape(CONV, DC, P).transpose(2, 1, 0).reshape(P, DC * CONV),
        "b_dw": vec(w["conv_b_dw"][0]), "ln_g": vec(w["conv_ln_g"][0]), "ln_b": vec(w["conv_ln_b"][0]),
        "b_pw2": vec(w["conv_b_pw2"][0]), "g_sub": vec(w["diff_subln_g"][0]),
        "lam": np.concatenate([every(w[f"diff_lambda_{n}"][0]) for n in ("q1", "k1", "q2", "k2")], 1),
        "g_pre2": vec(w["attn_pre_norm_2"][0]), "g_post2": vec(w["attn_post_norm_2"][0]),
        "g_out2": np.concatenate([vec(w["nsa_out_norm_2"][0][rows]), vec(w["swa_out_norm_2"][0][rows])], 1),
        "pe": w["cmp_pos_2"][0].reshape(2, 16, 2, HD2).transpose(2, 3, 0, 1).reshape(P, 32),
        "cmp_w2": w["cmp_w2_2"][0].reshape(2, 2, P, HD2).transpose(2, 0, 1, 3).reshape(P, 256),
        "sinks": every(w["swa_sinks_2"][0][pairs]),
        "g_fpre2": vec(w["ffn_pre_norm_2"][0]), "g_fpost2": vec(w["ffn_post_norm_2"][0]),
        "cw2": in_turn(w["conv_w_2"][0], FF).reshape(3, 2 * FC, P).transpose(2, 1, 0).reshape(P, 6 * FC),
        "cb2": vec(in_turn(w["conv_b_2"][0], FF)),
    }
    p, t = np.arange(P), np.arange(S)
    f32 = np.float32
    inv1 = (np.float32(500000.0) ** (-np.arange(0, ROT1, 2, dtype=f32) / f32(ROT1))).astype(f32)
    parts["invf"] = np.where(p % 64 < ROT1, inv1[p % 8], 0).astype(f32)[:, None]
    parts["ident"] = np.eye(P, dtype=f32)
    perm1, perm2 = np.zeros((P, P), f32), np.zeros((P, P), f32)
    for c in range(0, P, 64):
        for k in range(8):
            perm1[c + 8 + k, c + k], perm1[c + k, c + 8 + k] = -1, 1
        for k in range(32):
            perm2[c + 32 + k, c + k], perm2[c + k, c + 32 + k] = -1, 1
    parts["perm1"], parts["perm2"] = perm1, perm2
    parts["causal"] = np.where(p[None, :] <= p[:, None], 0, NEG).astype(f32)
    parts["band"] = np.where(p[None, :] > p[:, None], 0, NEG).astype(f32)
    cm = np.zeros((P, 2, 16), f32)
    ends = np.arange(NCMP) * CMP_STRIDE + CMP_LEN - 1
    for tt in range(NT):
        cm[:, tt, :NCMP] = np.where(ends[None, :] <= (tt * P + p)[:, None], 0, NEG)
    parts["cmask"] = cm.reshape(P, 32)
    parts["rowok"] = np.stack([(tt * P + p >= CMP_LEN - 1) for tt in range(NT)], 1).astype(f32)
    inv2 = (np.float32(10000.0) ** (-np.arange(32, dtype=f32) / f32(32))).astype(f32)
    ang = t.astype(f32)[None, :] * inv2[p % 32][:, None]
    parts["cos2"], parts["sin2"] = np.cos(ang).astype(f32), np.sin(ang).astype(f32)
    for name, n in CONSTS:
        assert parts[name].shape == (P, n), (name, parts[name].shape)
    return np.concatenate([parts[name] for name, _ in CONSTS], 1)


def kernel(**inputs):
    import concourse.bacc as bacc
    from concourse.bass_utils import run_bass_kernel_spmd

    w = {k: np.asarray(v) for k, v in inputs.items()}
    tiles, rows = weight_tiles(w)
    arrays = {
        "weights": tiles, "consts": np.ascontiguousarray(packed_constants(w, rows)),
        "x_in": np.ascontiguousarray(w["x"][0].T), "mem_in": np.ascontiguousarray(w["mem"][0].T),
        "positions": w["positions"],
    }
    nc = bacc.Bacc("TRN2", target_bir_lowering=False, num_devices=1)
    args = [nc.dram_tensor(n, a.shape, mybir.dt.from_np(a.dtype), kind="ExternalInput").ap() for n, a in arrays.items()]
    args.append(nc.dram_tensor("out", (D, S), F32, kind="ExternalOutput").ap())
    build(nc, *args)
    r = run_bass_kernel_spmd(nc, [arrays], core_ids=[0])
    return np.ascontiguousarray(r.results[0]["out"].T)[None]
```

```python
import concourse.bass as bass
from concourse import mybir
from contextlib import ExitStack, contextmanager
import math
import numpy as np

F32 = mybir.dt.float32
F32R = mybir.dt.float32r
BF16 = mybir.dt.bfloat16
I32 = mybir.dt.int32
U32 = mybir.dt.uint32
ALU = mybir.AluOpType
ACT = mybir.ActivationFunctionType
AX_X = mybir.AxisListType.X

P = 128
D = 1024
S = 256
NT = S // P
DC = D // P
FF = 2816
FC = FF // P
KC = 8
MB = 256
CONV = 31
DIFF_HEADS = 8
DIFF_SCALE = 64 ** -0.5
MEM_HEADS = 4
MEM_SCALE = 256 ** -0.5
LAMBDA_INIT = 0.8 - 0.6 * math.exp(-0.3)
ROT1 = 16
CMP_LEN, CMP_STRIDE = 32, 16
NCMP = S // CMP_STRIDE - 1
ROWS = 2 * NCMP
HD2 = 64
NSA_SCALE = HD2 ** -0.5
NEG = -1e30
MAGIC = 1.5 * 2 ** 23
TWO_PI = (6.28125, 0.0019350051879882812, 3.0199159819573245e-07)
PI_IN = 3.1415925
RMS_EPS, LN_EPS, SUBLN_EPS = 1e-6, 1e-5, 1e-5
CONV_ACT = (8, 4)
LO_POOL = 3

PLAN = [
    ("pw1", 8, 8), ("memk", 8, 8), ("memv", 8, 8), ("pw2", 4, 4),
    ("memq0", 4, 4), ("attn_mem0", 0, 4), ("memo0", 4, 4), ("gu0", 22, 22), ("down0", 12, 4),
    ("diffk", 4, 4), ("diffq", 4, 4), ("diffv", 4, 4), ("attn_diff", 0, 8), ("diffo", 4, 4),
    ("memq1", 4, 4), ("attn_mem1", 0, 4), ("memo1", 4, 4), ("gu1", 22, 22), ("down1", 12, 4),
    ("win", 8, 8), ("winv", 2, 2), ("cmp", 4, 2), ("attn_nsa", 0, 8), ("wout", 4, 4),
    ("up2", 22, 22), ("down2", 12, 4),
]
T0, G0 = {}, {}
_t = _g = 0
for _name, _nt, _ng in PLAN:
    T0[_name], G0[_name] = _t, _g
    _t, _g = _t + _nt, _g + _ng
TILES = _t
NTILES = {n: t for n, t, _ in PLAN}

CONSTS = [
    ("g_mix0", 8), ("g_mem0", 8), ("g_ffn0", 8), ("g_kv", 8), ("g_mix1", 8), ("g_mem1", 8), ("g_ffn1", 8),
    ("g_final", 8), ("b_pw1", 16), ("w_dw", DC * CONV), ("b_dw", 8), ("ln_g", 8), ("ln_b", 8), ("b_pw2", 8),
    ("g_sub", 1), ("lam", 256), ("g_pre2", 8), ("g_post2", 8), ("g_out2", 8), ("pe", 32), ("cmp_w2", 256),
    ("sinks", 8), ("g_fpre2", 8), ("g_fpost2", 8), ("cw2", 132), ("cb2", 44),
    ("invf", 1), ("ident", P), ("perm1", P), ("perm2", P), ("causal", P), ("band", P), ("cmask", 32),
    ("rowok", 2), ("cos2", S), ("sin2", S),
]
C0 = {}
_c = 0
for _name, _n in CONSTS:
    C0[_name] = (_c, _n)
    _c += _n
NCONST = _c
C0["g_both"] = (NCONST, DC)


class Chain:

    def __init__(self, eng, sem):
        self.eng, self.sem, self.base, self.k, self.i, self.per = eng, sem, 0, 0, None, 0

    def link(self, ins):
        self.wait(self.mark(ins))
        return ins

    def mark(self, ins):
        ins.then_inc(self.sem, 1)
        self.k += 1
        return self.k

    def wait(self, k):
        at = self.base + k
        self.eng.wait_ge(self.sem, at if self.i is None else self.i * self.per + at)

    @contextmanager
    def loop(self, n, per, start=0):
        self.base += self.k
        self.k = 0
        if n - start == 1:
            yield start
            assert self.k == per, (self.k, per)
            self.base += per
        else:
            with self.eng.Fori(start, n) as i:
                self.i, self.per = i, per
                self.base -= start * per
                yield i
                assert self.k == per, (self.k, per)
                self.i = None
            self.base += n * per
        self.k = 0


@contextmanager
def loop(eng, n, start=0):
    if n - start == 1:
        yield start
    else:
        with eng.Fori(start, n) as i:
            yield i


class Steps:

    def __init__(self, sem, steps):
        self.sem, self.first, self.n = sem, {}, dict(steps)
        total = 0
        for name, n in steps:
            self.first[name] = total
            total += n

    def at(self, name, k=None):
        return self.first[name] + (self.n[name] if k is None else k)


def build(nc, weights, consts, x_in, mem_in, positions, out):
    ctx = ExitStack()
    with ctx:
        def sb(name, shape, dt=F32, where=ctx):
            return where.enter_context(nc.sbuf_tensor(name, shape, dt))

        def sem(name):
            return ctx.enter_context(nc.semaphore(name))

        raw = [sb(f"raw{j}", [P, KC, MB]) for j in range(2)]
        whi = [sb(f"whi{j}", [P, KC, MB], F32R) for j in range(2)]
        wlo = [sb(f"wlo{j}", [P, KC, MB], F32R) for j in range(2)]
        X = sb("X", [P, DC, S])
        SQ = sb("SQ", [P, DC, S])
        Hhi, Hlo = sb("Hhi", [P, DC, S], F32R), sb("Hlo", [P, DC, S], F32R)
        H2hi, H2lo = sb("H2hi", [P, DC, S], F32R), sb("H2lo", [P, DC, S], F32R)
        FH = sb("FH", [P, FC, S], F32R)
        MKV = sb("MKV", [P, 4 * DC, S])
        cst = sb("cst", [P, NCONST + DC])
        R = sb("R", [P, S])
        TG, TU = sb("TG", [P, 2, S + 2]), sb("TU", [P, 2, S + 2])
        SG = sb("SG", [P, 2, S])
        E = sb("E", [P, 3, 2, S])
        PT = sb("PT", [P, 2, 2 * S])
        rope_c, rope_s = sb("rope_c", [P, S]), sb("rope_s", [P, S])
        ones = sb("ones", [P, P])
        rt = sb("rt", [P, 4, 16])
        nw = sb("nw", [P, 3, S])
        nwi = sb("nwi", [P, S], I32)
        mx, nb, sm, rs = (sb(n, [P, 2, 2]) for n in ("mx", "nb", "smx", "rs"))
        sk, ske = sb("skm", [P, 2, 2]), sb("ske", [P, 2, 2])
        lam, gsub = sb("lamt", [P, 4]), sb("gsub", [P, 1])
        gates = sb("gates", [P, NT, 24])
        HCm = sb("HCm", [P, 2, 2, 32])
        KCm, VCm = sb("KCm", [P, 16]), sb("VCm", [16, P])
        ident_b, causal_b, band_b = (sb(n, [P, P], BF16) for n in ("ident_b", "causal_b", "band_b"))
        cmask_b = sb("cmask_b", [P, 32], BF16)
        with ExitStack() as shared:
            FL = sb("FL", [P, FC, S], F32R, shared)
        A = sb("A", [P, FC, S])
        Af = A[:, :, :].rearrange("p c s -> p (c s)")
        U = Af[:, 0:DC * (S + CONV - 1)].rearrange("p (c s) -> p c s", c=DC)
        UC = A[:, 10:18, :]
        FHf = FH[:, :, :].rearrange("p c s -> p (c s)")
        Ohi, Olo = FH[:, 0:8, :], FH[:, 8:16, :]
        V2 = Af[:, 16 * S:20 * S].rearrange("p (t n) -> p t n", t=NT)
        ZT = Af[:, 20 * S:20 * S + 480]
        dve_sum = E[:, 2, 0, :]
        batch_sum, pool_sum = E[:, 0, 0:1, :], E[:, 1, 0:1, :]
        products = SQ[:, 0:8, :], A[:, 18:22, :]
        SQF = MKV[:, 8:16, :]
        RF = TU[:, 0, 2:2 + S]
        MG = MKV[:, 16:24, :]
        M2 = MKV[:, 0:8, :]

        acc = [ctx.enter_context(nc.psum_tensor(f"acc{j}", [P, 2, S], F32)) for j in range(2)]
        sc = ctx.enter_context(nc.psum_tensor("sc", [P, 4, 2 * S], F32))
        tp = ctx.enter_context(nc.psum_tensor("tp", [P, 2 * S], F32))
        st = ctx.enter_context(nc.psum_tensor("st", [P, 2 * S], F32))

        raw_loaded = [sem(f"raw_loaded{j}") for j in range(2)]
        cst_loaded, x_loaded, mem_loaded, pos_loaded = (sem(n) for n in ("cst_loaded", "x_loaded", "mem_loaded", "pos_loaded"))
        hi_out, lo_dve, lo_pool = sem("hi_out"), sem("lo_dve"), sem("lo_pool")
        tile_done, acc_free = sem("tile_done"), sem("acc_free")
        s_given, s_taken, s_sq, s_h = sem("given"), sem("taken"), sem("sq_ready"), sem("h_ready")
        stat_ready, rt_ready, spread_ready, st_used = (sem(n) for n in ("stat_ready", "rt_ready", "spread_ready", "st_used"))
        gain_loaded, mem_upper = sem("gain_loaded"), sem("mem_upper")
        tokens_ready, hid_turned, hid_copied = sem("tokens_ready"), sem("hid_turned"), sem("hid_copied")
        s_done, nb_ready, exp_done, p_ready = sem("s_done"), sem("nb_ready"), sem("exp_done"), sem("p_ready")
        t_done, pt_ready, pv_done = sem("t_done"), sem("pt_ready"), sem("pv_done")
        rot_ready, rot_used = sem("rot_ready"), sem("rot_used")
        consts_ready, conv_done, hid_ready, cmp_mm, cmp_ready = (sem(n) for n in ("consts_ready", "conv_done", "hid_ready", "cmp_mm", "cmp_ready"))
        x_final, out_done, u_ready = sem("x_final"), sem("out_done"), sem("u_ready")
        prod_ready, prod_used, conv_share = sem("prod_ready"), sem("prod_used"), sem("conv_share")
        dve_chain, act_chain, pool_chain = sem("dve_chain"), sem("act_chain"), sem("pool_chain")

        given = Steps(s_given, [("ln_sq", 4), ("ln", 4), ("lam", 1), ("rope", 1), ("gu0", 11), ("sub", 4), ("gu1", 11),
                                ("z", 2), ("outn", 4), ("post", 4), ("up2", 22)])
        taken = Steps(s_taken, [("x0", 4), ("pw1", 4), ("ln", 4), ("lam", 1), ("rope", 1), ("pw2", 4),
                                ("attn_mem0", 4), ("memo0", 4), ("gu0", 22), ("down0", 4), ("sub", 4), ("diffo", 4),
                                ("attn_mem1", 4), ("memo1", 4), ("gu1", 22), ("down1", 4), ("z", 2), ("gates", 1),
                                ("outn", 4), ("post", 4), ("up2", 22)])
        sq = Steps(s_sq, [("mix0", 1), ("ln", 4), ("pw2", 4), ("memo0", 4), ("down0", 4), ("attn_diff", 8), ("diffo", 4),
                          ("memo1", 4), ("down1", 4), ("attn_nsa", 8), ("wout", 4), ("post", 4), ("down2", 4)])
        h = Steps(s_h, [("x0", 4), ("mem", 1), ("ln", 4), ("pw2", 4), ("attn_mem0", 4), ("memo0", 4), ("gu0", 11),
                        ("down0", 4), ("sub", 4), ("diffo", 4), ("attn_mem1", 4), ("memo1", 4), ("gu1", 11), ("down1", 4),
                        ("z", 2), ("outn", 4), ("post", 4), ("up2", 11)])
        NORMS = ["mix0", "ln_mu", "ln_var", "mem0", "ffn0", "attn1", "sub", "mem1", "ffn1", "final", "pre2", "out2",
                 "post2", "fpre2", "fpost2"]
        N0 = {name: k for k, name in enumerate(NORMS)}
        RT = {"sub": 0, "out2": 1, "attn1": 2, "pre2": 3}
        SQ_OF = {"mix0": "mix0", "mem0": "pw2", "ffn0": "memo0", "attn1": "down0", "mem1": "diffo", "ffn1": "memo1",
                 "pre2": "down1", "fpre2": "post"}
        ROT0 = {"diffk": 0, "diffq": 4, "win": 8}
        ROTS = {"diffk": 4, "diffq": 4, "win": 7}
        ROT_SLOT = {"diffk": 8, "diffq": 0, "win": 0}
        KC_SLOT, Q_SLOT, KS_SLOT, KW_SLOT, KSW_SLOT, VC_SLOT = 0, 2, 10, 11, 12, 14

        def C(name, a=0, n=None):
            c0, width = C0[name]
            return cst[:, c0 + a:c0 + a + (width - a if n is None else n)]

        def mem_units(layer):
            units = []
            for h in range(MEM_HEADS):
                kv = 2 * DC + 8 * layer + 2 * h
                u = dict(kind="mem", scale=MEM_SCALE, keys=S, group=h, last=True, S=[], T=[], PV=[])
                for m in range(2):
                    u["S"].append(([(A[:, 2 * h + c, m * P:(m + 1) * P], MKV[:, 8 * layer + 2 * h + c, :])
                                    for c in range(2)], []))
                for m in range(2):
                    for kt in range(NT):
                        u["T"].append((m, kt * P, P, kt * S + m * P))
                for e in range(2):
                    u["PV"] += [((slice(0, P), e * S, S), MKV[:, kv + kt, e * P:(e + 1) * P],
                                 (P, kt * S, S), kt == 0, kt == NT - 1) for kt in range(NT)]
                units.append(u)
            return units

        def diff_units():
            units = []
            for h in range(DIFF_HEADS):
                for qt in range(NT):
                    nk = (qt + 1) * P
                    u = dict(kind="diff", scale=DIFF_SCALE, keys=nk, group=h, slot=h, last=qt == NT - 1, S=[], T=[], PV=[])
                    for m in range(2):
                        r = slice(64 * m, 64 * m + 64)
                        u["S"].append(([(A[r, h, qt * P:(qt + 1) * P], A[r, 8 + h, 0:nk])],
                                       [(causal_b, nk - P, P)]))
                    for kt in range(qt + 1):
                        u["T"].append((0, kt * P, P, kt * P))
                        u["PV"].append(((slice(0, P), qt * P, P),
                                        MKV[:, 2 * DC + 2 * (h // 2) + kt, (h % 2) * P:(h % 2 + 1) * P],
                                        (P, kt * P, P), kt == 0, kt == qt))
                    units.append(u)
            return units

        def nsa_units():
            units = []
            for n, c in enumerate((4, 5, 6, 7, 0, 1, 2, 3)):
                swa = c >= 4
                for qt in range(NT):
                    branches = ["swa"] if swa else ["slc", "win", "cmp"]
                    for b, kind in enumerate(branches):
                        nk = NCMP if kind == "cmp" else (qt + 1) * P
                        u = dict(kind=kind, scale=NSA_SCALE, keys=nk, group=n, slot=Q_SLOT + c, S=[], T=[], PV=[], qt=qt, c=c,
                                 last=qt == NT - 1 and b == len(branches) - 1)
                        for m in range(2):
                            r = slice(64 * m, 64 * m + 64)
                            k = {"slc": A[r, KS_SLOT, 0:nk], "win": A[r, KW_SLOT, 0:nk], "swa": A[r, KSW_SLOT, 0:nk],
                                 "cmp": KCm[r, 0:NCMP]}[kind]
                            masks = [(causal_b, nk - P, P)] if kind != "cmp" else [(cmask_b[:, 16 * qt:16 * qt + NCMP], 0, NCMP)]
                            if kind == "swa" and qt == 1:
                                masks.append((band_b, 0, P))
                            u["S"].append(([(A[r, Q_SLOT + c, qt * P:(qt + 1) * P], k)], masks))
                            first, end = b == 0, b == len(branches) - 1
                            kts = 1 if kind == "cmp" else qt + 1
                            for kt in range(kts):
                                rows = NCMP if kind == "cmp" else P
                                u["T"].append((m, kt * P, rows, m * S + kt * P))
                                v = (VCm[0:NCMP, 64 * m:64 * m + 64] if kind == "cmp" else
                                     V2[:, kt, {"slc": 0, "win": P, "swa": 2 * P}[kind] + 64 * m:][:, 0:64])
                                u["PV"].append(((r, qt * P, P), v, (rows, m * S + kt * P, P),
                                                first and kt == 0, end and kt == kts - 1))
                        units.append(u)
            return units

        ATTN = {"attn_mem0": mem_units(0), "attn_diff": diff_units(), "attn_mem1": mem_units(1),
                "attn_nsa": nsa_units()}
        U0, n_units = {}, 0
        for name, _, _ in PLAN:
            if name in ATTN:
                U0[name] = n_units
                n_units += len(ATTN[name])

        def tiles_done(name):
            return T0[name] + NTILES[name]

        block = ctx.enter_context(nc.Block())

        @block.sync
        def _(sp):
            cols = lambda ap: ap.rearrange("(c p) t -> p c t", p=P)
            gains = C0["b_pw1"][0]
            sp.dma_start(cst[:, 0:gains], consts[:, 0:gains]).then_inc(gain_loaded, 16)
            sp.dma_start(X[:, :, :], cols(x_in)).then_inc(x_loaded, 16)
            for j in range(2):
                sp.dma_start(raw[j][:, :, :], weights[j].rearrange("p (k m) -> p k m", k=KC)).then_inc(raw_loaded[j], 16)
            sp.dma_start(cst[:, gains:NCONST], consts[:, gains:]).then_inc(cst_loaded, 16)
            sp.dma_start(UC, cols(mem_in)).then_inc(mem_loaded, 16)
            sp.dma_start(PT[:, 0, 0:S].bitcast(I32), positions.partition_broadcast(P)).then_inc(pos_loaded, 16)
            with sp.Fori(1, TILES // 2) as i:
                for j in range(2):
                    sp.wait_ge(lo_dve, 2 * i + (j - 1))
                    sp.wait_ge(lo_pool, 2 * i + (j - 1))
                    sp.dma_start(raw[j][:, :, :], weights[bass.ds(2 * i + j, 1)].rearrange("o p (k m) -> p (o k) m", k=KC))\
                        .then_inc(raw_loaded[j], 16)
            for p in range(4):
                sp.wait_ge(x_final, p + 1)
                sp.dma_start(cols(out)[:, 2 * p:2 * p + 2, :], X[:, 2 * p:2 * p + 2, :]).then_inc(out_done, 16)
            sp.wait_ge(out_done, 4 * 16)

        @block.gpsimd
        def _(pool):
            pc = Chain(pool, pool_chain)

            def lower(i, j):
                pool.wait_ge(hi_out, 4 * i + (2 * j + 1))
                pool.tensor_tensor(out=wlo[j][:, 0:LO_POOL, :], in0=raw[j][:, 0:LO_POOL, :],
                                   in1=whi[j][:, 0:LO_POOL, :].bitcast(F32), op=ALU.subtract).then_inc(lo_pool, 1)

            for i in range(2):
                for j in range(2):
                    lower(i, j)
            with pc.loop(DC + 2, 4, 2) as i:
                lower(i, 0)
                for b in range(2):
                    pool.wait_ge(prod_ready, 2 * i + (b - 3))
                    n = CONV_ACT[b] // 2
                    while n > 1:
                        lo, up = products[b][:, 0:n, :], products[b][:, n:2 * n, :]
                        pc.link(pool.tensor_tensor(out=lo, in0=lo, in1=up, op=ALU.add))
                        n //= 2
                    first, second = products[b][:, 0:1, :], products[b][:, 1:2, :]
                    if b == 0:
                        pool.tensor_tensor(out=batch_sum, in0=first, in1=second, op=ALU.add).then_inc(prod_used, 1)
                        lower(i, 1)
                    else:
                        pc.link(pool.tensor_tensor(out=first, in0=first, in1=second, op=ALU.add))
                        pool.wait_ge(prod_used, i)
                        pool.wait_ge(conv_done, i - 1)
                        pool.tensor_tensor(out=pool_sum, in0=batch_sum, in1=first, op=ALU.add).then_inc(conv_share, 1)
                        pool.wait_ge(conv_share, i)
            with pool.Fori(DC + 2, TILES // 2) as i:
                for j in range(2):
                    lower(i, j)

        @block.tensor
        def _(pe):
            ident = C("ident")

            def three(dst, w, wl, x, xl, first, last):
                pe.matmul(dst, w, x, start=first, stop=False)
                pe.matmul(dst, w, xl, start=False, stop=False)
                return pe.matmul(dst, wl, x, start=False, stop=last)

            def tile_in(t):
                pe.wait_ge(lo_dve, t + 1)
                pe.wait_ge(lo_pool, t + 1)

            def columns(j, xhi, xlo, m, ks=range(KC), turned=False, first=True, last=True):
                o = slice(m * P, (m + 1) * P)
                for k in ks:
                    w, wl, x, xl = whi[j][:, k, :], wlo[j][:, k, :], xhi[:, k, :], xlo[:, k, :]
                    a, z = first and k == ks[0], last and k == ks[-1]
                    if turned:
                        mm = three(acc[j][:, m, :], x[:, o], xl[:, o], w, wl, a, z)
                    else:
                        mm = three(acc[j][:, m, :], w[:, o], wl[:, o], x, xl, a, z)
                return mm

            def turn(name, i, t):
                per, k = t
                n = ROT0[name] + k
                perm = C("perm2" if name == "win" else "perm1")
                if per == 0:
                    at = ROT_SLOT[name] + 2 * k
                    pe.wait_ge(acc_free, G0[name] + k + 3)
                    if n >= 2:
                        pe.wait_ge(rot_used, n - 1)
                    pairs = A[:, at:at + 2, :]
                else:
                    pe.wait_ge(acc_free, per * i + (G0[name] + k + 3))
                    pe.wait_ge(rot_used, per * i + (n - 1))
                    pairs = A[:, bass.ds(2 * per * i + (ROT_SLOT[name] + 2 * k), 2), :]
                pe.matmul(sc[:, n % 2, :], perm, pairs, start=True, stop=True).then_inc(rot_ready, 1)

            def stage(name, xhi, xlo, turned=False, source=None, norm_name=None, rotated=None):
                start = 0
                if source is not None:
                    start = 1
                    tile_in(T0[name])
                    pe.wait_ge(acc_free, G0[name] + 1)
                    if h.n[source] == 4:
                        pe.wait_ge(s_h, h.at(source, 3))
                        for m in range(2):
                            columns(0, xhi, xlo, m, range(6), first=m == 0, last=False)
                        pe.wait_ge(s_h, h.at(source))
                        for m in range(2):
                            mm = columns(0, xhi, xlo, m, range(6, KC), first=False, last=m == 1)
                    else:
                        pe.wait_ge(s_h, h.at(source))
                        for m in range(2):
                            mm = columns(0, xhi, xlo, m)
                    mm.then_inc(tile_done, 1)
                    if norm_name:
                        pe.wait_ge(s_sq, sq.at(SQ_OF[norm_name]))
                        if norm_name == "pre2":
                            norm_stats("final")
                        norm_stats(norm_name, SQF if norm_name == "pre2" else SQ)
                    tile_in(T0[name] + 1)
                    pe.wait_ge(acc_free, G0[name] + 2)
                    columns(1, xhi, xlo, 0)
                    columns(1, xhi, xlo, 1).then_inc(tile_done, 1)
                    if name in ROT0:
                        turn(name, 0, (0, 0))
                turns = NTILES[name] // 2
                for begin, end in ((0, 1), (1, turns)) if rotated else ((start, turns),):
                    with loop(pe, end, begin) as i:
                      for j in range(2):
                          tile_in(2 * i + (T0[name] + j))
                          pe.wait_ge(acc_free, 2 * i + (G0[name] + j + 1))
                          for m in range(2):
                              mm = columns(j, xhi, xlo, m, turned=turned)
                          mm.then_inc(tile_done, 1)
                          if rotated and begin == j == 0:
                              turn(rotated, 0, (0, ROTS[rotated] - 1))
                          elif name in ROT0 and isinstance(i, int):
                              turn(name, 0, (0, 2 * i + j - 1))
                          elif name in ROT0:
                              turn(name, i, (2, j - 1))

            def down(name, source):
                def group(i, g, follow=False):
                    pe.wait_ge(acc_free, 2 * i + (G0[name] + g + 1))
                    for part in range(3):
                        j = (3 * g + part) % 2
                        ks = range(8 * part, min(8 * part + 8, FC))
                        tile_in(6 * i + (T0[name] + 3 * g + part))
                        for some in (ks[:4], ks[4:]):
                            if follow:
                                pe.wait_ge(s_h, h.at(source, some[-1] // 2 + 1))
                            for m in range(2):
                                for k in some:
                                    o = slice(m * P, (m + 1) * P)
                                    mm = three(acc[g][:, m, :], whi[j][:, k - 8 * part, o], wlo[j][:, k - 8 * part, o],
                                               FH[:, k, :], FL[:, k, :], m == k == 0, m == 1 and k == FC - 1)
                        mm.then_inc(tile_done, 1)

                group(0, 0, follow=True)
                group(0, 1)
                for g in range(2):
                    group(1, g)

            def norm_stats(name, src=SQ, ready=None):
                if N0[name] > 0:
                    pe.wait_ge(st_used, N0[name])
                for k in range(DC):
                    if ready:
                        ready(k)
                    mm = pe.matmul(st[:, 0:S], ones[:, :], src[:, k, :], start=k == 0, stop=k == DC - 1)
                mm.then_inc(stat_ready, 1)

            def norm(name, before):
                norm_stats(name, SQ, lambda k: pe.wait_ge(s_sq, sq.at(before, k // 2 + 1)) if k % 2 == 0 else None)

            def to_tokens(name):
                pe.wait_ge(st_used, N0[name] + 1)
                pe.wait_ge(acc_free, G0[{"attn1": "diffk", "pre2": "win"}[name]] + 3)
                for tt in range(NT):
                    mm = pe.matmul(st[:, tt:tt + 1], R[0:1, tt * P:(tt + 1) * P], ones[0:1, 0:1], start=True, stop=True)
                mm.then_inc(tokens_ready, 1)

            def group_stats(name, g):
                norm_name, columns_of = {"attn_diff": ("sub", lambda slot: slot), "attn_nsa": ("out2", lambda slot: slot // 4)}[name]
                slot = [u["slot"] for u in ATTN[name] if u["group"] == g][0] - (Q_SLOT if name == "attn_nsa" else 0)
                pe.wait_ge(s_sq, sq.at(name, g + 1))
                if g == 0:
                    pe.wait_ge(st_used, N0[norm_name])
                for tt in range(NT):
                    col = 2 * columns_of(slot) + tt
                    mm = pe.matmul(st[:, col:col + 1], SQ[:, slot, tt * P:(tt + 1) * P], ones[:, 0:1],
                                   start=g == tt == 0, stop=g == 7 and tt == NT - 1)
                if g == 7:
                    mm.then_inc(stat_ready, 1)

            def spread(name, jobs):
                pe.wait_ge(rt_ready, RT[name] + 1)
                for col, dst in jobs:
                    mm = pe.matmul(dst, rt[:, RT[name], col:col + 1].broadcast_to((P, P)), ident, start=True, stop=True)
                mm.then_inc(spread_ready, 1)

            def attention(name, steps={}):
                units, u0 = ATTN[name], U0[name]
                summed = 8 if "mem" in name else 0
                ends = {u["group"]: k for k, u in enumerate(units)}
                for s in range(len(units) + 3):
                    if s in steps:
                        steps[s]()
                    if s < len(units):
                        u, n = units[s], u0 + s
                        if n >= 2:
                            pe.wait_ge(exp_done, n - 1)
                        for m, (products, masks) in enumerate(u["S"]):
                            dst = sc[:, 2 * (n % 2) + m, :]
                            for k, (q, key) in enumerate(products):
                                mm = pe.matmul(dst[:, 0:u["keys"]], q, key, start=k == 0,
                                               stop=k == len(products) - 1 and not masks)
                            for k, (mask, c0, w) in enumerate(masks):
                                mm = pe.matmul(dst[:, c0:c0 + w], ident_b[:, :], mask if w < P else mask[:, :],
                                               start=False, stop=k == len(masks) - 1)
                        mm.then_inc(s_done, 1)
                    if 2 <= s < len(units) + 2:
                        u, n = units[s - 2], u0 + s - 2
                        pe.wait_ge(p_ready, n + 1)
                        if n >= 1:
                            pe.wait_ge(pt_ready, n)
                        for m, c0, w, to in u["T"]:
                            mm = pe.transpose(tp[0:w, to:to + P], E[:, n % 3, m, c0:c0 + w], ident)
                        mm.then_inc(t_done, 1)
                    if s >= 3:
                        u, n = units[s - 3], u0 + s - 3
                        g = G0[name] + u["group"]
                        pe.wait_ge(pt_ready, n + 1)
                        pe.wait_ge(acc_free, g + 1)
                        for (rows, c0, w), v, (kn, p0, pw), first, last in u["PV"]:
                            dst = acc[g % 2][:, :, :].rearrange("p a b -> p (a b)")
                            mm = pe.matmul(dst[rows, c0:c0 + w], v, PT[0:kn, n % 2, p0:p0 + pw], start=first, stop=last)
                        mm.then_inc(pv_done, 1)
                    if summed < 8 and s >= ends[summed] + 7 and (name == "attn_diff" or s > 10):
                        group_stats(name, summed)
                        summed += 1
                while summed < 8:
                    group_stats(name, summed)
                    summed += 1

            def wait_h(name):
                pe.wait_ge(s_h, h.at(name))

            stage("pw1", Hhi, Hlo, source="x0", norm_name="mix0")
            wait_h("mem")
            stage("memk", H2hi, H2lo)
            def value_tile(k):
                tile_in(T0["memv"] + k)
                pe.wait_ge(acc_free, G0["memv"] + k + 1)
                for m in range(2):
                    mm = columns(k % 2, H2hi, H2lo, m, turned=True)
                mm.then_inc(tile_done, 1)

            for k in (0, 1, 2):
                value_tile(k)
            norm_stats("ln_mu", UC, lambda k: pe.wait_ge(conv_done, 1 + k + 1))
            value_tile(3)
            norm("ln_var", "ln")
            for k in (4, 5, 6, 7):
                value_tile(k)
            stage("pw2", Ohi, Olo, source="ln")
            pe.wait_ge(consts_ready, 1)
            for layer, before in ((0, "pw2"), (1, "diffo")):
                stage(f"memq{layer}", Hhi, Hlo, source=before, norm_name=f"mem{layer}")
                pe.wait_ge(acc_free, G0[f"attn_mem{layer}"] + 2)
                attention(f"attn_mem{layer}")
                stage(f"memo{layer}", Ohi, Olo, source=f"attn_mem{layer}")
                stage(f"gu{layer}", Hhi, Hlo, source=f"memo{layer}", norm_name=f"ffn{layer}")
                down(f"down{layer}", f"gu{layer}")
                if layer == 1:
                    break
                stage("diffk", Hhi, Hlo, source="down0", norm_name="attn1")
                stage("diffq", H2hi, H2lo, rotated="diffk")
                to_tokens("attn1")
                stage("diffv", Hhi, Hlo, turned=True, rotated="diffq")
                pe.wait_ge(acc_free, G0["attn_diff"] + 2)
                pe.wait_ge(rot_used, ROT0["win"])
                attention("attn_diff")
                spread("sub", [(2 * hd + tt, sc[:, hd // 2, (hd % 2) * S + tt * P:][:, 0:P])
                               for hd in range(DIFF_HEADS) for tt in range(NT)])
                stage("diffo", Ohi, Olo, source="sub")
            stage("win", Hhi, Hlo, source="down1", norm_name="pre2")
            to_tokens("pre2")
            stage("winv", Hhi, Hlo, turned=True)
            for kv in range(2):
                pe.wait_ge(s_h, h.at("z", kv + 1))
                pe.wait_ge(acc_free, G0["cmp"] + kv + 1)
                for part in range(2):
                    tile_in(T0["cmp"] + 2 * kv + part)
                    for k in range(KC):
                        z = [FHf[:, (2 * kv + l) * 480 + (8 * part + k) * ROWS:][:, 0:ROWS] for l in range(2)]
                        mm = three(acc[kv][0:ROWS, 0, :], z[0], z[1], whi[part][:, k, :], wlo[part][:, k, :],
                                   part == k == 0, part == 1 and k == KC - 1)
                    mm.then_inc(tile_done, 1)

            def turn_hidden():
                pe.wait_ge(hid_ready, 2)
                pe.wait_ge(st_used, N0["pre2"] + 1)
                for kv in range(2):
                    for m in range(2):
                        mm = pe.transpose(st[:, (2 * kv + m) * 64:][:, 0:ROWS], SG[0:ROWS, kv, m * P:(m + 1) * P],
                                          C("ident")[0:ROWS, 0:ROWS])
                mm.then_inc(hid_turned, 1)

            def compressed():
                pe.wait_ge(hid_copied, 1)
                for hd in range(2):
                    for m in range(2):
                        pe.matmul(st[64 * hd:64 * hd + 64, S:S + NCMP], C("cmp_w2", 64 * m, 64),
                                  HCm[:, 0, m, hd * NCMP:(hd + 1) * NCMP], start=m == 0, stop=m == 1)
                for hd in range(2):
                    for m in range(2):
                        mm = pe.matmul(st[0:NCMP, S + P + 64 * hd:][:, 0:64], HCm[:, 1, m, hd * NCMP:(hd + 1) * NCMP],
                                       C("cmp_w2", 128 + 64 * m, 64), start=m == 0, stop=m == 1)
                mm.then_inc(cmp_mm, 1)

            pe.wait_ge(rot_used, ROT0["win"] + ROTS["win"])
            attention("attn_nsa", {3: turn_hidden, 7: compressed, 10: lambda: pe.wait_ge(cmp_ready, 1)})
            spread("out2", [(2 * b + tt, sc[:, 0, b * S + tt * P:][:, 0:P]) for b in range(2) for tt in range(NT)])
            stage("wout", Ohi, Olo, source="outn")
            norm("post2", "wout")
            stage("up2", Hhi, Hlo, source="post", norm_name="fpre2")
            down("down2", "up2")
            norm("fpost2", "down2")

        @block.scalar
        def _(act):
            ac = Chain(act, act_chain)

            def split(load, j, done=None):
                act.wait_ge(raw_loaded[j], load)
                if done is not None:
                    act.wait_ge(tile_done, done)
                act.activation(whi[j][:, 0:LO_POOL, :], raw[j][:, 0:LO_POOL, :], ACT.Copy).then_inc(hi_out, 1)
                act.activation(whi[j][:, LO_POOL:KC, :], raw[j][:, LO_POOL:KC, :], ACT.Copy).then_inc(hi_out, 1)

            def ahead(name, i, per, k, last=False):
                if not last:
                    t = T0[name] + k
                    split(16 * (per // 2) * i + 16 * (t // 2 + 2), k % 2, per * i + (t + 1))

            def acc_out(name, g):
                act.wait_ge(acc_free, g + (G0[name] + 3))

            def hi_scaled(dst, src, gain, g0):
                for c in range(2):
                    ins = act.activation(dst[:, c, :], src[:, c, :], ACT.Copy, scale=gain(g0 + c))
                return ins

            def gcol(name):
                return lambda c: cst[:, bass.ds(c + C0[name][0], 1)] if not isinstance(c, int) else C(name, c, 1)

            def pair(t, c):
                return t[:, bass.ds(c, 2), :] if not isinstance(c, int) else t[:, c:c + 2, :]

            def residual(name, per, outs, last_stage=False):
                n = 2
                for start, stop in ([(0, 2)] if not last_stage else [(0, 1), (1, 2)]):
                    with loop(act, stop, start) as i:
                        for g in range(2):
                            def weights(ks):
                                for kk in ks:
                                    ahead(name, i, per, kk, last=last_stage and start == 1 and kk >= per - 2)

                            ks = range(g * per // 2, (g + 1) * per // 2)
                            weights(ks[:-1] if g else ks)
                            c = 4 * i + 2 * g
                            acc_out(name, 2 * i + g)
                            src = X if name not in ("wout", "down2") else M2
                            for b, gain in outs:
                                ins = hi_scaled(pair(b, c), pair(src, c), gcol(gain), c)
                            if outs:
                                ins.then_inc(s_taken, 1)
                            if g:
                                weights(ks[-1:])
                            if name == "down1":
                                for k in range(2):
                                    act.activation(pair(SQF, c)[:, k, :], pair(src, c)[:, k, :], ACT.Square,
                                                   scale=gcol("g_final")(c + k))
                            act.activation(pair(SQ, c), pair(src, c), ACT.Square).then_inc(s_sq, 1)

            def plain(name):
                with loop(act, NTILES[name] // 2) as i:
                    for j in range(2):
                        ahead(name, i, 2, j)

            def ffn(name, func):
                conv = name == "up2"
                src = E[:, 1, :, :] if conv else TU[:, :, 2:2 + S]

                def hidden(i):
                    act.wait_ge(s_given, 2 * i + given.at(name, 2) if conv else i + given.at(name, 1))
                    act.activation(pair(FH, 2 * i), src, ACT.Copy).then_inc(s_taken, 1)

                for start, stop in ((0, 1), (1, 11)):
                    with loop(act, stop, start) as i:
                        ahead(name, i, 2, 0)
                        if start:
                            hidden(i + (-1))
                        if conv:
                            act.wait_ge(s_given, 2 * i + given.at(name, 1))
                            for c in range(2):
                                ins = act.activation(SG[:, c, :], E[:, 0, c, :], func, bias=gcol("cb2")(4 * i + c))
                            ins.then_inc(s_taken, 1)
                        else:
                            acc_out(name, 2 * i)
                            act.activation(SG[:, :, :], TG[:, :, 2:2 + S], func).then_inc(s_taken, 1)
                        ahead(name, i, 2, 1)
                hidden(10)

            def attention(name):
                units, u0 = ATTN[name], U0[name]
                for s in range(len(units) + 5):
                    if s < len(units):
                        u, n = units[s], u0 + s
                        act.wait_ge(nb_ready, n + 1)
                        if n >= 3:
                            act.wait_ge(t_done, n - 2)
                        for m in range(2):
                            ins = act.activation(E[:, n % 3, m, 0:u["keys"]], sc[:, 2 * (n % 2) + m, 0:u["keys"]], ACT.Exp,
                                                 bias=nb[:, n % 2, m:m + 1], scale=u["scale"],
                                                 accum_out=rs[:, n % 2, m:m + 1])
                        if u["kind"] == "swa":
                            ins = act.activation(ske[:, n % 2, :], sk[:, n % 2, :], ACT.Exp)
                        ins.then_inc(exp_done, 1)
                    if 2 <= s < len(units) + 2:
                        u, n = units[s - 2], u0 + s - 2
                        act.wait_ge(t_done, n + 1)
                        if n >= 2:
                            act.wait_ge(pv_done, n - 1)
                        rows = u["T"][0][2]
                        if u["kind"] == "cmp":
                            a, b = (t.rearrange("p (m k) -> p m k", m=2)[0:rows, :, 0:P] for t in (PT[:, n % 2, :], tp[:, :]))
                        elif u["kind"] in ("mem", "diff") or u["keys"] == S:
                            w = max(to for *_, to in u["T"]) + P
                            a, b = PT[:, n % 2, 0:w], tp[:, 0:w]
                        else:
                            a, b = (t.rearrange("p (m k) -> p m k", m=2)[:, :, 0:P] for t in (PT[:, n % 2, :], tp[:, :]))
                        act.activation(a, b, ACT.Copy).then_inc(pt_ready, 1)
                    if s >= 5 and units[s - 5]["last"]:
                        g = units[s - 5]["group"]
                        acc_out(name, g)
                        if "mem" in name:
                            act.activation(Ohi[:, 2 * g:2 * g + 2, :], A[:, 2 * g:2 * g + 2, :], ACT.Copy).then_inc(s_taken, 1)
                        else:
                            slot = units[s - 5]["slot"]
                            to = slot - (Q_SLOT if name == "attn_nsa" else 0)
                            act.activation(SQ[:, to, :], A[:, slot, :], ACT.Square).then_inc(s_sq, 1)

            act.wait_ge(gain_loaded, 16)
            act.wait_ge(x_loaded, 16)
            for p in range(4):
                hi_scaled(pair(Hhi, 2 * p), pair(X, 2 * p), gcol("g_mix0"), 2 * p).then_inc(s_taken, 1)
            split(16, 0)
            act.activation(SQ[:, :, :], X[:, :, :], ACT.Square).then_inc(s_sq, 1)
            split(16, 1)
            act.wait_ge(cst_loaded, 16)

            def conv_products(i, base, b):
                c = i + base
                act.wait_ge(u_ready, c + 1)
                if b == 0:
                    act.wait_ge(prod_used, i + (base + 1))
                else:
                    act.wait_ge(conv_share, i + (base + 1))
                for k in range(CONV_ACT[b]):
                    tap = CONV - sum(CONV_ACT[b:]) + k
                    o = C0["w_dw"][0] + CONV * base + tap
                    if isinstance(c, int):
                        src, w = U[:, c, tap:tap + S], cst[:, CONV * i + o:CONV * i + o + 1]
                    else:
                        src = U[:, bass.ds(c, 1), tap:tap + S].rearrange("p o s -> p (o s)")
                        w = cst[:, bass.ds(CONV * i + o, 1)]
                    ins = act.activation(products[b][:, k, :], src, ACT.Copy, scale=w)
                ins.then_inc(prod_ready, 1)

            for start, stop in ((0, 1), (1, 4)):
                with loop(act, stop, start) as i:
                    ahead("pw1", i, 2, 0)
                    if start:
                        conv_products(i, -1, 0)
                    ahead("pw1", i, 2, 1)
                    acc_out("pw1", 2 * i + 1)
                    for c in range(2):
                        ins = act.activation(SG[:, c, :], TU[:, c, 2:2 + S], ACT.Sigmoid, bias=gcol("b_pw1")(4 * i + (2 + c)))
                    ins.then_inc(s_taken, 1)
                    if start:
                        conv_products(i, -1, 1)
                    else:
                        act.wait_ge(mem_loaded, 16)
                        act.activation(H2hi[:, :, :], UC, ACT.Copy).then_inc(mem_upper, 1)
            act.wait_ge(acc_free, G0["memk"] + 2)
            with loop(act, 4) as i:
                for j in range(2):
                    ahead("memk", i, 2, j)
                    act.activation(pair(MKV, 4 * i + 2 * j), acc[j][:, :, :], ACT.Copy).then_inc(acc_free, 1)
                    conv_products(i, 3, j)

            def value_tile(k):
                ahead("memv", 0, 8, k)
                act.activation(pair(MKV, 2 * DC + 2 * k), acc[k % 2][:, :, :], ACT.Copy).then_inc(acc_free, 1)

            for k in (0, 1):
                value_tile(k)
                conv_products(0, 7, k)
            value_tile(2)
            for p in range(4):
                act.wait_ge(s_given, given.at("ln_sq", p + 1))
                act.activation(pair(SQ, 2 * p), pair(UC, 2 * p), ACT.Square).then_inc(s_sq, 1)
            value_tile(3)
            for p in range(4):
                act.wait_ge(s_given, given.at("ln", p + 1))
                for c in range(2 * p, 2 * p + 2):
                    ac.link(act.activation(SQ[:, c, :], UC[:, c, :], ACT.Silu, scale=C("ln_g", c, 1), bias=C("ln_b", c, 1)))
                act.activation(Ohi[:, 2 * p:2 * p + 2, :], SQ[:, 2 * p:2 * p + 2, :], ACT.Copy).then_inc(s_taken, 1)
                if p != 2:
                    value_tile((4, 5, None, 6)[p])
            value_tile(7)
            act.wait_ge(s_given, given.at("lam"))
            act.activation(lam[:, 2:4], lam[:, 0:2], ACT.Exp).then_inc(s_taken, 1)
            act.wait_ge(s_given, given.at("rope"))
            act.activation(rope_s[:, :], TG[:, 0, 0:S], ACT.Sin)
            act.activation(rope_c[:, :], TG[:, 1, 0:S], ACT.Sin).then_inc(s_taken, 1)
            residual("pw2", 2, [(Hhi, "g_mem0")])
            for layer in range(2):
                plain(f"memq{layer}")
                attention(f"attn_mem{layer}")
                residual(f"memo{layer}", 2, [(Hhi, f"g_ffn{layer}")])
                ffn(f"gu{layer}", ACT.Silu)
                if layer == 1:
                    break
                residual("down0", 6, [(Hhi, "g_kv"), (H2hi, "g_mix1")])
                plain("diffk")
                plain("diffq")
                plain("diffv")
                attention("attn_diff")
                for p in range(4):
                    act.wait_ge(s_given, given.at("sub", p + 1))
                    act.activation(Ohi[:, 2 * p:2 * p + 2, :], A[:, 2 * p:2 * p + 2, :], ACT.Copy,
                                   scale=gsub[:, 0:1]).then_inc(s_taken, 1)
                residual("diffo", 2, [(Hhi, "g_mem1")])
            residual("down1", 6, [(Hhi, "g_both")])

            def ready_chunks(name, src, dst, gain, squares=True):
                for p in range(4):
                    act.wait_ge(s_given, given.at(name, p + 1))
                    hi_scaled(pair(dst, 2 * p), pair(src, 2 * p), gcol(gain), 2 * p).then_inc(s_taken, 1)
                    if squares:
                        act.activation(pair(SQ, 2 * p), pair(src, 2 * p), ACT.Square).then_inc(s_sq, 1)

            plain("win")
            for kv in range(2):
                act.wait_ge(s_given, given.at("z", kv + 1))
                act.activation(FHf[:, 2 * kv * 480:(2 * kv + 1) * 480], ZT, ACT.Copy).then_inc(s_taken, 1)
                ahead("winv", 0, 2, kv)
            acc_out("winv", 1)
            act.activation(gates[:, :, :], V2[:, :, 3 * P:3 * P + 24], ACT.Sigmoid).then_inc(s_taken, 1)
            for kv in range(2):
                ahead("cmp", 0, 4, 2 * kv)
                ahead("cmp", 0, 4, 2 * kv + 1)
                acc_out("cmp", kv)
                act.activation(SG[0:ROWS, kv, :], TG[0:ROWS, kv, 2:2 + S], ACT.Gelu_apprx_tanh).then_inc(hid_ready, 1)
            attention("attn_nsa")
            ready_chunks("outn", A[:, Q_SLOT:Q_SLOT + 8, :], Ohi, "g_out2", squares=False)
            residual("wout", 2, [])
            ready_chunks("post", X, Hhi, "g_fpre2")
            ffn("up2", ACT.Gelu_apprx_tanh)
            residual("down2", 6, [], last_stage=True)

        @block.vector
        def _(dve):
            ch = Chain(dve, dve_chain)
            link = ch.link
            f = lambda ap: ap.bitcast(F32)

            def lower(j, after):
                dve.wait_ge(hi_out, after)
                dve.tensor_tensor(out=wlo[j][:, LO_POOL:KC, :], in0=raw[j][:, LO_POOL:KC, :], in1=f(whi[j][:, LO_POOL:KC, :]),
                                  op=ALU.subtract).then_inc(lo_dve, 1)

            def ahead(name, i, per, k, last=False):
                if not last:
                    lower(k % 2, 2 * per * i + 2 * (T0[name] + k + 3))

            def tile(name, i, per, k):
                dve.wait_ge(tile_done, per * i + (T0[name] + k + 1))

            def col(name, c):
                return cst[:, bass.ds(c + C0[name][0], 1)] if not isinstance(c, int) else C(name, c, 1)

            def pair(t, c):
                return t[:, bass.ds(c, 2), :] if not isinstance(c, int) else t[:, c:c + 2, :]

            def both(ap):
                return ap.unsqueeze(1).broadcast_to((P, 2, S))

            def out_acc(ins):
                ins.then_inc(acc_free, 1)

            def lo_scaled(dst, src, hi, name, c):
                for k in range(2):
                    ins = dve.scalar_tensor_tensor(out=dst[:, k, :], in0=src[:, k, :], scalar=col(name, c + k),
                                                   in1=f(hi[:, k, :]), op0=ALU.mult, op1=ALU.subtract)
                return ins

            def inverse_root(name, n, div, eps, dst, times=None):
                dve.wait_ge(stat_ready, N0[name] + 1)
                v, y, a = (nw[:, q, 0:n] for q in range(3))
                if times is None:
                    dve.tensor_scalar(v, st[:, 0:n], 1.0 / div, eps, op0=ALU.mult, op1=ALU.add).then_inc(st_used, 1)
                    dve.wait_ge(st_used, N0[name] + 1)
                else:
                    dve.scalar_tensor_tensor(out=v, in0=st[:, 0:n], scalar=1.0 / div, in1=times, op0=ALU.mult, op1=ALU.mult)\
                        .then_inc(st_used, 1)
                    dve.wait_ge(st_used, N0[name] + 1)
                    link(dve.tensor_scalar(v, v, eps, None, op0=ALU.add))
                link(dve.tensor_scalar(nwi[:, 0:n], v.bitcast(I32), 1, None, op0=ALU.logical_shift_right))
                link(dve.tensor_scalar(y.bitcast(I32), nwi[:, 0:n], -1, 0x5F3759DF, op0=ALU.mult, op1=ALU.add))
                for step in range(3):
                    link(dve.scalar_tensor_tensor(out=a, in0=y, scalar=-0.5, in1=v, op0=ALU.mult, op1=ALU.mult))
                    link(dve.tensor_tensor(out=a, in0=a, in1=y, op=ALU.mult))
                    ins = dve.scalar_tensor_tensor(out=y if step < 2 else dst, in0=a, scalar=1.5, in1=y, op0=ALU.add, op1=ALU.mult)
                    if step < 2:
                        link(ins)
                return ins

            NORM_LINKS = 2 + 3 * 3

            def norm(name, eps=RMS_EPS):
                if name != "pre2":
                    link(inverse_root(name, S, D, eps, R[:, :]))
                    return
                link(inverse_root("final", S, D, eps, RF))
                link(dve.tensor_tensor(out=R[:, :], in0=RF, in1=RF, op=ALU.mult))
                link(inverse_root("pre2", S, D, eps, R[:, :], times=R[:, :]))
                link(dve.tensor_tensor(out=R[:, :], in0=R[:, :], in1=RF, op=ALU.mult))

            def norm_columns(name, n, div, eps):
                inverse_root(name, n, div, eps, rt[:, RT[name], 0:n]).then_inc(rt_ready, 1)

            def residual(name, per, outs, last_stage=False):
                for start, stop in ([(0, 2)] if not last_stage else [(0, 1), (1, 2)]):
                    with loop(dve, stop, start) as i:
                        for g in range(2):
                            def weights(ks):
                                for kk in ks:
                                    ahead(name, i, per, kk, last=last_stage and start == 1 and kk >= per - 2)

                            ks = range(g * per // 2, (g + 1) * per // 2)
                            weights(ks[:-1])
                            tile(name, i, per, ks[-1])
                            c = 4 * i + 2 * g
                            if name in ("wout", "down2"):
                                dve.tensor_copy(pair(M2, c), acc[g][:, :, :]).then_inc(acc_free, 1)
                                dve.wait_ge(acc_free, 2 * i + (G0[name] + g + 3))
                                gain = "g_post2" if name == "wout" else "g_fpost2"
                                for k in range(2):
                                    dve.tensor_scalar(pair(MG, c)[:, k, :], pair(M2, c)[:, k, :], col(gain, c + k), None, op0=ALU.mult)
                            elif name == "pw2":
                                dve.scalar_tensor_tensor(out=pair(X, c)[:, 0, :], in0=acc[g][:, 0, :], scalar=col("b_pw2", c),
                                                         in1=pair(X, c)[:, 0, :], op0=ALU.add, op1=ALU.add)
                                dve.scalar_tensor_tensor(out=pair(X, c)[:, 1, :], in0=acc[g][:, 1, :], scalar=col("b_pw2", c + 1),
                                                         in1=pair(X, c)[:, 1, :], op0=ALU.add, op1=ALU.add).then_inc(acc_free, 1)
                            else:
                                dve.tensor_tensor(out=pair(X, c), in0=acc[g][:, :, :], in1=pair(X, c), op=ALU.add)\
                                    .then_inc(acc_free, 1)
                            if not g:
                                weights(ks[-1:])
                            if outs:
                                dve.wait_ge(acc_free, 2 * i + (G0[name] + g + 3))
                                dve.wait_ge(s_taken, 2 * i + taken.at(name, g + 1))
                            for hi, lo, gain in outs:
                                ins = lo_scaled(pair(lo, c), pair(X, c), pair(hi, c), gain, c)
                            if outs:
                                ins.then_inc(s_h, 1)
                            if g:
                                weights(ks[-1:])

            def first_turn(eng_loop, norm_name):
                return ((0, 1), (1, eng_loop)) if norm_name and eng_loop > 1 else ((0, eng_loop),)

            def evacuate(name, i, j, ins, norm_name, more=None):
                tile(name, i, 2, j)
                if norm_name and j == 0 and isinstance(i, int) and i == 0:
                    ahead(name, i, 2, j)
                    norm(norm_name)
                    out_acc(ins())
                    if more:
                        more()
                else:
                    out_acc(ins())
                    if more:
                        more()
                    ahead(name, i, 2, j)

            def times_r(dst, j):
                return lambda: dve.tensor_tensor(out=dst, in0=acc[j][:, :, :], in1=both(R[:, :]), op=ALU.mult)

            def rotate(before, name, i, j):
                cos, sin = (C("cos2"), C("sin2")) if before == "win" else (rope_c[:, :], rope_s[:, :])
                if before != name:
                    i, t = 0, ROTS[before] - 1
                else:
                    t = j - 1
                r = t + ROT0[before]
                dve.wait_ge(rot_ready, 2 * i + (r + 1))
                q, turned = pair(A, 4 * i + (2 * t + ROT_SLOT[before])), E[:, r % 2, :, :]
                link(dve.tensor_tensor(out=turned, in0=sc[:, r % 2, :].rearrange("p (a b) -> p a b", a=2), in1=both(sin), op=ALU.mult))
                link(dve.tensor_tensor(out=q, in0=q, in1=both(cos), op=ALU.mult))
                dve.tensor_tensor(out=q, in0=q, in1=turned, op=ALU.add).then_inc(rot_used, 1)

            def project(name, dst, norm_name=None, before=None):
                turns = first_turn(NTILES[name] // 2, norm_name or name in ROT0)
                for start, stop in turns:
                    links = (0 if name not in ROT0 else 4 if start or before else 2) + (0 if start or not norm_name else 2 * NORM_LINKS + 3 if norm_name == "pre2" else NORM_LINKS)
                    with ch.loop(stop, links, start) as i:
                        for j in range(2):
                            evacuate(name, i, j, times_r(pair(dst, 4 * i + 2 * j), j), norm_name)
                            if name in ROT0 and (start or j):
                                rotate(name, name, i, j)
                            elif before and j == 0:
                                rotate(before, name, i, j)

            def hidden_rest(name, i, src):
                dve.wait_ge(s_taken, 2 * i + taken.at(name, 2))
                dve.tensor_tensor(out=pair(FL, 2 * i), in0=src, in1=f(pair(FH, 2 * i)), op=ALU.subtract).then_inc(s_h, 1)

            def ffn(name, norm_name):
                up = TU[:, :, 2:2 + S]
                for start, stop in first_turn(11, norm_name):
                    with loop(dve, stop, start) as i:
                        evacuate(name, i, 0, times_r(TG[:, :, 2:2 + S], 0), norm_name)
                        if start:
                            dve.wait_ge(s_given, i + given.at(name, 0))
                            hidden_rest(name, i + (-1), up)
                            dve.wait_ge(s_h, i + h.at(name, 0))
                        evacuate(name, i, 1, times_r(up, 1), norm_name)
                        dve.wait_ge(acc_free, 2 * i + (G0[name] + 4))
                        dve.wait_ge(s_taken, 2 * i + taken.at(name, 1))
                        dve.tensor_tensor(out=up, in0=up, in1=SG[:, :, :], op=ALU.mult).then_inc(s_given, 1)
                dve.wait_ge(s_given, given.at(name, 11))
                hidden_rest(name, 10, up)

            def short_conv(dst, src, c):
                before = [None, None]
                for tap in range(3):
                    for k in range(2):
                        w = col("cw2", 3 * (c + k) + tap)
                        s_ = src[:, k, tap:tap + S]
                        if tap == 0:
                            ins = dve.tensor_scalar(dst[:, k, :], s_, w, None, op0=ALU.mult)
                        else:
                            ch.wait(before[k])
                            ins = dve.scalar_tensor_tensor(out=dst[:, k, :], in0=s_, scalar=w, in1=dst[:, k, :],
                                                           op0=ALU.mult, op1=ALU.add)
                        if tap < 2 or k == 0:
                            before[k] = ch.mark(ins)
                return ins

            def conv_ffn(name, norm_name):
                up = E[:, 1, :, :]
                for start, stop in first_turn(11, norm_name):
                    with ch.loop(stop, 5 + 6 + (0 if start else NORM_LINKS), start) as i:
                        def gate_conv():
                            dve.wait_ge(acc_free, 2 * i + (G0[name] + 3))
                            short_conv(E[:, 0, :, :], TG, 4 * i).then_inc(s_given, 1)

                        def up_conv():
                            dve.wait_ge(acc_free, 2 * i + (G0[name] + 4))
                            ch.link(short_conv(up, TU, 4 * i + 2))

                        evacuate(name, i, 0, times_r(TG[:, :, 2:2 + S], 0), norm_name, gate_conv)
                        if start:
                            dve.wait_ge(s_given, 2 * i + given.at(name, 0))
                            hidden_rest(name, i + (-1), up)
                            dve.wait_ge(s_h, i + h.at(name, 0))
                        evacuate(name, i, 1, times_r(TU[:, :, 2:2 + S], 1), norm_name, up_conv)
                        dve.wait_ge(s_taken, 2 * i + taken.at(name, 1))
                        for k in range(2):
                            ins = dve.scalar_tensor_tensor(out=up[:, k, :], in0=up[:, k, :], scalar=col("cb2", 4 * i + (2 + k)),
                                                           in1=SG[:, k, :], op0=ALU.add, op1=ALU.mult)
                        ins.then_inc(s_given, 1)
                dve.wait_ge(s_given, given.at(name))
                hidden_rest(name, 10, up)

            def attention(name, steps={}):
                units, u0 = ATTN[name], U0[name]
                for s in range(len(units) + 6):
                    if s in steps:
                        steps[s]()
                    if s < len(units):
                        u, n = units[s], u0 + s
                        r = n % 2
                        dve.wait_ge(s_done, n + 1)
                        link(dve.reduce_max(mx[:, r, :], sc[:, 2 * r:2 * r + 2, 0:u["keys"]], axis=AX_X))
                        if u["kind"] == "swa":
                            sinks = C("sinks", 2 * (u["c"] - 4), 2)
                            link(dve.scalar_tensor_tensor(out=mx[:, r, :], in0=mx[:, r, :], scalar=u["scale"], in1=sinks,
                                                          op0=ALU.mult, op1=ALU.max))
                            link(dve.tensor_scalar(nb[:, r, :], mx[:, r, :], -1.0, None, op0=ALU.mult))
                            dve.tensor_tensor(out=sk[:, r, :], in0=nb[:, r, :], in1=sinks, op=ALU.add).then_inc(nb_ready, 1)
                        else:
                            dve.tensor_scalar(nb[:, r, :], mx[:, r, :], -u["scale"], None, op0=ALU.mult).then_inc(nb_ready, 1)
                    if 1 <= s <= len(units):
                        u, n = units[s - 1], u0 + s - 1
                        r, kind = n % 2, u["kind"]
                        dve.wait_ge(exp_done, n + 1)
                        rr = rs[:, r, :]
                        if kind == "swa":
                            link(dve.tensor_tensor(out=rr, in0=rr, in1=ske[:, r, :], op=ALU.add))
                        if kind == "cmp":
                            link(dve.tensor_scalar(rr, rr, 1e-30, None, op0=ALU.max))
                        link(dve.reciprocal(rr, rr))
                        if kind in ("slc", "win", "cmp"):
                            b = {"cmp": 0, "slc": 1, "win": 2}[kind]
                            gate = gates[:, u["qt"], 8 * b + 2 * u["c"]:][:, 0:2]
                            if kind == "cmp":
                                link(dve.scalar_tensor_tensor(out=rr, in0=rr, scalar=C("rowok", u["qt"], 1), in1=gate,
                                                              op0=ALU.mult, op1=ALU.mult))
                            else:
                                link(dve.tensor_tensor(out=rr, in0=rr, in1=gate, op=ALU.mult))
                        if kind == "diff":
                            link(dve.tensor_scalar(rr[:, 1:2], rr[:, 1:2], lam[:, 0:1], None, op0=ALU.mult))
                        e = [E[:, n % 3, m, 0:u["keys"]] for m in range(2)]
                        ins = dve.tensor_scalar(e[0], e[0], rr[:, 0:1], None, op0=ALU.mult)
                        if kind == "diff":
                            link(ins)
                            ins = dve.scalar_tensor_tensor(out=e[0], in0=e[1], scalar=rr[:, 1:2], in1=e[0],
                                                           op0=ALU.mult, op1=ALU.add)
                        else:
                            ins = dve.tensor_scalar(e[1], e[1], rr[:, 1:2], None, op0=ALU.mult)
                        ins.then_inc(p_ready, 1)
                    if 4 <= s < len(units) + 4 and units[s - 4]["last"]:
                        n, g = u0 + s - 4, units[s - 4]["group"]
                        a = acc[(G0[name] + g) % 2]
                        dve.wait_ge(pv_done, n + 1)
                        if "mem" in name:
                            out_acc(dve.tensor_copy(A[:, 2 * g:2 * g + 2, :], a[:, :, :]))
                        else:
                            out_acc(dve.tensor_copy(A[:, units[s - 4]["slot"], :], a[:, 0, :]))
                    if "mem" in name and s >= 6:
                        g = units[s - 6]["group"]
                        dve.wait_ge(s_taken, taken.at(name, g + 1))
                        dve.tensor_tensor(out=Olo[:, 2 * g:2 * g + 2, :], in0=A[:, 2 * g:2 * g + 2, :],
                                          in1=f(Ohi[:, 2 * g:2 * g + 2, :]), op=ALU.subtract).then_inc(s_h, 1)

            dve.memset(ones[:, :], 1.0)
            dve.memset(TG[:, :, :], 0.0)
            link(dve.memset(TU[:, :, :], 0.0))
            link(dve.memset(U[:, :, 0:CONV - 1], 0.0))
            dve.sem_inc(conv_done, 1)
            dve.sem_inc(prod_used, 1)
            dve.sem_inc(conv_share, 1)
            dve.sem_inc(acc_free, 2)
            dve.wait_ge(x_loaded, 16)
            for p in range(4):
                dve.wait_ge(s_taken, taken.at("x0", p + 1))
                lo_scaled(pair(Hlo, 2 * p), pair(X, 2 * p), pair(Hhi, 2 * p), "g_mix0", 2 * p).then_inc(s_h, 1)
            for j in range(2):
                lower(j, 2 * j + 2)
            dve.wait_ge(cst_loaded, 16)

            def conv_chunk(i, base, between):
                c = i + base
                at = lambda t: t[:, bass.ds(c, 1), :].rearrange("p o s -> p (o s)") if not isinstance(c, int) else t[:, c, :]
                taps = lambda tap: (U[:, bass.ds(c, 1), tap:tap + S].rearrange("p o s -> p (o s)") if not isinstance(c, int)
                                    else U[:, c, tap:tap + S])
                dst, before = [at(UC), dve_sum], [None, None]
                for tap in range(CONV - sum(CONV_ACT)):
                    if tap in between:
                        between[tap]()
                    k = tap % 2
                    o = C0["w_dw"][0] + CONV * base + tap
                    w = cst[:, bass.ds(CONV * i + o, 1)] if not isinstance(c, int) else cst[:, CONV * i + o:CONV * i + o + 1]
                    if tap == 0:
                        ins = dve.tensor_scalar(dst[k], taps(tap), w, col("b_dw", c), op0=ALU.mult, op1=ALU.add)
                    elif tap == 1:
                        ins = dve.tensor_scalar(dst[k], taps(tap), w, None, op0=ALU.mult)
                    else:
                        ch.wait(before[k])
                        ins = dve.scalar_tensor_tensor(out=dst[k], in0=taps(tap), scalar=w, in1=dst[k], op0=ALU.mult, op1=ALU.add)
                    before[k] = ch.mark(ins)
                ch.wait(before[0])
                ch.link(dve.tensor_tensor(out=dst[0], in0=dst[0], in1=dst[1], op=ALU.add))
                dve.wait_ge(conv_share, i + (base + 2))
                dve.tensor_tensor(out=dst[0], in0=dst[0], in1=pool_sum[:, 0, :], op=ALU.add).then_inc(conv_done, 1)
                dve.wait_ge(conv_done, i + (base + 2))

            links = CONV - sum(CONV_ACT) + 1
            for start, stop in first_turn(4, "mix0"):
                with ch.loop(stop, links if start else NORM_LINKS, start) as i:
                    def second_tile():
                        evacuate("pw1", i, 1, times_r(TU[:, :, 2:2 + S], 1), "mix0")

                    def gated():
                        dve.wait_ge(acc_free, 2 * i + (G0["pw1"] + 4))
                        dve.wait_ge(s_taken, i + taken.at("pw1", 1))
                        for k in range(2):
                            dve.scalar_tensor_tensor(out=U[:, bass.ds(2 * i + k, 1), CONV - 1:CONV - 1 + S].rearrange("p o s -> p (o s)"),
                                                     in0=TG[:, k, 2:2 + S], scalar=col("b_pw1", 4 * i + k), in1=SG[:, k, :],
                                                     op0=ALU.add, op1=ALU.mult).then_inc(u_ready, 1)
                        dve.wait_ge(u_ready, 2 * i + 2)

                    evacuate("pw1", i, 0, times_r(TG[:, :, 2:2 + S], 0), "mix0")
                    if start:
                        conv_chunk(i, -1, {9: second_tile, 14: gated})
                    else:
                        second_tile()
                        gated()
                        dve.wait_ge(mem_loaded, 16)
                        dve.wait_ge(mem_upper, 1)
                        dve.tensor_tensor(out=H2lo[:, :, :], in0=UC, in1=f(H2hi[:, :, :]), op=ALU.subtract).then_inc(s_h, 1)
                        dve.wait_ge(s_h, h.at("mem"))
            with ch.loop(4, links) as i:
                conv_chunk(i, 3, {tap: (lambda k=k: ahead("memk", i, 2, k)) for k, tap in enumerate((4, 15))})
            conv_chunk(0, 7, {tap: (lambda k=k: ahead("memv", 0, 8, k)) for k, tap in enumerate((4, 15))})
            ahead("memv", 0, 8, 2)
            dve.wait_ge(stat_ready, N0["ln_mu"] + 1)
            for p in range(4):
                u = pair(UC, 2 * p)
                ins = dve.scalar_tensor_tensor(out=u, in0=both(st[:, 0:S]), scalar=-1.0 / D, in1=u, op0=ALU.mult, op1=ALU.add)
                ins.then_inc(s_given, 1)
            dve.wait_ge(s_given, given.at("ln_sq"))
            dve.sem_inc(st_used, 1)
            ahead("memv", 0, 8, 3)
            norm("ln_var", LN_EPS)
            for p in range(4):
                dve.tensor_tensor(out=pair(UC, 2 * p), in0=pair(UC, 2 * p), in1=both(R[:, :]), op=ALU.mult).then_inc(s_given, 1)
            for p in range(4):
                if p < 3:
                    ahead("memv", 0, 8, 4 + p)
                dve.wait_ge(s_taken, taken.at("ln", p + 1))
                dve.tensor_tensor(out=Olo[:, 2 * p:2 * p + 2, :], in0=SQ[:, 2 * p:2 * p + 2, :],
                                  in1=f(Ohi[:, 2 * p:2 * p + 2, :]), op=ALU.subtract).then_inc(s_h, 1)
            ahead("memv", 0, 8, 7)
            dve.tensor_copy(ident_b[:, :], C("ident"))
            dve.tensor_copy(causal_b[:, :], C("causal"))
            dve.tensor_copy(band_b[:, :], C("band"))
            dve.tensor_tensor(out=C("g_both"), in0=C("g_final"), in1=C("g_pre2"), op=ALU.mult)
            dve.tensor_copy(cmask_b[:, :], C("cmask")).then_inc(consts_ready, 1)
            lv = C("lam").rearrange("p (a b c) -> p a b c", a=2, b=2)
            prod = TU[:, 1, 0:P].rearrange("p (a c) -> p a c", a=2)
            link(dve.tensor_tensor(out=prod, in0=lv[:, :, 0, :], in1=lv[:, :, 1, :], op=ALU.mult))
            dve.reduce_sum(lam[:, 0:2], prod, axis=AX_X).then_inc(s_given, 1)
            dve.wait_ge(s_taken, taken.at("lam"))
            link(dve.tensor_tensor(out=lam[:, 0:1], in0=lam[:, 3:4], in1=lam[:, 2:3], op=ALU.subtract))
            link(dve.tensor_scalar(lam[:, 0:1], lam[:, 0:1], -LAMBDA_INIT, None, op0=ALU.add))
            link(dve.tensor_scalar(gsub[:, :], C("g_sub"), 1.0 - LAMBDA_INIT, None, op0=ALU.mult))
            dve.wait_ge(pos_loaded, 16)
            ang, turn, r0, r1 = TU[:, 0, 0:S], TU[:, 1, 0:S], TG[:, 0, 0:S], TG[:, 1, 0:S]
            link(dve.tensor_copy(ang, PT[:, 0, 0:S].bitcast(I32)))
            link(dve.tensor_scalar(ang, ang, C("invf"), None, op0=ALU.mult))
            link(dve.tensor_scalar(turn, ang, 1.0 / (2 * math.pi), MAGIC, op0=ALU.mult, op1=ALU.add))
            link(dve.tensor_scalar(turn, turn, -MAGIC, None, op0=ALU.add))
            for k, part in enumerate(TWO_PI):
                link(dve.scalar_tensor_tensor(out=r0, in0=turn, scalar=-part, in1=ang if k == 0 else r0,
                                              op0=ALU.mult, op1=ALU.add))
            link(dve.tensor_scalar(r0, r0, -PI_IN, PI_IN, op0=ALU.max, op1=ALU.min))
            link(dve.scalar_tensor_tensor(out=r1, in0=r0, scalar=-1.0, in1=r0, op0=ALU.mult, op1=ALU.max))
            dve.tensor_scalar(r1, r1, -1.0, math.pi / 2, op0=ALU.mult, op1=ALU.add).then_inc(s_given, 1)
            dve.wait_ge(s_taken, taken.at("rope"))
            dve.wait_ge(acc_free, G0["pw2"] + 2)
            residual("pw2", 2, [(Hhi, Hlo, "g_mem0")])

            def to_tokens(name):
                dve.wait_ge(tokens_ready, RT[name] - 1)
                link(dve.tensor_copy(rt[:, RT[name], 0:NT], st[:, 0:NT]))

            def values(name, dst, norm_name, before):
                to_tokens(norm_name)
                for start, stop in ((0, 1), (1, 2)):
                    with loop(dve, stop, start) as i:
                        for j in range(2):
                            tile(name, i, 2, j)
                            for tt in range(NT):
                                ins = dve.tensor_scalar(dst(i, j, tt), acc[j][:, tt, :], rt[:, RT[norm_name], tt:tt + 1], None, op0=ALU.mult)
                            out_acc(ins)
                            ahead(name, i, 2, j)
                            if start == j == 0:
                                rotate(before, name, i, j)

            def slot(t, c):
                return t[:, bass.ds(c, 1), :].rearrange("p o s -> p (o s)") if not isinstance(c, int) else t[:, c, :]

            for layer in range(2):
                project(f"memq{layer}", A, f"mem{layer}")
                dve.wait_ge(acc_free, G0[f"attn_mem{layer}"] + 2)
                attention(f"attn_mem{layer}")
                residual(f"memo{layer}", 2, [(Hhi, Hlo, f"g_ffn{layer}")])
                ffn(f"gu{layer}", f"ffn{layer}")
                if layer == 1:
                    break
                residual("down0", 6, [(Hhi, Hlo, "g_kv"), (H2hi, H2lo, "g_mix1")])
                project("diffk", A[:, 8:16, :], "attn1")
                project("diffq", A[:, 0:8, :], before="diffk")
                values("diffv", lambda i, j, tt: slot(MKV, 4 * i + (2 * DC + 2 * j + tt)), "attn1", "diffq")
                attention("attn_diff")
                norm_columns("sub", 16, P, SUBLN_EPS)
                dve.wait_ge(spread_ready, RT["sub"] + 1)
                dve.wait_ge(acc_free, G0["attn_diff"] + 8 + 2)
                for p in range(4):
                    q = A[:, 2 * p:2 * p + 2, :]
                    dve.tensor_tensor(out=q, in0=sc[:, p, :].rearrange("p (a b) -> p a b", a=2), in1=q, op=ALU.mult).then_inc(s_given, 1)
                for p in range(4):
                    dve.wait_ge(s_taken, taken.at("sub", p + 1))
                    q = slice(2 * p, 2 * p + 2)
                    dve.scalar_tensor_tensor(out=Olo[:, q, :], in0=A[:, q, :], scalar=gsub[:, 0:1], in1=f(Ohi[:, q, :]),
                                             op0=ALU.mult, op1=ALU.subtract).then_inc(s_h, 1)
                residual("diffo", 2, [(Hhi, Hlo, "g_mem1")])
            residual("down1", 6, [(Hhi, Hlo, "g_both")])

            def by_pairs(name, make, dst, src, hi, gain):
                def rest(p):
                    dve.wait_ge(s_taken, taken.at(name, p + 1))
                    lo_scaled(pair(dst, 2 * p), pair(src, 2 * p), pair(hi, 2 * p), gain, 2 * p).then_inc(s_h, 1)

                for p in range(3):
                    make(p)
                for p in range(3):
                    rest(p)
                make(3)
                rest(3)

            project("win", A, "pre2")
            dve.wait_ge(rot_used, ROT0["win"] + 1)
            for kv, slot0 in enumerate((KC_SLOT, VC_SLOT)):
                if kv:
                    dve.wait_ge(s_h, h.at("z", kv))
                    dve.wait_ge(acc_free, G0["win"] + 8 + 2)
                z = ZT.rearrange("p (j h c) -> p j h c", j=16, h=2)
                for hd in range(2):
                    for half in range(2):
                        rows = slice(64 * half, 64 * half + 64)
                        for jh in range(2):
                            at = (slot0 + hd) * S + half + 16 * jh
                            src = Af[rows, at:at + 16 * NCMP].rearrange("p (c j two) -> p j c two", j=8, two=2)[:, :, :, 0]
                            pe_ = C("pe", 16 * kv + 8 * jh, 8)[rows, :].unsqueeze(2).broadcast_to((64, 8, NCMP))
                            ins = dve.tensor_tensor(out=z[rows, 8 * jh:8 * jh + 8, hd, :], in0=src, in1=pe_, op=ALU.add)
                ins.then_inc(s_given, 1)
                if kv == 0:
                    to_tokens("pre2")
                tile("winv", 0, 2, kv)
                for tt in range(NT):
                    ins = dve.tensor_scalar(V2[:, tt, kv * S:(kv + 1) * S], acc[kv][:, tt, :], rt[:, RT["pre2"], tt:tt + 1],
                                            None, op0=ALU.mult)
                out_acc(ins)
                ahead("winv", 0, 2, kv)
                dve.wait_ge(s_given, given.at("z", kv + 1))
                dve.wait_ge(s_taken, taken.at("z", kv + 1))
                dve.tensor_tensor(out=FHf[:, (2 * kv + 1) * 480:(2 * kv + 2) * 480], in0=ZT,
                                  in1=f(FHf[:, 2 * kv * 480:(2 * kv + 1) * 480]), op=ALU.subtract).then_inc(s_h, 1)
            for c in range(DC):
                dve.scalar_tensor_tensor(out=X[:, c, :], in0=X[:, c, :], scalar=C("g_final", c, 1), in1=RF,
                                         op0=ALU.mult, op1=ALU.mult)
            for kv in range(2):
                ahead("cmp", 0, 4, 2 * kv)
                tile("cmp", 0, 4, 2 * kv + 1)
                out_acc(dve.tensor_copy(TG[0:ROWS, kv, 2:2 + S], acc[kv][0:ROWS, 0, :]))
                ahead("cmp", 0, 4, 2 * kv + 1)

            def copy_hidden():
                dve.wait_ge(hid_turned, 1)
                four = st[:, 0:S].rearrange("p (a b c) -> p a b c", a=2, b=2)
                dve.tensor_copy(HCm[:, :, :, 0:ROWS], four[:, :, :, 0:ROWS]).then_inc(hid_copied, 1)

            def compressed():
                dve.wait_ge(cmp_mm, 1)
                dve.tensor_copy(KCm[:, 0:NCMP], st[:, S:S + NCMP])
                dve.tensor_copy(VCm[0:NCMP, :], st[0:NCMP, S + P:2 * S]).then_inc(cmp_ready, 1)

            dve.wait_ge(s_taken, taken.at("gates"))
            attention("attn_nsa", {5: copy_hidden, 9: compressed})
            norm_columns("out2", 4, D // 2, RMS_EPS)
            dve.wait_ge(spread_ready, RT["out2"] + 1)
            dve.wait_ge(acc_free, G0["attn_nsa"] + 8 + 2)

            def normed_out(p):
                b, o = p // 2, pair(A, Q_SLOT + 2 * p)
                dve.tensor_tensor(out=o, in0=both(sc[:, 0, b * S:(b + 1) * S]), in1=o, op=ALU.mult).then_inc(s_given, 1)

            by_pairs("outn", normed_out, Olo, A[:, Q_SLOT:Q_SLOT + 8, :], Ohi, "g_out2")
            residual("wout", 2, [])
            norm("post2")

            def add_normed(done):
                def add(p):
                    link(dve.tensor_tensor(out=pair(MG, 2 * p), in0=pair(MG, 2 * p), in1=both(R[:, :]), op=ALU.mult))
                    dve.tensor_tensor(out=pair(X, 2 * p), in0=pair(X, 2 * p), in1=pair(MG, 2 * p), op=ALU.add).then_inc(done, 1)

                return add

            by_pairs("post", add_normed(s_given), Hlo, X, Hhi, "g_fpre2")
            dve.memset(TG[:, :, 0:2], 0.0)
            link(dve.memset(TU[:, :, 0:2], 0.0))
            conv_ffn("up2", "fpre2")
            residual("down2", 6, [], last_stage=True)
            norm("fpost2")
            for p in range(4):
                add_normed(x_final)(p)


def column_tile(w, cols, k0=0):
    part = w[k0:k0 + KC * P][:, cols]
    tile = np.zeros((KC * P, MB), w.dtype)
    tile[:part.shape[0], :part.shape[1]] = part
    return tile.reshape(KC, P, MB).transpose(1, 0, 2).reshape(P, KC * MB)


def weight_tiles(w):
    rng = lambda a, n=MB: list(range(a, a + n))
    tiles = []

    def plain(m):
        for c in range(0, m.shape[1], MB):
            tiles.append(column_tile(m, rng(c)))

    def halves(m, width):
        for c in range(0, width, MB):
            tiles.append(column_tile(m, rng(c)))
            tiles.append(column_tile(m, rng(width + c)))

    def deep(m):
        for c in range(0, D, MB):
            for k in range(0, FF, KC * P):
                tiles.append(column_tile(m, rng(c), k))

    halves(w["conv_w_pw1"][0], D)
    for name in ("mem_w_k", "mem_w_v"):
        for layer in range(2):
            plain(w[name][layer])
    plain(w["conv_w_pw2"][0])
    for layer in range(2):
        plain(w["mem_w_q"][layer])
        plain(w["mem_w_o"][layer])
        for c in range(0, FF, MB):
            tiles.append(column_tile(w["ffn_w_gate"][layer], rng(c)))
            tiles.append(column_tile(w["ffn_w_up"][layer], rng(c)))
        deep(w["ffn_w_down"][layer])
        if layer == 0:
            plain(w["w_k_shared"])
            plain(w["diff_w_q"][0])
            plain(w["w_v_shared"])
            plain(w["diff_w_o"][0])
    win = w["w_in_2"][0]
    at = np.cumsum([0, 512, 128, 128, 128, 128, 128, 128, 24, 512, 128, 128])
    q_n, k_c, v_c, k_s, v_s, k_w, v_w, g_n, q_w, k_sw, v_sw = (int(a) for a in at[:-1])
    pairs = [hd for c in range(4) for hd in (c, 4 + c)]
    both = lambda c: column_tile(win, rng(c, 64) * 2 + rng(c + 64, 64) * 2)
    tiles.append(both(k_c))
    for q in (q_n, q_w):
        order = [q + 64 * hd + d for hd in pairs for d in range(64)]
        tiles.append(column_tile(win, order[0:MB]))
        tiles.append(column_tile(win, order[MB:]))
    tiles.append(column_tile(win, rng(k_s, P) + rng(k_w, P)))
    tiles.append(column_tile(win, rng(k_sw, P)))
    tiles.append(both(v_c))
    tiles.append(column_tile(win, rng(v_s, P) + rng(v_w, P)))
    tiles.append(column_tile(win, rng(v_sw, P) + [g_n + 3 * hd + b for b in range(3) for hd in pairs]))
    for kv in range(2):
        for k in range(0, CMP_LEN * HD2, KC * P):
            tiles.append(column_tile(w["cmp_w1_2"][0, kv], rng(0), k))
    rows = [64 * hd + d for hd in pairs for d in range(64)]
    plain(w["w_out_2"][0][rows + [512 + r for r in rows]])
    halves(w["w_up_2"][0], FF)
    deep(w["w_down_2"][0])
    assert len(tiles) == TILES
    return np.stack(tiles), rows


def packed_constants(w, rows):
    def vec(v):
        return v.reshape(-1, P).T

    def every(v):
        return np.broadcast_to(v.reshape(1, -1), (P, v.size))

    def in_turn(v, width):
        m = v.reshape(v.shape[:-1] + (2, width // MB, MB))
        return np.moveaxis(m, -3, -2).reshape(v.shape)

    pairs = [hd for c in range(4) for hd in (c, 4 + c)]
    parts = {
        "g_mix0": vec(w["norm_mix"][0]), "g_mem0": vec(w["norm_mem"][0]), "g_ffn0": vec(w["norm_ffn"][0]),
        "g_kv": vec(w["kv_norm"]), "g_mix1": vec(w["norm_mix"][1]), "g_mem1": vec(w["norm_mem"][1]),
        "g_ffn1": vec(w["norm_ffn"][1]), "g_final": vec(w["norm_final"]),
        "b_pw1": vec(in_turn(w["conv_b_pw1"][0], D)),
        "w_dw": w["conv_w_dw"][0].reshape(CONV, DC, P).transpose(2, 1, 0).reshape(P, DC * CONV),
        "b_dw": vec(w["conv_b_dw"][0]), "ln_g": vec(w["conv_ln_g"][0]), "ln_b": vec(w["conv_ln_b"][0]),
        "b_pw2": vec(w["conv_b_pw2"][0]), "g_sub": vec(w["diff_subln_g"][0]),
        "lam": np.concatenate([every(w[f"diff_lambda_{n}"][0]) for n in ("q1", "k1", "q2", "k2")], 1),
        "g_pre2": vec(w["attn_pre_norm_2"][0]), "g_post2": vec(w["attn_post_norm_2"][0]),
        "g_out2": np.concatenate([vec(w["nsa_out_norm_2"][0][rows]), vec(w["swa_out_norm_2"][0][rows])], 1),
        "pe": w["cmp_pos_2"][0].reshape(2, 16, 2, HD2).transpose(2, 3, 0, 1).reshape(P, 32),
        "cmp_w2": w["cmp_w2_2"][0].reshape(2, 2, P, HD2).transpose(2, 0, 1, 3).reshape(P, 256),
        "sinks": every(w["swa_sinks_2"][0][pairs]),
        "g_fpre2": vec(w["ffn_pre_norm_2"][0]), "g_fpost2": vec(w["ffn_post_norm_2"][0]),
        "cw2": in_turn(w["conv_w_2"][0], FF).reshape(3, 2 * FC, P).transpose(2, 1, 0).reshape(P, 6 * FC),
        "cb2": vec(in_turn(w["conv_b_2"][0], FF)),
    }
    p, t = np.arange(P), np.arange(S)
    f32 = np.float32
    inv1 = (np.float32(500000.0) ** (-np.arange(0, ROT1, 2, dtype=f32) / f32(ROT1))).astype(f32)
    parts["invf"] = np.where(p % 64 < ROT1, inv1[p % 8], 0).astype(f32)[:, None]
    parts["ident"] = np.eye(P, dtype=f32)
    perm1, perm2 = np.zeros((P, P), f32), np.zeros((P, P), f32)
    for c in range(0, P, 64):
        for k in range(8):
            perm1[c + 8 + k, c + k], perm1[c + k, c + 8 + k] = -1, 1
        for k in range(32):
            perm2[c + 32 + k, c + k], perm2[c + k, c + 32 + k] = -1, 1
    parts["perm1"], parts["perm2"] = perm1, perm2
    parts["causal"] = np.where(p[None, :] <= p[:, None], 0, NEG).astype(f32)
    parts["band"] = np.where(p[None, :] > p[:, None], 0, NEG).astype(f32)
    cm = np.zeros((P, 2, 16), f32)
    ends = np.arange(NCMP) * CMP_STRIDE + CMP_LEN - 1
    for tt in range(NT):
        cm[:, tt, :NCMP] = np.where(ends[None, :] <= (tt * P + p)[:, None], 0, NEG)
    parts["cmask"] = cm.reshape(P, 32)
    parts["rowok"] = np.stack([(tt * P + p >= CMP_LEN - 1) for tt in range(NT)], 1).astype(f32)
    inv2 = (np.float32(10000.0) ** (-np.arange(32, dtype=f32) / f32(32))).astype(f32)
    ang = t.astype(f32)[None, :] * inv2[p % 32][:, None]
    parts["cos2"], parts["sin2"] = np.cos(ang).astype(f32), np.sin(ang).astype(f32)
    for name, n in CONSTS:
        assert parts[name].shape == (P, n), (name, parts[name].shape)
    return np.concatenate([parts[name] for name, _ in CONSTS], 1)


def kernel(**inputs):
    import concourse.bacc as bacc
    from concourse.bass_utils import run_bass_kernel_spmd

    w = {k: np.asarray(v) for k, v in inputs.items()}
    tiles, rows = weight_tiles(w)
    arrays = {
        "weights": tiles, "consts": np.ascontiguousarray(packed_constants(w, rows)),
        "x_in": np.ascontiguousarray(w["x"][0].T), "mem_in": np.ascontiguousarray(w["mem"][0].T),
        "positions": w["positions"],
    }
    nc = bacc.Bacc("TRN2", target_bir_lowering=False, num_devices=1)
    args = [nc.dram_tensor(n, a.shape, mybir.dt.from_np(a.dtype), kind="ExternalInput").ap() for n, a in arrays.items()]
    args.append(nc.dram_tensor("out", (D, S), F32, kind="ExternalOutput").ap())
    build(nc, *args)
    r = run_bass_kernel_spmd(nc, [arrays], core_ids=[0])
    return np.ascontiguousarray(r.results[0]["out"].T)[None]
```
